# Optimizing a Trainium2 kernel written in Bass

```python
import jax, jax.numpy as jnp
from jax import lax
import numpy as np

D_MODEL = 1024
BATCH = 1
SEQ = 1024
DEPTH = 1
DEC_BATCH = 8
DEC_SEQ = 8
PAST_LEN = 1024
PAGE_SIZE = 128

M_HEADS = 4
M_DQK = 128
M_DV = D_MODEL // M_HEADS
M_CHUNK = 64
A_HEADS = 16
A_KV = 4
A_HD = D_MODEL // A_HEADS
A_GROUP = A_HEADS // A_KV
WINDOW = 128
WIN_CACHE = min(WINDOW, PAST_LEN)
D_FF = 4 * D_MODEL
EPS = 1e-6
F_BIAS = 3.0
_SIZES = (M_HEADS * M_DQK, M_HEADS * M_DQK, M_HEADS * M_DV, M_HEADS * M_DV, M_HEADS, M_HEADS,
          A_HEADS * A_HD, A_KV * A_HD, A_KV * A_HD, D_MODEL, D_MODEL)
D_IN = 2 * M_HEADS * M_DQK + 2 * M_HEADS * M_DV + 2 * M_HEADS + A_HEADS * A_HD + 2 * A_KV * A_HD + 2 * D_MODEL

kernel_name = 'hybrid_mlstm_swa_sink_decoder_step'

def rmsnorm(x, g):
    xf = x.astype(jnp.float32)
    y = xf * lax.rsqrt(jnp.mean(xf * xf, axis=-1, keepdims=True) + EPS)
    return (y * g.astype(jnp.float32)).astype(x.dtype)

def mlstm_chunked(q, k, v, i_log, logf, C0, n0, m0):
    f32 = jnp.float32
    B, H, T, dk = q.shape
    L = M_CHUNK if T % M_CHUNK == 0 else T
    nc = T // L

    def to_chunks(a):
        return jnp.moveaxis(a.astype(f32).reshape(B, H, nc, L, *a.shape[3:]), 2, 0)

    xs = (to_chunks(q), to_chunks(k), to_chunks(v), to_chunks(i_log), to_chunks(logf))
    causal = jnp.tril(jnp.ones((L, L), dtype=bool))

    def step(carry, inp):
        C, n, m = carry
        qc, kc, vc, ic, fc = inp
        b = jnp.cumsum(fc, axis=-1)
        dmat = jnp.where(causal, b[..., :, None] - b[..., None, :] + ic[..., None, :], -jnp.inf)
        inter = b + m[..., None]
        m_row = jnp.maximum(inter, jnp.max(dmat, axis=-1))
        w = jnp.exp(dmat - m_row[..., None])
        w_int = jnp.exp(inter - m_row)
        s = jnp.einsum('bhtd,bhsd->bhts', qc, kc) * w
        num = w_int[..., None] * jnp.einsum('bhtd,bhde->bhte', qc, C) + jnp.einsum('bhts,bhse->bhte', s, vc)
        den = w_int * jnp.einsum('bhtd,bhd->bht', qc, n) + jnp.sum(s, axis=-1)
        h = num / jnp.maximum(jnp.abs(den), jnp.exp(-m_row))[..., None]
        m_new = m_row[..., -1]
        wk = jnp.exp(b[..., -1:] - b + ic - m_new[..., None])
        decay = jnp.exp(inter[..., -1] - m_new)
        C_new = decay[..., None, None] * C + jnp.einsum('bhs,bhsd,bhse->bhde', wk, kc, vc)
        n_new = decay[..., None] * n + jnp.einsum('bhs,bhsd->bhd', wk, kc)
        return (C_new, n_new, m_new), h

    (C, n, m), hs = lax.scan(step, (C0.astype(f32), n0.astype(f32), m0.astype(f32)), xs)
    h = jnp.moveaxis(hs, 0, 2).reshape(B, H, T, -1)
    return h, C, n, m

def sink_attend(q, k, v, mask, sinks):
    f32 = jnp.float32
    s = jnp.einsum('...kgqd,...ksd->...kgqs', q, k).astype(f32) * (A_HD ** -0.5)
    s = jnp.where(mask, s, -jnp.inf)
    sk = sinks.astype(f32)[:, :, None]
    mx = jnp.maximum(jnp.max(s, axis=-1), sk)
    p = jnp.exp(s - mx[..., None])
    den = jnp.sum(p, axis=-1) + jnp.exp(sk - mx)
    return jnp.einsum('...kgqs,...ksd->...kgqd', (p / den[..., None]).astype(v.dtype), v)

def swa_prompt(q, k, v, sinks):
    B, T = q.shape[:2]
    nb = T // WINDOW
    qb = q.reshape(B, nb, WINDOW, A_KV, A_GROUP, A_HD).transpose(0, 1, 3, 4, 2, 5)

    def band(a):
        ab = a.reshape(B, nb, WINDOW, A_KV, A_HD)
        prev = jnp.concatenate([jnp.zeros_like(ab[:, :1]), ab[:, :-1]], axis=1)
        return jnp.concatenate([prev, ab], axis=2).transpose(0, 1, 3, 2, 4)

    qpos = jnp.arange(nb)[:, None] * WINDOW + jnp.arange(WINDOW)[None, :]
    kpos = jnp.arange(nb)[:, None] * WINDOW - WINDOW + jnp.arange(2 * WINDOW)[None, :]
    diff = qpos[:, :, None] - kpos[:, None, :]
    mask = (diff >= 0) & (diff < WINDOW) & (kpos[:, None, :] >= 0)
    o = sink_attend(qb, band(k), band(v), mask[:, None, None], sinks)
    o = o.transpose(0, 1, 4, 2, 3, 5).reshape(B, T, A_HEADS * A_HD)
    return o, k[:, -WIN_CACHE:], v[:, -WIN_CACHE:]

def swa_sample(q, k, v, ck, cv, sinks):
    B, T = q.shape[:2]
    wc = ck.shape[1]
    kk = jnp.concatenate([ck.astype(k.dtype), k], axis=1)
    vv = jnp.concatenate([cv.astype(v.dtype), v], axis=1)
    qpos = PAST_LEN + jnp.arange(T)
    kpos = PAST_LEN - wc + jnp.arange(wc + T)
    diff = qpos[:, None] - kpos[None, :]
    mask = (diff >= 0) & (diff < WINDOW)
    qh = q.reshape(B, T, A_KV, A_GROUP, A_HD).transpose(0, 2, 3, 1, 4)
    o = sink_attend(qh, kk.transpose(0, 2, 1, 3), vv.transpose(0, 2, 1, 3), mask, sinks)
    o = o.transpose(0, 3, 1, 2, 4).reshape(B, T, A_HEADS * A_HD)
    return o, kk[:, -wc:], vv[:, -wc:]

def trunk_layer(x, norm_attn, w_in, b_gate, mlstm_norm, sinks, w_out, norm_mlp, w_up, w_down,
                C0, n0, m0, ck=None, cv=None):
    f32 = jnp.float32
    B, T, _ = x.shape
    xn = rmsnorm(x, norm_attn)
    proj = xn @ w_in
    mq, mk, mv, mo, mi, mf, aq, ak, av, ga, gb = jnp.split(proj, np.cumsum(_SIZES)[:-1].tolist(), axis=-1)
    gates = jnp.concatenate([mi, mf], axis=-1).astype(f32) + b_gate.astype(f32)
    i_log = gates[..., :M_HEADS].transpose(0, 2, 1)
    logf = jax.nn.log_sigmoid(gates[..., M_HEADS:]).transpose(0, 2, 1)
    hq = mq.reshape(B, T, M_HEADS, M_DQK).transpose(0, 2, 1, 3) * (M_DQK ** -0.5)
    hk = mk.reshape(B, T, M_HEADS, M_DQK).transpose(0, 2, 1, 3)
    hv = mv.reshape(B, T, M_HEADS, M_DV).transpose(0, 2, 1, 3)
    h, C, n, m = mlstm_chunked(hq, hk, hv, i_log, logf, C0, n0, m0)
    h = h.transpose(0, 2, 1, 3)
    h = h * lax.rsqrt(jnp.mean(h * h, axis=-1, keepdims=True) + EPS) * mlstm_norm.astype(f32).reshape(M_HEADS, M_DV)
    branch_a = jax.nn.sigmoid(mo) * h.reshape(B, T, M_HEADS * M_DV).astype(x.dtype)
    sk = sinks.reshape(A_KV, A_GROUP)
    qa = aq.reshape(B, T, A_HEADS, A_HD)
    ka = ak.reshape(B, T, A_KV, A_HD)
    va = av.reshape(B, T, A_KV, A_HD)
    if ck is None:
        branch_b, kc, vc = swa_prompt(qa, ka, va, sk)
    else:
        branch_b, kc, vc = swa_sample(qa, ka, va, ck, cv, sk)
    merged = jax.nn.sigmoid(ga) * branch_a + jax.nn.sigmoid(gb) * branch_b
    x = x + merged @ w_out
    xn2 = rmsnorm(x, norm_mlp)
    x = x + jnp.square(jax.nn.relu(xn2 @ w_up)) @ w_down
    return x, C, n, m, kc, vc

def setup_inputs(seed: int = 0) -> dict:
    key = jax.random.key(seed)
    ks = jax.random.split(key, 20)
    nrm = lambda k, shape, scale: jax.random.normal(k, shape, jnp.float32) * scale
    b_i = nrm(ks[9], (DEPTH, M_HEADS), 0.1)
    b_f = F_BIAS + nrm(ks[10], (DEPTH, M_HEADS), 0.5)
    return {
        'x_prompt': nrm(ks[0], (BATCH, SEQ, D_MODEL), 1.0),
        'x_sample': nrm(ks[1], (DEC_BATCH, DEC_SEQ, D_MODEL), 1.0),
        'state_C': nrm(ks[2], (DEPTH, DEC_BATCH, M_HEADS, M_DQK, M_DV), 0.3),
        'state_n': nrm(ks[3], (DEPTH, DEC_BATCH, M_HEADS, M_DQK), 1.0),
        'state_m': jax.random.uniform(ks[4], (DEPTH, DEC_BATCH, M_HEADS), jnp.float32, -1.0, 1.0),
        'cache_k': nrm(ks[5], (DEPTH, DEC_BATCH, WIN_CACHE, A_KV, A_HD), 1.0),
        'cache_v': nrm(ks[6], (DEPTH, DEC_BATCH, WIN_CACHE, A_KV, A_HD), 1.0),
        'norm_attn': 1.0 + nrm(ks[7], (DEPTH, D_MODEL), 0.02),
        'w_in': nrm(ks[8], (DEPTH, D_MODEL, D_IN), D_MODEL ** -0.5),
        'b_gate': jnp.concatenate([b_i, b_f], axis=-1),
        'mlstm_norm': 1.0 + nrm(ks[11], (DEPTH, M_HEADS * M_DV), 0.02),
        'sinks': nrm(ks[12], (DEPTH, A_HEADS), 0.5),
        'w_out': nrm(ks[13], (DEPTH, D_MODEL, D_MODEL), D_MODEL ** -0.5),
        'norm_mlp': 1.0 + nrm(ks[14], (DEPTH, D_MODEL), 0.02),
        'w_up': nrm(ks[15], (DEPTH, D_MODEL, D_FF), D_MODEL ** -0.5),
        'w_down': nrm(ks[16], (DEPTH, D_FF, D_MODEL), D_FF ** -0.5),
        'norm_final': 1.0 + nrm(ks[17], (D_MODEL,), 0.02),
    }

def reference(x_prompt, x_sample, state_C, state_n, state_m, cache_k, cache_v,
              norm_attn, w_in, b_gate, mlstm_norm, sinks, w_out, norm_mlp, w_up, w_down, norm_final):
    f32 = jnp.float32
    xp, xs = x_prompt, x_sample
    pC, pn, pm, pk, pv = [], [], [], [], []
    sC, sn, sm, skk, svv = [], [], [], [], []
    zC = jnp.zeros((BATCH, M_HEADS, M_DQK, M_DV), f32)
    zn = jnp.zeros((BATCH, M_HEADS, M_DQK), f32)
    zm = jnp.zeros((BATCH, M_HEADS), f32)
    for l in range(DEPTH):
        w = (norm_attn[l], w_in[l], b_gate[l], mlstm_norm[l], sinks[l], w_out[l], norm_mlp[l], w_up[l], w_down[l])
        xp, C, n, m, kc, vc = trunk_layer(xp, *w, zC, zn, zm)
        pC.append(C); pn.append(n); pm.append(m); pk.append(kc); pv.append(vc)
        xs, C, n, m, kc, vc = trunk_layer(xs, *w, state_C[l], state_n[l], state_m[l], cache_k[l], cache_v[l])
        sC.append(C); sn.append(n); sm.append(m); skk.append(kc); svv.append(vc)
    y_prompt = rmsnorm(xp, norm_final)
    y_sample = rmsnorm(xs, norm_final)
    p_C, p_n, p_m, p_k, p_v = jnp.stack(pC), jnp.stack(pn), jnp.stack(pm), jnp.stack(pk), jnp.stack(pv)
    s_C, s_n, s_m, s_k, s_v = jnp.stack(sC), jnp.stack(sn), jnp.stack(sm), jnp.stack(skk), jnp.stack(svv)
    return (y_prompt, y_sample, p_C, p_n, p_m, p_k, p_v, s_C, s_n, s_m, s_k, s_v)


_drawn_inputs = setup_inputs


def setup_inputs(seed=0):
    import zlib

    import numpy as np

    out = dict(_drawn_inputs(seed))
    spreads = {}
    factors = {'mlstm_norm': 21.572, 'sinks': 200.0, 'norm_mlp': 9.047, 'norm_final': 23.528}
    for name, (base, spread) in spreads.items():
        noise = np.random.default_rng([zlib.crc32(name.encode()), seed]).standard_normal(out[name].shape)
        drawn = base * np.exp(spread * noise) if base else spread * noise
        out[name] = __import__('jax').numpy.asarray(drawn.astype(out[name].dtype))
    for name, factor in factors.items():
        out[name] = (out[name] * factor).astype(out[name].dtype)
    return out
```

```python
from contextlib import ExitStack

import concourse.bass as bass
from concourse import mybir

F32 = mybir.dt.float32
F32R = mybir.dt.float32r
ALU = mybir.AluOpType
ACT = mybir.ActivationFunctionType

P = 128
D = 1024
SEQ = 1024
NSEQ = 8
DSEQ = 8
T = SEQ + NSEQ * DSEQ
NT = (T + P - 1) // P
KT = D // P
MH = 4
DK = 128
DV = 256
VA = DV + 1
HD = 64
NKV = 4
GRP = 4
WIN = 128
FF = 4096
EPS = 1e-6
BIG = 1e30
C_MQ, C_MK, C_MV, C_MO = 0, 512, 1024, 2048
C_GATE = 3072
C_AQ = 3080
C_AK = 4104
C_AV = 4360
C_GA = 4616
C_GB = 5640
WCOLS = 256
BLK = KT * (WCOLS + 8)
CHUNKS = [(0, 384), (384, 384), (768, 320)]
QK_SCALE = float(DK) ** -0.5
ATT_SCALE = float(HD) ** -0.5
NG = FF // WCOLS


def rows_of(i):
    return P if i < NT - 1 else T - P * (NT - 1)


def block_list():
    out = [("v", 0), ("v", 1), ("mk", 0), ("mq", 0), ("v", 2), ("v", 3), ("mk", 1), ("mq", 1), ("av",), ("ak",)]
    out += [("aq", p, gg) for p in range(2) for gg in range(2)]
    out += [(kind, p, gg) for p in range(2) for gg in range(2) for kind in ("mo", "ga", "gb")]
    out += [("out", cq) for cq in range(4)]
    return out


BLOCKS = block_list()
NPROJ = len(BLOCKS) - 4
NATURAL = ("v", "av", "out")


def n_units(b):
    return NT if BLOCKS[b][0] in NATURAL else 2 * len(CHUNKS)


FIRST_UNIT = [sum(n_units(x) for x in range(b)) for b in range(NPROJ + 1)]
PROJ_UNITS = FIRST_UNIT[NPROJ]
OUT_UNITS = 4 * NT
B_MLP = len(BLOCKS)
UP_UNITS = 2 * len(CHUNKS)
DN_UNITS = 2 * NT


def layer_kernel(nc, x_prompt, x_sample, state_C, state_n, state_m, cache_k, cache_v, norm_attn, w_in, b_gate,
                 mlstm_norm, sinks, w_out, norm_mlp, w_up, w_down, norm_final,
                 y_prompt, y_sample, p_C, p_n, p_m, p_k, p_v, s_C, s_n, s_m, s_k, s_v):
    xs_flat = x_sample.rearrange("b t d -> (b t) d")
    ys_flat = y_sample.rearrange("b t d -> (b t) d")

    def x_rows(i):
        return x_prompt[0, i * P:(i + 1) * P, :] if i < NT - 1 else xs_flat

    def y_rows(i):
        return y_prompt[0, i * P:(i + 1) * P, :] if i < NT - 1 else ys_flat

    w_in_k = w_in[0].rearrange("(k p) c -> p k c", p=P)
    w_up_k = w_up[0].rearrange("(k p) c -> p k c", p=P)
    w_dn_k = w_down[0].rearrange("(k p) c -> p k c", p=P)
    gate_rows = nc.dram_tensor("gate_rows", (2, MH, T), F32, kind="Internal").ap()
    ends_dram = nc.dram_tensor("ends_dram", (MH, 16), F32, kind="Internal").ap()
    mask_dram = nc.dram_tensor("mask_dram", (DSEQ, NSEQ * 192), F32, kind="Internal").ap()

    ctx = ExitStack()
    with ctx:
        def scope_alloc(stack):
            def alloc(name, shape, dt=F32):
                return stack.enter_context(nc.sbuf_tensor(name, shape, dt))
            return alloc

        sb = scope_alloc(ctx)

        def sem(name):
            return ctx.enter_context(nc.semaphore(name))

        bank = [ctx.enter_context(nc.psum_tensor(f"bank{n}", [P, 512], F32)) for n in range(8)]

        ident = sb("ident", [P, P])
        causal = sb("causal", [P, P])
        causal8 = sb("causal8", [64, 64])
        seq_ind = sb("seq_ind", [64, NSEQ])
        gain_b = sb("gain_b", [P, D])
        raw = sb("raw", [P, BLK])
        w_hi = sb("w_hi", [P, 2, BLK], F32R)
        w_lo = sb("w_lo", [P, 2, BLK], F32R)
        xT_hi = sb("xT_hi", [P, KT, T], F32R)
        xT_lo = sb("xT_lo", [P, KT, T], F32R)
        stat = sb("stat", [P, 3, NT])
        rstd = sb("rstd", [P, 3, NT])
        neghalf = sb("neghalf", [P, 2])
        mnorm = sb("mnorm", [P, KT])
        sink_b = sb("sink_b", [P, 16])
        sink_s = sb("sink_s", [P, 1])

        with ExitStack() as s:
            a = scope_alloc(s)
            xin = a("xin", [P, 3, D])
            xn = a("xn", [P, 2, D])
            junk = a("junk", [P, D])
        s = ExitStack()
        with s:
            a = scope_alloc(s)
            hT = a("hT", [P, KT, T])
            mqT = a("mqT", [P, 2, T])
            mkT = a("mkT", [P, 2, T])
            vaug = a("vaug", [P, NT, 2, VA])
            gnat = a("gnat", [P, NT, 8])
            nat = a("nat", [P, NT, 4, MH])
            sm_rows = a("sm_rows", [MH, NSEQ])
            bias_i = a("bias_i", [MH, 1])
            bias_f = a("bias_f", [MH, 1])
            ends = a("ends", [MH, 16])
            m_out = a("m_out", [MH, NSEQ + 1])
            dec = a("dec", [P, MH, 16])
            bc = a("bc", [P, 2, 4, P])
            Cst = a("Cst", [P, 2, VA])
            Cin = a("Cin", [P, 2, 4, VA])
            small = a("small", [P, 2, 8])
            wgt = a("wgt", [P, 2, 2, P])
            qs = a("qs", [P, 2, 2, P])
            kw = a("kw", [P, 2, 2, P])
            hh_b = a("hh_b", [P, 2, GRP, 2, HD])
            hjunk = a("hjunk", [P, DV])
            qz = a("qz", [P, 2, 576])
            kwz = a("kwz", [64, NSEQ, P])
        with ExitStack() as s:
            a = scope_alloc(s)
            row_i = a("row_i", [MH, T])
            row_f = a("row_f", [MH, T])
            row_t = a("row_t", [MH, T])
            row_b = a("row_b", [MH, T])
            row_m = a("row_m", [MH, T])
            row_x = a("row_x", [MH, T])
            row_r = a("row_r", [MH, T])
            q4 = a("q4", [P, T])
        with ExitStack() as s:
            a = scope_alloc(s)
            a("under_hT", [P, KT, T])
            aqT = a("aqT", [P, KT, T])
            akT = a("akT", [P, 2, T])
            avn = a("avn", [P, NT, NKV * HD])
            with ExitStack() as s2:
                a2 = scope_alloc(s2)
                amask = a2("amask", [P, 2 * P])
                prob = a2("prob", [P, 2, GRP, 2 * P])
                pT = a2("pT", [P, 2, GRP * P])
                ast = a2("ast", [P, 2, 6, GRP])
            with ExitStack() as s2:
                a2 = scope_alloc(s2)
                smask = a2("smask", [P, NSEQ, 192])
                kc = a2("kc", [P, 2, NKV * HD])
                vc = a2("vc", [P, 2, NKV * HD])
                kcT = a2("kcT", [P, 2, 2, P])
                sprob = a2("sprob", [P, 2, 192])
                spT = a2("spT", [P, 2, P])
                o2 = a2("o2", [P, P])
                qsmp = a2("qsmp", [P, 2, NSEQ, GRP, DSEQ])
                sst = a2("sst", [P, 2, 6])
                kout = a2("kout", [P, 2, NKV * HD])
            sig = a("sig", [P, 2, 384])
        with ExitStack() as s:
            a = scope_alloc(s)
            x2 = a("x2", [P, NT, D])
            hid_hi = a("hid_hi", [P, 2, 2, T], F32R)
            hid_lo = a("hid_lo", [P, 2, 2, T], F32R)
            relu = a("relu", [P, 2, 384])
            sqr = a("sqr", [P, 2, 384])
            ybuf = a("ybuf", [P, 2, D])
            junk2 = a("junk2", [P, D])

        x_in = [sem(f"x_in{n}") for n in range(3)]
        raw_in = sem("raw_in")
        w_hi_done = sem("w_hi_done")
        w_lo_done = sem("w_lo_done")
        gain_in = sem("gain_in")
        const_in = sem("const_in")
        consts = sem("consts")
        norm_sq = sem("norm_sq")
        norm_rs = sem("norm_rs")
        norm_xn = sem("norm_xn")
        norm_tp = sem("norm_tp")
        norm_hi = sem("norm_hi")
        norm_lo = sem("norm_lo")
        gemm_a = sem("gemm_a")
        free_a = sem("free_a")
        gemm_v = sem("gemm_v")
        free_v = sem("free_v")
        act_chain = sem("act_chain")
        dve_chain = sem("dve_chain")
        pool_chain = sem("pool_chain")
        gate_tp = sem("gate_tp")
        gate_ev = sem("gate_ev")
        gate_ln = sem("gate_ln")
        gate_arg = sem("gate_arg")
        gate_exp = sem("gate_exp")
        gate_fin = sem("gate_fin")
        gate_q4 = sem("gate_q4")
        gate_nat = sem("gate_nat")
        rows_out = sem("rows_out")
        dec_in = sem("dec_in")
        bc_in = [sem(f"bc_in{n}") for n in range(2)]
        ml_kt = sem("ml_kt")
        ml_st = sem("ml_st")
        ml_wa = sem("ml_wa")
        ml_we = sem("ml_we")
        ml_sw = sem("ml_sw")
        ml_qs = sem("ml_qs")
        ml_kw = sem("ml_kw")
        ml_n = sem("ml_n")
        ml_u = sem("ml_u")
        ml_ab = sem("ml_ab")
        ml_rc = sem("ml_rc")
        ml_h0 = sem("ml_h0")
        ml_h1 = sem("ml_h1")
        ml_ss = sem("ml_ss")
        ml_rs = sem("ml_rs")
        ml_hn = sem("ml_hn")
        ml_c = sem("ml_c")
        ml_t = sem("ml_t")
        ml_te = sem("ml_te")
        ml_kz = sem("ml_kz")
        ml_su = sem("ml_su")
        ml_sc = sem("ml_sc")
        ml_cl = sem("ml_cl")
        cin_in = [sem(f"cin_in{n}") for n in range(2)]
        cin_out = sem("cin_out")
        pc_out = sem("pc_out")
        at_s = sem("at_s")
        at_m = sem("at_m")
        at_e = sem("at_e")
        at_p = sem("at_p")
        at_t = sem("at_t")
        at_p0 = sem("at_p0")
        at_p1 = sem("at_p1")
        at_v = sem("at_v")
        at_o = sem("at_o")
        kc_in = [sem(f"kc_in{n}") for n in range(2)]
        mask_made = sem("mask_made")
        mask_io = sem("mask_io")
        sk_t = sem("sk_t")
        sk_e = sem("sk_e")
        ss_q = sem("ss_q")
        ss_s = sem("ss_s")
        ss_m = sem("ss_m")
        ss_e = sem("ss_e")
        ss_p = sem("ss_p")
        ss_t = sem("ss_t")
        ss_te = sem("ss_te")
        ss_v = sem("ss_v")
        ss_o2 = sem("ss_o2")
        ss_ot = sem("ss_ot")
        ss_o = sem("ss_o")
        ko_t = sem("ko_t")
        ko_e = sem("ko_e")
        sg_use = sem("sg_use")
        mg_hi = sem("mg_hi")
        mg_lo = sem("mg_lo")
        x2_in = [sem(f"x2_in{n}") for n in range(NT)]
        re_done = sem("re_done")
        hi_done = sem("hi_done")
        sq_done = sem("sq_done")
        lo_done = sem("lo_done")
        y_out = [sem(f"y_out{n}") for n in range(2)]
        y_rdy = sem("y_rdy")
        out_dma = sem("out_dma")

        def w_view(t, b, k):
            n = WCOLS + 8 if b == 0 else WCOLS
            return t[:, b % 2, k * n:(k + 1) * n]

        def w_stat(t, b, k, tile):
            return w_view(t, b, k)[:, tile * P:(tile + 1) * P]

        def split_views(b):
            if BLOCKS[b][0] not in ("aq", "mo", "ga", "gb"):
                n = BLK if b == 0 else KT * WCOLS
                return [(raw[:, 0:n], lambda t: t[:, b % 2, 0:n])]
            out = []
            for g in range(2):
                src = raw[:, 0:KT * WCOLS].rearrange("p (k h g c) -> p k h g c", k=KT, h=2, g=2)[:, :, :, g, :]
                out.append((src, lambda t, g=g: t[:, b % 2, 0:KT * WCOLS]
                            .rearrange("p (k g h c) -> p k g h c", k=KT, g=2, h=2)[:, :, g, :, :]))
            return out

        def half_view(n, rows):
            return bank[n][:, :].rearrange("p (k t) -> p k t", t=P)[:, :, 0:rows]

        RAW_DMAS = [{"v": 1, "aq": 2, "mo": 2, "ga": 2, "gb": 2, "out": 4}.get(x[0], 1) for x in BLOCKS]
        RAW_DMAS[0] = 2
        RAW_AT = [16 * sum(RAW_DMAS[:b + 1]) for b in range(B_MLP)]
        RAW_ALL = RAW_AT[-1]

        def by_group(v):
            return v.rearrange("t (g c) -> t g c", g=GRP)

        def cols(i):
            return slice(i * P, i * P + rows_of(i))

        def done_before(b):
            if b < NPROJ:
                return gemm_a, FIRST_UNIT[b + 1]
            return gemm_v, NT * (b - NPROJ + 1)

        S_PER = NT
        ML_AFTER = {3: 0, 7: 1}
        ATT_AFTER = 13

        block = ctx.enter_context(nc.Block())

        @block.sync
        def _(sp):
            def load_block(b):
                kind = BLOCKS[b][0]
                if b >= 1:
                    sp.wait_ge(w_lo_done, b)
                r = raw[:, 0:KT * WCOLS].rearrange("p (k c) -> p k c", k=KT)
                if b == 0:
                    r = raw[:, 0:BLK].rearrange("p (k c) -> p k c", k=KT)
                    sp.dma_start(r[:, :, 0:8], w_in_k[:, :, C_GATE:C_GATE + 8],
                                 allow_slow_non_contiguous=True).then_inc(raw_in, 16)
                    sp.dma_start(r[:, :, 8:], w_in_k[:, :, C_MV:C_MV + DV]).then_inc(raw_in, 16)
                elif kind in ("v", "mk", "mq", "av", "ak"):
                    c0 = {"v": C_MV, "mk": C_MK, "mq": C_MQ, "av": C_AV, "ak": C_AK}[kind]
                    c0 += WCOLS * (BLOCKS[b][1] if len(BLOCKS[b]) > 1 else 0)
                    sp.dma_start(r, w_in_k[:, :, c0:c0 + WCOLS]).then_inc(raw_in, 16)
                elif kind == "out":
                    cq = BLOCKS[b][1]
                    src = w_out[0].rearrange("(p h g c) n -> h p c g n", p=2, h=2, g=GRP)
                    for h in range(2):
                        for p in range(2):
                            sp.dma_start(r[64 * h:64 * h + 64, GRP * p:GRP * p + GRP, :],
                                         src[h, p, :, :, cq * WCOLS:(cq + 1) * WCOLS]).then_inc(raw_in, 16)
                else:
                    c0 = {"aq": C_AQ, "mo": C_MO, "ga": C_GA, "gb": C_GB}[kind]
                    _, p, gg = BLOCKS[b]
                    for h in range(2):
                        at = c0 + (2 * p + h) * 256 + gg * P
                        sp.dma_start(r[:, :, h * P:(h + 1) * P], w_in_k[:, :, at:at + P]).then_inc(raw_in, 16)

            def small(dst, src):
                sp.dma_start(dst, src, allow_slow_non_contiguous=True).then_inc(const_in, 16)

            def load_x(i):
                if i >= 3:
                    sp.wait_ge(norm_xn, i - 2)
                sp.dma_start(xin[0:rows_of(i), i % 3, :], x_rows(i)).then_inc(x_in[i % 3], 16)

            load_x(0)
            sp.dma_start(gain_b[:, :], norm_attn[0].partition_broadcast(P)).then_inc(gain_in, 16)
            load_x(1)
            load_block(0)
            load_x(2)
            small(bias_i[:, :], b_gate[0, 0:MH].unsqueeze(1))
            small(bias_f[:, :], b_gate[0, MH:2 * MH].unsqueeze(1))
            small(sm_rows[:, :], state_m[0].rearrange("b h -> h b"))
            small(sink_b[:, :], sinks[0].partition_broadcast(P))
            small(sink_s[:, :], sinks[0].unsqueeze(1).broadcast_to([16, DSEQ]).unsqueeze(2))
            mn = mlstm_norm[0].rearrange("(p h g c) -> h p c g", p=2, h=2, g=GRP)
            for h in range(2):
                for p in range(2):
                    small(mnorm[64 * h:64 * h + 64, GRP * p:GRP * p + GRP], mn[h, p])
            load_x(3)
            load_block(1)
            for i in range(4, NT):
                load_x(i)
            for b in range(NSEQ):
                sp.dma_start(s_k[0, b, 0:WIN - DSEQ], cache_k[0, b, DSEQ:WIN]).then_inc(out_dma, 16)
                sp.dma_start(s_v[0, b, 0:WIN - DSEQ], cache_v[0, b, DSEQ:WIN]).then_inc(out_dma, 16)
            sp.wait_ge(norm_xn, NT)
            sp.dma_start(gain_b[:, :], norm_mlp[0].partition_broadcast(P)).then_inc(gain_in, 16)

            def store_gate_rows():
                sp.wait_ge(gate_fin, 1)
                sp.dma_start(gate_rows[0], row_x[:, :]).then_inc(rows_out, 16)
                sp.dma_start(gate_rows[1], row_t[:, :]).then_inc(rows_out, 16)
                sp.dma_start(ends_dram, ends[:, :]).then_inc(rows_out, 16)
                sp.dma_start(p_m[0].rearrange("b h -> h b"), m_out[:, NSEQ:NSEQ + 1],
                             allow_slow_non_contiguous=True).then_inc(out_dma, 16)
                sp.dma_start(s_m[0].rearrange("b h -> h b"), m_out[:, 0:NSEQ],
                             allow_slow_non_contiguous=True).then_inc(out_dma, 16)
                sp.wait_ge(rows_out, 48)
                sp.dma_start(dec[:, :, :].rearrange("p h e -> p (h e)"),
                             ends_dram.rearrange("h e -> (h e)").unsqueeze(0).broadcast_to([P, MH * 16]))\
                    .then_inc(dec_in, 16)

            def load_bc(s):
                p, i = divmod(s, S_PER)
                if s >= 2:
                    sp.wait_ge(ml_wa, s - 1)
                    sp.wait_ge(ml_qs, s - 1)
                for q in range(2):
                    sp.dma_start(bc[:, s % 2, 2 * q:2 * q + 2, 0:rows_of(i)],
                                 gate_rows[q, 2 * p:2 * p + 2, cols(i)].unsqueeze(0)
                                 .broadcast_to([P, 2, rows_of(i)])).then_inc(bc_in[s % 2], 16)

            def load_cin(n):
                p, hh, half = n // 4, n // 2 % 2, n % 2
                h = 2 * p + hh
                if n >= 2:
                    sp.wait_ge(cin_out, 32 * (n - 1))
                sp.dma_start(Cin[:, half, :, 0:DV],
                             state_C[0, 4 * half:4 * half + 4, h].rearrange("b k v -> k b v")).then_inc(cin_in[half], 16)
                sp.dma_start(Cin[:, half, :, DV:VA],
                             state_n[0, 4 * half:4 * half + 4, h].rearrange("b k -> k b").unsqueeze(2),
                             allow_slow_non_contiguous=True).then_inc(cin_in[half], 16)

            def store_cin(n):
                p, hh, half = n // 4, n // 2 % 2, n % 2
                h = 2 * p + hh
                sp.wait_ge(ml_sc, 4 * (n + 1))
                sp.dma_start(s_C[0, 4 * half:4 * half + 4, h].rearrange("b k v -> k b v"),
                             Cin[:, half, :, 0:DV]).then_inc(cin_out, 16)
                sp.dma_start(s_n[0, 4 * half:4 * half + 4, h].rearrange("b k -> k b").unsqueeze(2),
                             Cin[:, half, :, DV:VA], allow_slow_non_contiguous=True).then_inc(cin_out, 16)

            for b in range(NPROJ + 4):
                if b + 2 < B_MLP:
                    load_block(b + 2)
                if b == 2:
                    store_gate_rows()
                if b in ML_AFTER:
                    p = ML_AFTER[b]
                    load_cin(4 * p)
                    load_cin(4 * p + 1)
                    for i in range(NT):
                        load_bc(p * S_PER + i)
                    sp.wait_ge(ml_c, (NT - 1) * (p + 1))
                    sp.dma_start(p_C[0, 0, 2 * p:2 * p + 2].rearrange("h k v -> k h v"),
                                 Cst[:, :, 0:DV]).then_inc(pc_out, 16)
                    sp.dma_start(p_n[0, 0, 2 * p:2 * p + 2].rearrange("h k -> k h").unsqueeze(2),
                                 Cst[:, :, DV:VA], allow_slow_non_contiguous=True).then_inc(pc_out, 16)
                    for n in range(4 * p, 4 * p + 4):
                        store_cin(n)
                        if n < 4 * p + 2:
                            load_cin(n + 2)
                if b == ATT_AFTER:
                    sp.wait_ge(at_v, 8 * NKV)
                    sp.wait_ge(at_o, 8 * NKV)
                    sp.wait_ge(mask_made, 1)
                    sp.dma_start(mask_dram, smask[0:DSEQ, :, :].rearrange("t b c -> t (b c)")).then_inc(mask_io, 16)
                    sp.wait_ge(mask_io, 16)
                    for n in range(16):
                        sp.dma_start(smask[n * DSEQ:(n + 1) * DSEQ, :, :].rearrange("t b c -> t (b c)"),
                                     mask_dram).then_inc(mask_io, 16)
                    for s in range(NSEQ):
                        if s >= 2:
                            sp.wait_ge(sk_t, s - 1)
                            sp.wait_ge(ss_v, s - 1)
                        sp.dma_start(kc[:, s % 2, :], cache_k[0, s].rearrange("w h d -> w (h d)")).then_inc(kc_in[s % 2], 16)
                        sp.dma_start(vc[:, s % 2, :], cache_v[0, s].rearrange("w h d -> w (h d)")).then_inc(kc_in[s % 2], 16)
                    sp.wait_ge(ko_e, 2)
                    sp.dma_start(p_k[0, 0].rearrange("t h d -> t (h d)"), kout[:, 0, :]).then_inc(out_dma, 16)
                    sp.dma_start(p_v[0, 0].rearrange("t h d -> t (h d)"), avn[:, NT - 2, :]).then_inc(out_dma, 16)
                    for s in range(NSEQ):
                        at = slice(s * DSEQ, (s + 1) * DSEQ)
                        sp.dma_start(s_k[0, s, WIN - DSEQ:].rearrange("t h d -> t (h d)"),
                                     kout[at, 1, :]).then_inc(out_dma, 16)
                        sp.dma_start(s_v[0, s, WIN - DSEQ:].rearrange("t h d -> t (h d)"),
                                     avn[at, NT - 1, :]).then_inc(out_dma, 16)
                if b == NPROJ - 1:
                    sp.wait_ge(mg_lo, NT)
                    for i in range(NT):
                        sp.dma_start(x2[0:rows_of(i), i, :], x_rows(i)).then_inc(x2_in[i], 16)

            def up_dma(g, b):
                sp.wait_ge(w_lo_done, b)
                sp.dma_start(raw[:, 0:KT * WCOLS].rearrange("p (k c) -> p k c", k=KT),
                             w_up_k[:, :, bass.ds(g * WCOLS, WCOLS)]).then_inc(raw_in, 16)

            def dn_dma(g, b):
                sp.wait_ge(w_lo_done, b)
                sp.dma_start(raw[:, 0:2 * D].rearrange("p (k c) -> p k c", k=2),
                             w_dn_k[:, bass.ds(2 * g, 2), :]).then_inc(raw_in, 16)

            up_dma(0, B_MLP)
            with sp.Fori(1, NG) as g:
                up_dma(g, g * 2 + (B_MLP - 1))
                dn_dma(g - 1, g * 2 + B_MLP)
            sp.wait_ge(norm_xn, 2 * NT)
            sp.dma_start(gain_b[:, :], norm_final.partition_broadcast(P)).then_inc(gain_in, 16)
            dn_dma(NG - 1, B_MLP + 2 * NG - 1)
            for i in range(NT):
                sp.wait_ge(y_rdy, i + 1)
                sp.dma_start(y_rows(i), ybuf[0:rows_of(i), i % 2, :]).then_inc(y_out[i % 2], 16)
            sp.wait_ge(pc_out, 64)
            sp.wait_ge(cin_out, 32 * 8)
            sp.wait_ge(out_dma, 16 * (2 * NSEQ + 2 + 2 + 2 * NSEQ))
            sp.wait_ge(y_out[0], 16 * ((NT + 1) // 2))
            sp.wait_ge(y_out[1], 16 * (NT // 2))

        @block.tensor
        def _(pe):
            def tr(out, in_, rows):
                return nc.tensor.transpose(out, in_, ident[0:rows, 0:rows])

            def norm_transposes(t, src, hold=None):
                i = t % NT
                rows = rows_of(i)
                pe.wait_ge(norm_xn, t + 1)
                for h in range(2):
                    n = 2 * t + h
                    if n >= 4:
                        pe.wait_ge(norm_lo, n - 3)
                    for k in range(4):
                        last = tr(bank[4 + n % 4][:, k * P:k * P + rows],
                                  src[0:rows, i % 2, (4 * h + k) * P:(4 * h + k + 1) * P], rows)
                    last.then_inc(norm_tp, 1)

            PASSES = ((w_hi, xT_hi), (w_hi, xT_lo), (w_lo, xT_hi))

            def proj_unit(b, u):
                n = FIRST_UNIT[b] + u
                if n >= 4:
                    pe.wait_ge(free_a, n - 3)
                step = 0
                for k in range(KT):
                    for w, x in PASSES:
                        if BLOCKS[b][0] in NATURAL:
                            rhs = w_view(w, b, k)
                            out = bank[n % 4][0:rows_of(u), 0:WCOLS + 8 if b == 0 else WCOLS]
                            lhsT = x[:, k, cols(u)]
                        else:
                            tile, (c0, cn) = u // 3, CHUNKS[u % 3]
                            lhsT = w_stat(w, b, k, tile)
                            rhs = x[:, k, c0:c0 + cn]
                            out = bank[n % 4][:, 0:cn]
                        last = nc.tensor.matmul(out, lhsT, rhs, start=(step == 0), stop=(step == 3 * KT - 1))
                        step += 1
                last.then_inc(gemm_a, 1)

            def gate_transposes():
                pe.wait_ge(free_a, NT)
                def part(b, at, tiles, c):
                    for x, i in enumerate(tiles):
                        last = tr(bank[b][0:MH, at + x * P:at + x * P + rows_of(i)],
                                  gnat[0:rows_of(i), i, c:c + MH], rows_of(i))
                    return last
                pe.wait_ge(norm_lo, 2 * NT)
                part(4, 0, range(0, 4), 0).then_inc(gate_tp, 1)
                part(5, 0, range(4, 8), 0).then_inc(gate_tp, 1)
                part(6, 0, [8], 0)
                part(6, 64, [8], MH).then_inc(gate_tp, 1)
                part(7, 0, range(0, 4), MH).then_inc(gate_tp, 1)
                pe.wait_ge(gate_ev, 1)
                part(4, 0, range(4, 8), MH).then_inc(gate_tp, 1)

            def q4_transposes():
                pe.wait_ge(gate_exp, 3)
                pe.wait_ge(gate_ev, 6)
                for b, tiles in ((4, range(0, 4)), (5, range(4, 8)), (6, [8])):
                    for x, i in enumerate(tiles):
                        last = tr(bank[b][0:rows_of(i), x * P:x * P + P], q4[:, cols(i)], P)
                    last.then_inc(gate_q4, 1)

            def ml_scores(s):
                p, i = divmod(s, S_PER)
                n = rows_of(i)
                if s >= 1:
                    pe.wait_ge(ml_kw, s)
                    pe.wait_ge(ml_sw, s)
                for hh in range(2):
                    last = tr(bank[4][0:n, hh * P:(hh + 1) * P], mkT[:, hh, cols(i)], P)
                last.then_inc(ml_kt, 1)
                for hh in range(2):
                    last = nc.tensor.matmul(bank[5][0:n, hh * P:hh * P + n], mkT[:, hh, cols(i)], mqT[:, hh, cols(i)],
                                            start=True, stop=True)
                last.then_inc(ml_st, 1)

            def ml_step(s):
                p, i = divmod(s, S_PER)
                n = rows_of(i)
                pe.wait_ge(ml_sw, s + 1)
                pe.wait_ge(ml_qs, s + 1)
                if s >= 1:
                    pe.wait_ge(ml_h0, s)
                    pe.wait_ge(ml_h1, s)
                if i < NT - 1:
                    c = (NT - 1) * p + i
                    if c:
                        pe.wait_ge(ml_c, c)
                    for hh in range(2):
                        last = nc.tensor.matmul(bank[6 + hh][0:n, 0:VA], wgt[0:n, s % 2, hh, 0:n],
                                                vaug[0:n, i, hh, :], start=True, stop=(i == 0))
                        if i > 0:
                            last = nc.tensor.matmul(bank[6 + hh][0:n, 0:VA], qs[:, s % 2, hh, 0:n], Cst[:, hh, :],
                                                    start=False, stop=True)
                    last.then_inc(ml_n, 1)
                    pe.wait_ge(ml_kw, s + 1)
                    for hh in range(2):
                        last = nc.tensor.matmul(bank[hh][:, 0:VA], kw[0:n, s % 2, hh, :], vaug[0:n, i, hh, :],
                                                start=True, stop=True)
                    last.then_inc(ml_u, 1)
                    return
                for hh in range(2):
                    nc.tensor.matmul(bank[6 + hh][0:n, 0:VA], wgt[0:n, s % 2, hh, 0:n], vaug[0:n, i, hh, :],
                                     start=True, stop=False)
                    for half in range(2):
                        pe.wait_ge(cin_in[half], 32 * (2 * p + hh + 1))
                        for b in range(4 * half, 4 * half + 4):
                            last = nc.tensor.matmul(bank[6 + hh][0:n, 0:VA], qz[:, hh, 64 * b:64 * b + 64],
                                                    Cin[:, half, b % 4, :], start=False, stop=(b == NSEQ - 1))
                    if hh == 1:
                        last.then_inc(ml_n, 1)
                    pe.wait_ge(ml_kz, 2 * p + hh + 1)
                    for b in range(NSEQ):
                        c = (2 * p + hh) * NSEQ + b
                        if b >= 2:
                            pe.wait_ge(ml_sc, c - 1)
                        elif c:
                            pe.wait_ge(ml_sc, c)
                        if c == 2 * NSEQ * p:
                            pe.wait_ge(ml_c, (NT - 1) * (p + 1))
                        nc.tensor.matmul(bank[b % 2][:, 0:VA], kwz[0:n, b, :], vaug[0:n, i, hh, :],
                                         start=True, stop=True).then_inc(ml_su, 1)

            def ml_transposes(s):
                i = s % S_PER
                n = rows_of(i)
                pe.wait_ge(ml_hn, s + 1)
                if s >= 1:
                    pe.wait_ge(ml_te, s)
                for g in range(GRP):
                    last = tr(bank[2][:, g * P:g * P + n],
                              hh_b[0:n, s % 2, g, :, :].rearrange("t h c -> t (h c)"), n)
                last.then_inc(ml_t, 1)

            def mlstm(p):
                pe.wait_ge(free_a, FIRST_UNIT[4 * p + 4])
                pe.wait_ge(gate_nat, 1)
                s0 = p * S_PER
                ml_scores(s0)
                for s in range(s0, s0 + S_PER):
                    if s + 1 < s0 + S_PER:
                        ml_scores(s + 1)
                    ml_step(s)
                    if s > s0:
                        ml_transposes(s - 1)
                ml_transposes(s0 + S_PER - 1)
                pe.wait_ge(ml_te, s0 + S_PER)

            def at_scores(u):
                i, kv = divmod(u, NKV)
                p, half = divmod(kv, 2)
                lo = 0 if i else P
                if u >= 2:
                    pe.wait_ge(at_m, u - 1)
                at = slice(64 * half, 64 * half + 64)
                for g in range(GRP):
                    out = bank[2 * (u % 2) + g // 2][:, (g % 2) * 256 + lo:(g % 2) * 256 + 256]
                    last = nc.tensor.matmul(out, aqT[at, p * GRP + g, cols(i)],
                                            akT[at, p, (i - 1) * P + lo:(i + 1) * P], start=True, stop=True)
                last.then_inc(at_s, 1)

            def at_rest(u):
                i, kv = divmod(u, NKV)
                half = kv % 2
                pe.wait_ge(at_p, u + 1)
                if u > NKV:
                    pe.wait_ge(at_p0, u - NKV)
                if u >= 1:
                    pe.wait_ge(at_p1, u)
                for kb in range(2 if i else 1):
                    kb = kb if i else 1
                    for g in range(GRP):
                        last = tr(bank[4 + kb][:, g * P:(g + 1) * P], prob[:, u % 2, g, kb * P:(kb + 1) * P], P)
                last.then_inc(at_t, 1)
                if u >= 2:
                    pe.wait_ge(at_o, u - 1)
                out = bank[6 + u % 2][64 * half:64 * half + 64, :]
                for kb in range(2):
                    if kb:
                        pe.wait_ge(at_p1, u + 1)
                    elif i:
                        pe.wait_ge(at_p0, u + 1 - NKV)
                    if kb or i:
                        last = nc.tensor.matmul(out, avn[:, i - 1 + kb, kv * HD:(kv + 1) * HD], pT[:, kb, :],
                                                start=(kb == 0 or i == 0), stop=(kb == 1))
                last.then_inc(at_v, 1)

            def ss_keys(b):
                pe.wait_ge(kc_in[b % 2], 32 * (b // 2 + 1))
                if b >= 1:
                    pe.wait_ge(sk_e, b)
                for p in range(2):
                    last = tr(bank[0][:, p * P:(p + 1) * P], kc[:, b % 2, p * P:(p + 1) * P], P)
                last.then_inc(sk_t, 1)

            def ss_scores(b):
                pe.wait_ge(sk_e, b + 1)
                pe.wait_ge(ss_q, 1)
                if b >= 1:
                    pe.wait_ge(ss_m, b)
                for kv in range(NKV):
                    p, half = divmod(kv, 2)
                    at = slice(64 * half, 64 * half + 64)
                    q = qsmp[at, p, b, :, :].rearrange("c g t -> c (g t)")
                    out = bank[1][32 * kv:32 * kv + 32, :]
                    nc.tensor.matmul(out[:, 0:P], q, kcT[at, b % 2, p, :], start=True, stop=True)
                    last = nc.tensor.matmul(out[:, P:192], q, akT[at, p, SEQ:T], start=True, stop=True)
                last.then_inc(ss_s, 1)

            def ss_transposes(b):
                pe.wait_ge(ss_p, b + 1)
                if b >= 1:
                    pe.wait_ge(ss_te, b)
                tr(bank[2][:, 0:P], sprob[:, b % 2, 0:P], P)
                tr(bank[2][0:64, P:2 * P], sprob[:, b % 2, P:192], P).then_inc(ss_t, 1)

            def ss_values(b):
                pe.wait_ge(ss_te, b + 1)
                if b >= 1:
                    pe.wait_ge(ss_o2, b)
                nc.tensor.matmul(bank[3][:, 0:256], spT[:, 0, :], vc[:, b % 2, :], start=True, stop=False)
                nc.tensor.matmul(bank[3][:, 0:256], spT[0:64, 1, :], avn[0:64, NT - 1, :], start=False,
                                 stop=True).then_inc(ss_v, 1)

            def ss_outputs(b):
                pe.wait_ge(ss_o2, b + 1)
                if b >= 1:
                    pe.wait_ge(ss_o, b)
                tr(bank[6][:, 0:P], o2[:, :], P).then_inc(ss_ot, 1)

            def attention():
                pe.wait_ge(free_a, FIRST_UNIT[ATT_AFTER + 1])
                pe.wait_ge(ml_te, 2 * S_PER)
                n = 8 * NKV
                at_scores(0)
                for u in range(n):
                    if u + 1 < n:
                        at_scores(u + 1)
                    at_rest(u)
                pe.wait_ge(at_p1, n)
                for x, i in enumerate((NT - 2, NT - 1)):
                    for p in range(2):
                        last = tr(bank[4 + x][0:rows_of(i), p * P:(p + 1) * P], akT[:, p, cols(i)], P)
                    last.then_inc(ko_t, 1)
                pe.wait_ge(at_m, n)
                pe.wait_ge(at_o, n)
                ss_keys(0)
                ss_scores(0)
                for b in range(NSEQ):
                    if b + 1 < NSEQ:
                        ss_keys(b + 1)
                    if b >= 1:
                        ss_outputs(b - 1)
                    ss_transposes(b)
                    if b + 1 < NSEQ:
                        ss_scores(b + 1)
                    ss_values(b)
                ss_outputs(NSEQ - 1)
                pe.wait_ge(ss_o2, NSEQ)

            pe.wait_ge(consts, 1)
            norm_transposes(0, xn)
            norm_transposes(1, xn)
            pe.wait_ge(w_lo_done, 1)
            for u in range(NT):
                if u + 2 < NT:
                    norm_transposes(u + 2, xn)
                pe.wait_ge(norm_lo, 2 * (u + 1))
                proj_unit(0, u)
            gate_transposes()
            for b in range(1, NPROJ):
                pe.wait_ge(w_lo_done, b + 1)
                for u in range(n_units(b)):
                    proj_unit(b, u)
                if b == 2:
                    q4_transposes()
                if b in ML_AFTER:
                    mlstm(ML_AFTER[b])
                if b == ATT_AFTER:
                    attention()

            for cq in range(4):
                b = NPROJ + cq
                pe.wait_ge(w_lo_done, b + 1)
                for i in range(NT):
                    m = NT * cq + i
                    if cq == 0:
                        pe.wait_ge(mg_lo, i + 1)
                    if m >= 4:
                        pe.wait_ge(free_v, m - 3)
                    step = 0
                    for k in range(KT):
                        for w, x in PASSES:
                            last = nc.tensor.matmul(bank[m % 4][0:rows_of(i), 0:WCOLS], x[:, k, cols(i)],
                                                    w_view(w, b, k), start=(step == 0), stop=(step == 3 * KT - 1))
                            step += 1
                    last.then_inc(gemm_v, 1)
            for t in range(NT, 2 * NT):
                norm_transposes(t, ybuf)

            def up(g, wait_b, slot, hslot):
                pe.wait_ge(w_lo_done, wait_b)
                for u in range(UP_UNITS):
                    tile, (c0, cn) = u // 3, CHUNKS[u % 3]
                    n = hslot * UP_UNITS + u
                    pe.wait_ge(free_a, g * UP_UNITS + (PROJ_UNITS + u - 3))
                    step = 0
                    for k in range(KT):
                        for w, x in PASSES:
                            last = nc.tensor.matmul(
                                bank[n % 4][:, 0:cn], w[:, slot, k * WCOLS + tile * P:k * WCOLS + (tile + 1) * P],
                                x[:, k, c0:c0 + cn], start=(step == 0), stop=(step == 3 * KT - 1))
                            step += 1
                    last.then_inc(gemm_a, 1)

            def down(g, wait_b, slot, hslot):
                pe.wait_ge(w_lo_done, wait_b)
                pe.wait_ge(lo_done, g * UP_UNITS + UP_UNITS)
                for i in range(NT):
                    for half in range(2):
                        d = hslot * DN_UNITS + 2 * i + half
                        pe.wait_ge(free_v, g * DN_UNITS + (OUT_UNITS + 2 * i + half - 3))
                        step = 0
                        for k in range(2):
                            for w, x in ((w_hi, hid_hi), (w_hi, hid_lo), (w_lo, hid_hi)):
                                last = nc.tensor.matmul(
                                    bank[4 + d % 4][0:rows_of(i), :], x[:, hslot, k, cols(i)],
                                    w[:, slot, k * D + half * 512:k * D + half * 512 + 512],
                                    start=(step == 0), stop=(step == 5))
                                step += 1
                        last.then_inc(gemm_v, 1)

            pe.wait_ge(norm_lo, 4 * NT)
            pe.wait_ge(free_v, OUT_UNITS)
            up(0, B_MLP + 1, 0, 0)
            with pe.Fori(0, NG // 2 - 1) as it:
                for x in range(2):
                    up(it * 2 + (1 + x), it * 4 + (B_MLP + 2 + 2 * x), 1, (1 + x) % 2)
                    down(it * 2 + x, it * 4 + (B_MLP + 3 + 2 * x), 0, x)
            up(NG - 1, B_MLP + 2 * NG - 2, 1, 1)
            down(NG - 2, B_MLP + 2 * NG - 1, 0, 0)
            down(NG - 1, B_MLP + 2 * NG, 1, 1)

        @block.scalar
        def _(act):
            chain = [0]

            def link(ins):
                chain[0] += 1
                ins.then_inc(act_chain, 1)
                act.wait_ge(act_chain, chain[0])

            def split(b):
                act.wait_ge(raw_in, RAW_AT[b])
                if b >= 2:
                    act.wait_ge(*done_before(b - 2))
                for src, dst in split_views(b):
                    ins = nc.scalar.activation(dst(w_hi), src, ACT.Copy)
                ins.then_inc(w_hi_done, 1)

            def square(t, src, to):
                rows = rows_of(t % NT)
                if t:
                    act.wait_ge(norm_sq, t)
                ins = nc.scalar.activation(to[0:rows, :], src, ACT.Square,
                                           accum_out=stat[0:rows, t // NT, t % NT:t % NT + 1])
                ins.then_inc(norm_sq, 1)

            def round_x(t):
                i = t % NT
                for h in range(2):
                    n = 2 * t + h
                    act.wait_ge(norm_tp, n + 1)
                    if t >= NT and h == 0:
                        act.wait_ge(gemm_v, 3 * NT + i + 1)
                    nc.scalar.activation(xT_hi[:, 4 * h:4 * h + 4, cols(i)], half_view(4 + n % 4, rows_of(i)),
                                         ACT.Copy).then_inc(norm_hi, 1)

            def read_unit(b, u):
                kind = BLOCKS[b][0]
                n = FIRST_UNIT[b] + u
                src = bank[n % 4]
                act.wait_ge(gemm_a, n + 1)
                if kind == "v":
                    r = rows_of(u)
                    off = 8 if b == 0 else 0
                    if b == 0:
                        nc.scalar.activation(gnat[0:r, u, :], src[0:r, 0:8], ACT.Copy)
                    if b == 4 and u == 0:
                        act.wait_ge(ml_su, 2 * NSEQ)
                    dst = vaug[0:r, u, BLOCKS[b][1] % 2, 0:DV]
                    nc.scalar.activation(dst, src[0:r, off:off + DV], ACT.Copy).then_inc(free_a, 1)
                elif kind == "av":
                    r = rows_of(u)
                    if u == 0:
                        act.wait_ge(cin_out, 32 * 8)
                        act.wait_ge(pc_out, 64)
                        act.wait_ge(ml_hn, 2 * S_PER)
                    nc.scalar.activation(avn[0:r, u, :], src[0:r, 0:WCOLS], ACT.Copy).then_inc(free_a, 1)
                elif kind in ("mk", "mq", "ak", "aq"):
                    tile, (c0, cn) = u // 3, CHUNKS[u % 3]
                    if kind == "aq":
                        j = BLOCKS[b][1] * GRP + 2 * BLOCKS[b][2] + tile
                        dst = aqT[:, j, c0:c0 + cn]
                    else:
                        dst = {"mk": mkT, "mq": mqT, "ak": akT}[kind][:, tile, c0:c0 + cn]
                    nc.scalar.activation(dst, src[:, 0:cn], ACT.Copy,
                                         scale=QK_SCALE if kind == "mq" else 1.0).then_inc(free_a, 1)
                else:
                    c0, cn = CHUNKS[u % 3]
                    m = n - FIRST_UNIT[14]
                    if m >= 2:
                        act.wait_ge(sg_use, m - 1)
                    nc.scalar.activation(sig[:, m % 2, 0:cn], src[:, 0:cn], ACT.Sigmoid).then_inc(free_a, 1)

            def gate_rows_act():
                act.wait_ge(const_in, 16 * 9)
                def row(dst, at, n, b, c, bias, wait):
                    act.wait_ge(gate_tp, wait)
                    return nc.scalar.activation(dst[:, at:at + n], bank[b][0:MH, c:c + n], ACT.Identity,
                                                bias=bias[:, :])
                row(row_i, 0, 512, 4, 0, bias_i, 1).then_inc(gate_ev, 1)
                row(row_i, 512, 512, 5, 0, bias_i, 2).then_inc(gate_ev, 1)
                row(row_i, 1024, 64, 6, 0, bias_i, 3).then_inc(gate_ev, 1)
                row(row_f, 1024, 64, 6, 64, bias_f, 3).then_inc(gate_ev, 1)
                row(row_f, 0, 512, 7, 0, bias_f, 4).then_inc(gate_ev, 1)
                row(row_f, 512, 512, 4, 0, bias_f, 5).then_inc(gate_ev, 1)
                act.wait_ge(gate_ev, 6)
                link(nc.scalar.activation(row_t[:, :], row_f[:, :], ACT.Abs))
                link(nc.scalar.activation(row_t[:, :], row_t[:, :], ACT.Exp, scale=-1.0))
                nc.scalar.activation(row_t[:, :], row_t[:, :], ACT.Ln, bias=1.0).then_inc(gate_ln, 1)

            def gate_exps():
                act.wait_ge(gate_arg, 1)
                nc.scalar.activation(row_t[:, :], row_t[:, :], ACT.Exp).then_inc(gate_exp, 1)
                nc.scalar.activation(q4[64:64 + MH, :], row_m[:, :], ACT.Exp, scale=-1.0).then_inc(gate_exp, 1)
                nc.scalar.activation(q4[96:96 + MH, :], row_i[:, :], ACT.Exp).then_inc(gate_exp, 1)

            def ml_first(s):
                p, i = divmod(s, S_PER)
                n = rows_of(i)
                if s == 0:
                    act.wait_ge(gate_nat, 1)
                act.wait_ge(ml_kt, s + 1)
                if s == NT + 1:
                    act.wait_ge(ml_kz, 2)
                elif s >= 2:
                    act.wait_ge(ml_u, s - 1 - s // NT if s != NT else NT - 1)
                for hh in range(2):
                    ins = nc.scalar.activation(kw[0:n, s % 2, hh, :], bank[4][0:n, hh * P:(hh + 1) * P], ACT.Copy,
                                               scale=nat[0:n, i, 3, 2 * p + hh:2 * p + hh + 1])
                ins.then_inc(ml_kw, 1)
                act.wait_ge(ml_wa, s + 1)
                nc.scalar.activation(wgt[0:n, s % 2, :, 0:n], wgt[0:n, s % 2, :, 0:n], ACT.Exp).then_inc(ml_we, 1)

            def ml_second(s):
                p, i = divmod(s, S_PER)
                n = rows_of(i)
                act.wait_ge(ml_n, s + 1)
                for hh in range(2):
                    ins = nc.scalar.activation(small[0:n, s % 2, hh:hh + 1], bank[6 + hh][0:n, DV:VA], ACT.Abs)
                ins.then_inc(ml_ab, 1)
                act.wait_ge(ml_rc, s + 1)
                if s >= 2:
                    act.wait_ge(ml_t, s - 1)
                nc.scalar.activation(hh_b[0:n, s % 2, :, 0, :], by_group(bank[6][0:n, 0:DV]), ACT.Copy,
                                     scale=small[0:n, s % 2, 2:3]).then_inc(ml_h0, 1)
                for hh in range(2):
                    act.wait_ge((ml_h0, ml_h1)[hh], s + 1)
                    if s or hh:
                        act.wait_ge(ml_ss, 2 * s + hh)
                    ins = nc.scalar.activation(by_group(hjunk[0:n, :]), hh_b[0:n, s % 2, :, hh, :], ACT.Square,
                                               accum_out=small[0:n, s % 2, 4 + hh:5 + hh])
                    ins.then_inc(ml_ss, 1)

            def ml_third(s):
                p, i = divmod(s, S_PER)
                n = rows_of(i)
                act.wait_ge(ml_t, s + 1)
                nc.scalar.activation(hT[:, p * GRP:(p + 1) * GRP, cols(i)], half_view(2, n), ACT.Copy)\
                    .then_inc(ml_te, 1)

            def mlstm_act(p):
                s0 = p * S_PER
                ml_first(s0)
                for s in range(s0, s0 + S_PER):
                    if s + 1 < s0 + S_PER:
                        ml_first(s + 1)
                    ml_second(s)
                    if s > s0:
                        ml_third(s - 1)
                ml_third(s0 + S_PER - 1)

            def at_exps(u):
                i = u // NKV
                lo = 0 if i else P
                act.wait_ge(at_m, u + 1)
                nc.scalar.activation(ast[:, u % 2, 3, :], ast[:, u % 2, 3, :], ACT.Exp)
                for g in range(GRP):
                    v = prob[:, u % 2, g, lo:]
                    ins = nc.scalar.activation(v, v, ACT.Exp, bias=ast[:, u % 2, 2, g:g + 1], scale=ATT_SCALE,
                                               accum_out=ast[:, u % 2, 4, g:g + 1])
                ins.then_inc(at_e, 1)

            def at_prev(u):
                if u < NKV:
                    return
                act.wait_ge(at_t, u + 1)
                act.wait_ge(at_v, u)
                nc.scalar.activation(pT[:, 0, :], bank[4][:, :], ACT.Copy).then_inc(at_p0, 1)

            def at_out(u):
                i, kv = divmod(u, NKV)
                p, half = divmod(kv, 2)
                at = slice(64 * half, 64 * half + 64)
                act.wait_ge(at_v, u + 1)
                nc.scalar.activation(aqT[at, p * GRP:(p + 1) * GRP, cols(i)],
                                     bank[6 + u % 2][at, :].rearrange("c (g t) -> c g t", g=GRP),
                                     ACT.Copy).then_inc(at_o, 1)

            def ss_keys(b):
                act.wait_ge(sk_t, b + 1)
                if b >= 2:
                    act.wait_ge(ss_s, b - 1)
                nc.scalar.activation(kcT[:, b % 2, :, :], bank[0][:, 0:256].rearrange("c (p w) -> c p w", p=2),
                                     ACT.Copy).then_inc(sk_e, 1)

            def ss_exps(b):
                act.wait_ge(ss_m, b + 1)
                nc.scalar.activation(sst[:, b % 2, 3:4], sst[:, b % 2, 3:4], ACT.Exp)
                nc.scalar.activation(sprob[:, b % 2, :], sprob[:, b % 2, :], ACT.Exp, bias=sst[:, b % 2, 2:3],
                                     scale=ATT_SCALE, accum_out=sst[:, b % 2, 4:5]).then_inc(ss_e, 1)

            def ss_pT(b):
                act.wait_ge(ss_t, b + 1)
                if b >= 1:
                    act.wait_ge(ss_v, b)
                nc.scalar.activation(spT[:, 0, :], bank[2][:, 0:P], ACT.Copy)
                nc.scalar.activation(spT[0:64, 1, :], bank[2][0:64, P:2 * P], ACT.Copy).then_inc(ss_te, 1)

            def ss_out(b):
                act.wait_ge(ss_ot, b + 1)
                for half in range(2):
                    at = slice(64 * half, 64 * half + 64)
                    src = bank[6][at, 0:P].rearrange("c (p h r) -> c p h r", p=2, h=2)[:, :, half, :]
                    dst = aqT[at, :, SEQ + b * DSEQ:SEQ + (b + 1) * DSEQ]
                    for p in range(2):
                        ins = nc.scalar.activation(dst[:, p * GRP:(p + 1) * GRP, :],
                                                   src[:, p, :].rearrange("c (g t) -> c g t", g=GRP), ACT.Copy)
                ins.then_inc(ss_o, 1)

            def attention_act():
                n = 8 * NKV
                at_exps(0)
                for u in range(n):
                    if u + 1 < n:
                        at_exps(u + 1)
                    at_prev(u)
                    if u >= 1:
                        at_out(u - 1)
                at_out(n - 1)
                ss_keys(0)
                act.wait_ge(ko_t, 2)
                nc.scalar.activation(kout[:, 0, :], bank[4][:, 0:256], ACT.Copy).then_inc(ko_e, 1)
                nc.scalar.activation(kout[0:64, 1, :], bank[5][0:64, 0:256], ACT.Copy).then_inc(ko_e, 1)
                ss_exps(0)
                for b in range(NSEQ):
                    if b + 1 < NSEQ:
                        ss_keys(b + 1)
                    if b >= 1:
                        ss_out(b - 1)
                    ss_pT(b)
                    if b + 1 < NSEQ:
                        ss_exps(b + 1)
                ss_out(NSEQ - 1)

            def square_x(i):
                act.wait_ge(x_in[i % 3], 16 * (i // 3 + 1))
                square(i, xin[0:rows_of(i), i % 3, :], junk)

            square_x(0)
            square_x(1)
            round_x(0)
            split(0)
            square_x(2)
            round_x(1)
            for u in range(NT):
                if u + 3 < NT:
                    square_x(u + 3)
                if u + 2 < NT:
                    round_x(u + 2)
                if u == 4:
                    split(1)
                read_unit(0, u)
            gate_rows_act()
            for b in range(1, NPROJ):
                split(b + 1)
                if b == 2:
                    gate_exps()
                for u in range(n_units(b)):
                    read_unit(b, u)
                if b in ML_AFTER:
                    mlstm_act(ML_AFTER[b])
                if b == ATT_AFTER:
                    attention_act()

            act.wait_ge(gemm_a, PROJ_UNITS)
            act.wait_ge(sg_use, 72)
            for i in range(NT):
                nc.scalar.activation(xT_hi[:, :, cols(i)], hT[:, :, cols(i)], ACT.Copy).then_inc(mg_hi, 1)
            split(NPROJ + 1)
            split(NPROJ + 2)
            split(NPROJ + 3)

            def split_mlp(raw_n, slot, waits):
                act.wait_ge(raw_in, raw_n)
                for w in waits:
                    act.wait_ge(*w)
                n = KT * WCOLS
                nc.scalar.activation(w_hi[:, slot, 0:n], raw[:, 0:n], ACT.Copy).then_inc(w_hi_done, 1)

            split_mlp(RAW_ALL + 16, 0, [(gemm_v, 3 * NT)])
            for i in range(NT):
                t = NT + i
                act.wait_ge(free_v, 3 * NT + i + 1)
                square(t, x2[0:rows_of(i), i, :], junk2)
                if i >= 1:
                    round_x(t - 1)
            round_x(2 * NT - 1)

            def read_up(g, hslot):
                for u in range(UP_UNITS):
                    tile, (c0, cn) = u // 3, CHUNKS[u % 3]
                    n = hslot * UP_UNITS + u
                    act.wait_ge(gemm_a, g * UP_UNITS + (PROJ_UNITS + u + 1))
                    if u >= 2:
                        act.wait_ge(lo_done, g * UP_UNITS + (u - 1))
                    elif not isinstance(g, int) or g:
                        act.wait_ge(lo_done, g * UP_UNITS + (u - 1))
                    nc.scalar.activation(relu[:, u % 2, 0:cn], bank[n % 4][:, 0:cn], ACT.Relu).then_inc(free_a, 1)
                    act.wait_ge(free_a, g * UP_UNITS + (PROJ_UNITS + u + 1))
                    nc.scalar.activation(hid_hi[:, hslot, tile, c0:c0 + cn], relu[:, u % 2, 0:cn],
                                         ACT.Square).then_inc(hi_done, 1)

            split_mlp(RAW_ALL + 32, 1, [(gemm_v, OUT_UNITS)])
            read_up(0, 0)
            with act.Fori(0, NG // 2 - 1) as it:
                for x in range(2):
                    g = it * 2 + (1 + x)
                    split_mlp(it * 64 + (RAW_ALL + 48 + 32 * x), 0,
                              [(gemm_v, it * (2 * DN_UNITS) + (OUT_UNITS + DN_UNITS * x)),
                               (gemm_a, it * (2 * UP_UNITS) + (PROJ_UNITS + UP_UNITS * (1 + x)))])
                    read_up(g, (1 + x) % 2)
                    split_mlp(it * 64 + (RAW_ALL + 64 + 32 * x), 1,
                              [(gemm_a, it * (2 * UP_UNITS) + (PROJ_UNITS + UP_UNITS * (2 + x)))])
            g = NG - 1
            split_mlp(RAW_ALL + 16 * (2 * g + 1), 0, [(gemm_v, OUT_UNITS + DN_UNITS * (g - 1))])
            read_up(g, 1)
            split_mlp(RAW_ALL + 16 * (2 * g + 2), 1, [(gemm_a, PROJ_UNITS + UP_UNITS * NG)])
            for i in range(NT):
                act.wait_ge(free_v, OUT_UNITS + DN_UNITS * g + 2 * i + 2)
                square(2 * NT + i, x2[0:rows_of(i), i, :], junk2)

        @block.vector
        def _(dve):
            chain = [0]

            def link(ins):
                chain[0] += 1
                ins.then_inc(dve_chain, 1)
                dve.wait_ge(dve_chain, chain[0])

            def split(b):
                dve.wait_ge(w_hi_done, b + 1)
                for src, dst in split_views(b):
                    ins = nc.vector.tensor_tensor(dst(w_lo), src, dst(w_hi).bitcast(F32), ALU.subtract)
                ins.then_inc(w_lo_done, 1)

            def normalise(t, src, dst, wait_slot):
                i = t % NT
                rows = rows_of(i)
                dve.wait_ge(norm_rs, t + 1)
                wait_slot()
                return nc.vector.scalar_tensor_tensor(dst[0:rows, i % 2, :], src, rstd[0:rows, t // NT, i:i + 1],
                                                      gain_b[0:rows, :], ALU.mult, ALU.mult)

            def norm_tile(t, src, dst):
                def slot():
                    if t % NT >= 2:
                        dve.wait_ge(norm_tp, 2 * (t - 1))
                normalise(t, src, dst, slot).then_inc(norm_xn, 1)

            def rest_x(t):
                i = t % NT
                for h in range(2):
                    n = 2 * t + h
                    dve.wait_ge(norm_hi, n + 1)
                    out = xT_lo[:, 4 * h:4 * h + 4, cols(i)]
                    nc.vector.tensor_tensor(out, half_view(4 + n % 4, rows_of(i)),
                                            xT_hi[:, 4 * h:4 * h + 4, cols(i)].bitcast(F32),
                                            ALU.subtract).then_inc(norm_lo, 1)

            def gate_scans():
                dve.wait_ge(gate_ln, 1)
                dve.wait_ge(consts, 3)
                link(nc.vector.scalar_tensor_tensor(row_f[:, :], row_f[:, :], 0.0, row_t[:, :], ALU.min, ALU.subtract))
                nc.vector.tensor_tensor_scan(row_b[:, :], row_r[:, :], row_f[:, :], 0.0, ALU.mult, ALU.add)
                nc.vector.tensor_tensor_scan(row_m[:, 0:SEQ], row_f[:, 0:SEQ], row_i[:, 0:SEQ], 0.0, ALU.add, ALU.max)
                for b in range(NSEQ):
                    at = slice(SEQ + b * DSEQ, SEQ + (b + 1) * DSEQ)
                    ins = nc.vector.tensor_tensor_scan(row_m[:, at], row_f[:, at], row_i[:, at], sm_rows[:, b:b + 1],
                                                       ALU.add, ALU.max)
                link(ins)
                nc.vector.tensor_tensor(q4[0:MH, :], row_i[:, :], row_b[:, :], ALU.subtract)
                link(nc.vector.tensor_tensor(row_x[:, :], row_b[:, :], row_m[:, :], ALU.subtract))

                def runs(t, a, b, n):
                    return t[0:MH, a:b].rearrange("h (c t) -> h c t", t=n)

                def spread(v, c, n):
                    return v.unsqueeze(2).broadcast_to([MH, c, n])

                nc.vector.tensor_copy(row_t[:, 0:P], row_x[:, 0:P])
                nc.vector.tensor_tensor(runs(row_t, P, SEQ, P), runs(row_x, P, SEQ, P),
                                        spread(row_m[:, P - 1:SEQ - P:P], SEQ // P - 1, P), ALU.add)
                nc.vector.tensor_tensor(runs(row_t, SEQ, T, DSEQ), runs(row_x, SEQ, T, DSEQ),
                                        spread(sm_rows[:, :], NSEQ, DSEQ), ALU.add)
                nc.vector.tensor_tensor(runs(row_i, 0, SEQ, P), runs(q4, 0, SEQ, P),
                                        spread(row_x[:, P - 1:SEQ:P], SEQ // P, P), ALU.add)
                nc.vector.tensor_tensor(runs(row_i, SEQ, T, DSEQ), runs(q4, SEQ, T, DSEQ),
                                        spread(row_x[:, SEQ + DSEQ - 1:T:DSEQ], NSEQ, DSEQ), ALU.add)\
                    .then_inc(gate_arg, 1)

            def gate_ends():
                dve.wait_ge(gate_exp, 1)
                nc.vector.tensor_copy(ends[:, 0:8], row_t[:, P - 1:SEQ:P])
                nc.vector.tensor_copy(ends[:, 8:16], row_t[:, SEQ + DSEQ - 1:T:DSEQ])
                nc.vector.tensor_copy(m_out[:, 0:NSEQ], row_m[:, SEQ + DSEQ - 1:T:DSEQ])
                nc.vector.tensor_copy(m_out[:, NSEQ:NSEQ + 1], row_m[:, SEQ - 1:SEQ]).then_inc(gate_fin, 1)

            def gate_columns():
                dve.wait_ge(gate_q4, 3)
                for b, i0, k, r in ((4, 0, 4, P), (5, 4, 4, P), (6, 8, 1, 64)):
                    for q in range(4):
                        if q != 1:
                            src = bank[b][0:r, 0:k * P].rearrange("t (i q h) -> t i q h", q=4, h=32)[:, :, q, 0:MH]
                            ins = nc.vector.tensor_copy(nat[0:r, i0:i0 + k, q, :], src)
                ins.then_inc(gate_nat, 1)

            def ml_first(s):
                p, i = divmod(s, S_PER)
                n = rows_of(i)
                dve.wait_ge(bc_in[s % 2], 32 * (s // 2 + 1))
                if s >= 2:
                    dve.wait_ge(ml_n, s - 1)
                if s == 0:
                    dve.wait_ge(gate_nat, 1)
                    dve.wait_ge(consts, 3)
                mask = causal if n == P else causal8
                for hh in range(2):
                    ins = nc.vector.scalar_tensor_tensor(wgt[0:n, s % 2, hh, 0:n], bc[0:n, s % 2, hh, 0:n],
                                                         nat[0:n, i, 0, 2 * p + hh:2 * p + hh + 1], mask[0:n, 0:n],
                                                         ALU.add, ALU.min)
                ins.then_inc(ml_wa, 1)
                dve.wait_ge(ml_st, s + 1)
                dve.wait_ge(ml_we, s + 1)
                w = wgt[0:n, s % 2, :, 0:n]
                nc.vector.tensor_tensor(w, bank[5][0:n, 0:256].rearrange("s (h t) -> s h t", h=2)[:, :, 0:n], w,
                                        ALU.mult).then_inc(ml_sw, 1)

            def ml_norm(s):
                n = rows_of(s % S_PER)
                dve.wait_ge(ml_rs, s + 1)
                for hh in range(2):
                    v = hh_b[0:n, s % 2, :, hh, :]
                    ins = nc.vector.tensor_scalar(v, v, small[0:n, s % 2, 6 + hh:7 + hh], None, ALU.mult)
                ins.then_inc(ml_hn, 1)

            def sampled_states(p, hh):
                for b in range(NSEQ):
                    dve.wait_ge(ml_su, (2 * p + hh) * NSEQ + b + 1)
                    v = Cin[:, b // 4, b % 4, :]
                    nc.vector.scalar_tensor_tensor(v, v, dec[:, 2 * p + hh, 8 + b:9 + b], bank[b % 2][:, 0:VA],
                                                   ALU.mult, ALU.add).then_inc(ml_sc, 1)

            def ml_second(s):
                p, i = divmod(s, S_PER)
                n = rows_of(i)
                if i == NT - 1:
                    sampled_states(p, 0)
                dve.wait_ge(ml_ab, s + 1)
                link(nc.vector.tensor_tensor(small[0:n, s % 2, 2:4], small[0:n, s % 2, 0:2],
                                             nat[0:n, i, 2, 2 * p:2 * p + 2], ALU.max))
                ins = nc.vector.reciprocal(small[0:n, s % 2, 2:4], small[0:n, s % 2, 2:4])
                ins.then_inc(ml_rc, 1)
                dve.wait_ge(ml_rc, s + 1)
                nc.vector.tensor_scalar(hh_b[0:n, s % 2, :, 1, :], by_group(bank[7][0:n, 0:DV]), small[0:n, s % 2, 3:4], None,
                                        ALU.mult).then_inc(ml_h1, 1)
                if i < NT - 1:
                    c = (NT - 1) * p + i
                    dve.wait_ge(ml_u, c + 1)
                    if i == 0:
                        dve.wait_ge(dec_in, 16)
                        dve.wait_ge(ml_cl, p + 1)
                    else:
                        dve.wait_ge(ml_c, c)
                    for hh in range(2):
                        ins = nc.vector.scalar_tensor_tensor(Cst[:, hh, :], Cst[:, hh, :],
                                                             dec[:, 2 * p + hh, i:i + 1], bank[hh][:, 0:VA],
                                                             ALU.mult, ALU.add)
                    ins.then_inc(ml_c, 1)
                    return
                sampled_states(p, 1)

            def mlstm_dve(p):
                s0 = p * S_PER
                ml_first(s0)
                for s in range(s0, s0 + S_PER):
                    if s + 1 < s0 + S_PER:
                        ml_first(s + 1)
                    if s > s0:
                        ml_norm(s - 1)
                    ml_second(s)
                ml_norm(s0 + S_PER - 1)

            def at_mask(u):
                i, kv = divmod(u, NKV)
                lo = 0 if i else P
                dve.wait_ge(at_s, u + 1)
                if u == 0:
                    dve.wait_ge(consts, 6)
                if u >= 2:
                    dve.wait_ge(at_t, u - 1)
                st = ast[:, u % 2]
                for g in range(GRP):
                    src = bank[2 * (u % 2) + g // 2][:, (g % 2) * 256 + lo:(g % 2) * 256 + 256]
                    ins = nc.vector.tensor_tensor_reduce(out=prob[:, u % 2, g, lo:], in0=src, in1=amask[:, lo:],
                                                         scale=1.0, scalar=-BIG, op0=ALU.add, op1=ALU.max,
                                                         accum_out=st[:, 0, g:g + 1])
                link(ins)
                sk = sink_b[:, kv * GRP:(kv + 1) * GRP]
                link(nc.vector.scalar_tensor_tensor(st[:, 1, :], st[:, 0, :], ATT_SCALE, sk, ALU.mult, ALU.max))
                nc.vector.tensor_scalar(st[:, 2, :], st[:, 1, :], -1.0, None, ALU.mult)
                nc.vector.tensor_tensor(st[:, 3, :], sk, st[:, 1, :], ALU.subtract).then_inc(at_m, 1)

            def at_divide(u):
                lo = 0 if u >= NKV else P
                dve.wait_ge(at_e, u + 1)
                st = ast[:, u % 2]
                link(nc.vector.tensor_tensor(st[:, 5, :], st[:, 4, :], st[:, 3, :], ALU.add))
                link(nc.vector.reciprocal(st[:, 5, :], st[:, 5, :]))
                for g in range(GRP):
                    v = prob[:, u % 2, g, lo:]
                    ins = nc.vector.tensor_scalar(v, v, st[:, 5, g:g + 1], None, ALU.mult)
                ins.then_inc(at_p, 1)

            def at_own(u):
                dve.wait_ge(at_t, u + 1)
                if u >= 1:
                    dve.wait_ge(at_v, u)
                nc.vector.tensor_copy(pT[:, 1, :], bank[5][:, :]).then_inc(at_p1, 1)

            def ss_mask(b):
                dve.wait_ge(ss_s, b + 1)
                if b == 0:
                    dve.wait_ge(mask_io, 16 * 17)
                if b >= 2:
                    dve.wait_ge(ss_t, b - 1)
                st = sst[:, b % 2]
                link(nc.vector.tensor_tensor_reduce(out=sprob[:, b % 2, :], in0=bank[1][:, 0:192], in1=smask[:, b, :],
                                                    scale=1.0, scalar=-BIG, op0=ALU.add, op1=ALU.max,
                                                    accum_out=st[:, 0:1]))
                link(nc.vector.scalar_tensor_tensor(st[:, 1:2], st[:, 0:1], ATT_SCALE, sink_s[:, :], ALU.mult, ALU.max))
                nc.vector.tensor_scalar(st[:, 2:3], st[:, 1:2], -1.0, None, ALU.mult)
                nc.vector.tensor_tensor(st[:, 3:4], sink_s[:, :], st[:, 1:2], ALU.subtract).then_inc(ss_m, 1)

            def ss_divide(b):
                dve.wait_ge(ss_e, b + 1)
                st = sst[:, b % 2]
                link(nc.vector.tensor_tensor(st[:, 5:6], st[:, 4:5], st[:, 3:4], ALU.add))
                link(nc.vector.reciprocal(st[:, 5:6], st[:, 5:6]))
                v = sprob[:, b % 2, :]
                nc.vector.tensor_scalar(v, v, st[:, 5:6], None, ALU.mult).then_inc(ss_p, 1)

            def ss_gather(b):
                dve.wait_ge(ss_v, b + 1)
                if b >= 1:
                    dve.wait_ge(ss_ot, b)
                if b == 0:
                    link(nc.vector.memset(o2[:, :], 0.0))
                for kv in range(NKV):
                    at = slice(32 * kv, 32 * kv + 32)
                    half = kv % 2
                    ins = nc.vector.tensor_copy(o2[at, 64 * half:64 * half + 64], bank[3][at, kv * HD:(kv + 1) * HD])
                ins.then_inc(ss_o2, 1)

            def attention_dve():
                n = 8 * NKV
                at_mask(0)
                for u in range(n):
                    if u + 1 < n:
                        at_mask(u + 1)
                    at_divide(u)
                    at_own(u)
                dve.wait_ge(at_v, n)
                for p in range(2):
                    ins = nc.vector.tensor_copy(qsmp[:, p, :, :, :].rearrange("c b g t -> c g b t"),
                                                aqT[:, p * GRP:(p + 1) * GRP, SEQ:T]
                                                .rearrange("c g (b t) -> c g b t", t=DSEQ))
                ins.then_inc(ss_q, 1)
                ss_mask(0)
                for b in range(NSEQ):
                    ss_divide(b)
                    if b >= 1:
                        ss_gather(b - 1)
                    if b + 1 < NSEQ:
                        ss_mask(b + 1)
                ss_gather(NSEQ - 1)

            def gated(b, u):
                kind, p, gg = BLOCKS[b]
                m = FIRST_UNIT[b] + u - FIRST_UNIT[14]
                tile, (c0, cn) = u // 3, CHUNKS[u % 3]
                j = p * GRP + 2 * gg + tile
                dve.wait_ge(free_a, FIRST_UNIT[b] + u + 1)
                h = hT[:, j, c0:c0 + cn]
                g = sig[:, m % 2, 0:cn]
                if kind == "mo":
                    nc.vector.scalar_tensor_tensor(h, h, mnorm[:, j:j + 1], g, ALU.mult, ALU.mult).then_inc(sg_use, 1)
                elif kind == "ga":
                    dve.wait_ge(sg_use, m - 5)
                    nc.vector.tensor_tensor(h, h, g, ALU.mult).then_inc(sg_use, 1)
                else:
                    a = aqT[:, j, c0:c0 + cn]
                    dve.wait_ge(sg_use, m - 5)
                    link(nc.vector.tensor_tensor(a, a, g, ALU.mult))
                    nc.vector.tensor_tensor(h, h, a, ALU.add).then_inc(sg_use, 1)

            dve.wait_ge(gain_in, 16)
            norm_tile(0, xin[:, 0, :], xn)
            norm_tile(1, xin[:, 1, :], xn)
            rest_x(0)
            split(0)
            norm_tile(2, xin[:, 2, :], xn)
            rest_x(1)
            for i in range(3, NT + 1):
                if i < NT:
                    norm_tile(i, xin[0:rows_of(i), i % 3, :], xn)
                rest_x(i - 1)
                if i == 6:
                    split(1)
            for b in range(1, NPROJ):
                if b == 2:
                    gate_ends()
                split(b + 1)
                if b == 1:
                    gate_scans()
                if b == 3:
                    gate_columns()
                if b in ML_AFTER:
                    mlstm_dve(ML_AFTER[b])
                if b == ATT_AFTER:
                    attention_dve()
                if b >= 14:
                    for u in range(n_units(b)):
                        gated(b, u)

            for i in range(NT):
                dve.wait_ge(mg_hi, i + 1)
                nc.vector.tensor_tensor(xT_lo[:, :, cols(i)], hT[:, :, cols(i)], xT_hi[:, :, cols(i)].bitcast(F32),
                                        ALU.subtract).then_inc(mg_lo, 1)
            for cq in range(4):
                if cq < 3:
                    split(NPROJ + 1 + cq)
                for i in range(NT):
                    m = NT * cq + i
                    r = rows_of(i)
                    if cq == 0:
                        dve.wait_ge(x2_in[i], 16)
                    dve.wait_ge(gemm_v, m + 1)
                    v = x2[0:r, i, cq * WCOLS:(cq + 1) * WCOLS]
                    nc.vector.tensor_tensor(v, bank[m % 4][0:r, 0:WCOLS], v, ALU.add).then_inc(free_v, 1)

            def split_mlp(count, slot):
                dve.wait_ge(w_hi_done, count)
                n = KT * WCOLS
                nc.vector.tensor_tensor(w_lo[:, slot, 0:n], raw[:, 0:n], w_hi[:, slot, 0:n].bitcast(F32),
                                        ALU.subtract).then_inc(w_lo_done, 1)

            split_mlp(B_MLP + 1, 0)
            dve.wait_ge(gain_in, 32)
            for i in range(NT):
                norm_tile(NT + i, x2[0:rows_of(i), i, :], ybuf)
                if i >= 1:
                    rest_x(NT + i - 1)
            rest_x(2 * NT - 1)

            def hidden(g, hslot):
                for u in range(UP_UNITS):
                    tile, (c0, cn) = u // 3, CHUNKS[u % 3]
                    dve.wait_ge(free_a, g * UP_UNITS + (PROJ_UNITS + u + 1))
                    nc.vector.tensor_tensor(sqr[:, u % 2, 0:cn], relu[:, u % 2, 0:cn], relu[:, u % 2, 0:cn],
                                            ALU.mult).then_inc(sq_done, 1)
                    dve.wait_ge(sq_done, g * UP_UNITS + (u + 1))
                    dve.wait_ge(hi_done, g * UP_UNITS + (u + 1))
                    nc.vector.tensor_tensor(hid_lo[:, hslot, tile, c0:c0 + cn], sqr[:, u % 2, 0:cn],
                                            hid_hi[:, hslot, tile, c0:c0 + cn].bitcast(F32),
                                            ALU.subtract).then_inc(lo_done, 1)

            def accumulate(g, hslot, i):
                for half in range(2):
                    r = rows_of(i)
                    d = hslot * DN_UNITS + 2 * i + half
                    dve.wait_ge(gemm_v, g * DN_UNITS + (OUT_UNITS + 2 * i + half + 1))
                    v = x2[0:r, i, half * 512:half * 512 + 512]
                    nc.vector.tensor_tensor(v, bank[4 + d % 4][0:r, :], v, ALU.add).then_inc(free_v, 1)

            split_mlp(B_MLP + 2, 1)
            hidden(0, 0)
            with dve.Fori(0, NG // 2 - 1) as it:
                for x in range(2):
                    split_mlp(it * 4 + (B_MLP + 3 + 2 * x), 0)
                    hidden(it * 2 + (1 + x), (1 + x) % 2)
                    split_mlp(it * 4 + (B_MLP + 4 + 2 * x), 1)
                    for i in range(NT):
                        accumulate(it * 2 + x, x, i)
            split_mlp(B_MLP + 2 * NG - 1, 0)
            hidden(NG - 1, 1)
            split_mlp(B_MLP + 2 * NG, 1)
            for i in range(NT):
                accumulate(NG - 2, 0, i)
            dve.wait_ge(gain_in, 48)

            def final(i):
                def slot():
                    if i >= 2:
                        dve.wait_ge(y_out[i % 2], 16 * (i // 2))
                normalise(2 * NT + i, x2[0:rows_of(i), i, :], ybuf, slot).then_inc(y_rdy, 1)

            for i in range(NT):
                accumulate(NG - 1, 1, i)
                if i >= 1:
                    final(i - 1)
            final(NT - 1)

        @block.gpsimd
        def _(pool):
            chain = [0]

            def link(ins):
                chain[0] += 1
                ins.then_inc(pool_chain, 1)
                pool.wait_ge(pool_chain, chain[0])

            def keep_where(t, pattern, base, ch, op, fill):
                return nc.gpsimd.affine_select(out=t, in_=t, compare_op=op, fill=fill, base=base, pattern=pattern,
                                               channel_multiplier=ch)

            nc.gpsimd.memset(neghalf[:, :], -0.5)
            link(nc.gpsimd.memset(ident[:, :], 0.0))
            keep_where(ident[:, :], [[-1, P]], 0, 1, ALU.not_equal, 1.0).then_inc(consts, 1)

            def rms(t):
                rows = rows_of(t % NT)
                pool.wait_ge(norm_sq, t + 1)
                v = rstd[0:rows, t // NT, t % NT:t % NT + 1]
                link(nc.gpsimd.tensor_scalar(v, stat[0:rows, t // NT, t % NT:t % NT + 1], 1.0 / D, EPS,
                                             ALU.mult, ALU.add))
                nc.gpsimd.tensor_tensor(v, v, neghalf[0:rows, 0:1], ALU.pow).then_inc(norm_rs, 1)

            for t in range(NT):
                rms(t)
            nc.gpsimd.memset(causal8[:, :], BIG)
            nc.gpsimd.memset(seq_ind[:, :], 1.0)
            nc.gpsimd.memset(vaug[:, :, :, DV:VA], 1.0)
            link(nc.gpsimd.memset(causal[:, :], BIG))
            keep_where(causal[:, :], [[1, P]], 0, -1, ALU.is_ge, -BIG)
            link(keep_where(causal8[:, :], [[1, 64]], 0, -1, ALU.is_ge, -BIG))
            c8 = causal8[:, :].rearrange("s (b t) -> s b t", t=DSEQ)
            keep_where(c8, [[-DSEQ, NSEQ], [0, DSEQ]], 0, 1, ALU.is_ge, -BIG)
            link(keep_where(seq_ind[:, :], [[-DSEQ, NSEQ]], 0, 1, ALU.is_ge, 0.0))
            keep_where(seq_ind[:, :], [[DSEQ, NSEQ]], DSEQ - 1, -1, ALU.is_ge, 0.0)
            nc.gpsimd.memset(qz[:, :, :], 0.0)
            nc.gpsimd.memset(Cst[:, :, :], 0.0).then_inc(ml_cl, 1)
            pool.wait_ge(norm_tp, 2 * NT)
            pool.wait_ge(norm_xn, NT)
            nc.gpsimd.memset(q4[:, :], 0.0).then_inc(consts, 1)
            link(nc.gpsimd.memset(row_r[:, :], 1.0))
            nc.gpsimd.memset(row_r[:, 0:SEQ:P], 0.0)
            nc.gpsimd.memset(row_r[:, SEQ:T:DSEQ], 0.0).then_inc(consts, 1)

            def ml_query(s):
                p, i = divmod(s, S_PER)
                n = rows_of(i)
                pool.wait_ge(bc_in[s % 2], 32 * (s // 2 + 1))
                if i == 0:
                    pool.wait_ge(free_a, FIRST_UNIT[4 * p + 4])
                if i < NT - 1:
                    if s >= 2:
                        pool.wait_ge(ml_n, s - 1)
                    nc.gpsimd.tensor_tensor(qs[:, s % 2, :, 0:n], mqT[:, :, cols(i)], bc[:, s % 2, 2:4, 0:n],
                                            ALU.mult).then_inc(ml_qs, 1)
                    return
                for hh in range(2):
                    dst = qz[:, hh, :].rearrange("c (b x) -> c b x", x=72)[:, :, 0:DSEQ]
                    ins = nc.gpsimd.tensor_tensor(dst, mqT[:, hh, cols(i)].rearrange("c (b t) -> c b t", t=DSEQ),
                                                  bc[:, s % 2, 2 + hh, 0:n].rearrange("c (b t) -> c b t", t=DSEQ),
                                                  ALU.mult)
                ins.then_inc(ml_qs, 1)

            def ml_keys(s, hh):
                p = s // S_PER
                n = rows_of(NT - 1)
                pool.wait_ge(ml_kw, s + 1)
                if hh or p:
                    pool.wait_ge(ml_su, (2 * p + hh) * NSEQ)
                nc.gpsimd.tensor_tensor(kwz[:, :, :],
                                        kw[0:n, s % 2, hh, :].unsqueeze(1).broadcast_to([n, NSEQ, DK]),
                                        seq_ind[:, :].unsqueeze(2).broadcast_to([n, NSEQ, DK]),
                                        ALU.mult).then_inc(ml_kz, 1)

            def ml_rms(s):
                n = rows_of(s % S_PER)
                pool.wait_ge(ml_ss, 2 * s + 2)
                v = small[0:n, s % 2, 6:8]
                link(nc.gpsimd.tensor_scalar(v, small[0:n, s % 2, 4:6], 1.0 / DV, EPS, ALU.mult, ALU.add))
                nc.gpsimd.tensor_tensor(v, v, neghalf[0:n, :], ALU.pow).then_inc(ml_rs, 1)

            for p in range(2):
                if p:
                    pool.wait_ge(pc_out, 32)
                    nc.gpsimd.memset(Cst[:, :, :], 0.0).then_inc(ml_cl, 1)
                s0 = p * S_PER
                ml_query(s0)
                for s in range(s0, s0 + S_PER):
                    if s + 1 < s0 + S_PER:
                        ml_query(s + 1)
                    if s == s0 + NT - 2:
                        ml_keys(s + 1, 0)
                    if s == s0 + NT - 1:
                        ml_keys(s, 1)
                    ml_rms(s)

            pool.wait_ge(cin_out, 32 * 8)
            pool.wait_ge(pc_out, 64)
            pool.wait_ge(ml_hn, 2 * S_PER)
            pool.wait_ge(ml_t, 2 * S_PER)
            link(nc.gpsimd.memset(amask[:, :], 0.0))
            keep_where(amask[:, 0:P], [[1, P]], -1, -1, ALU.is_ge, -BIG).then_inc(consts, 2)
            keep_where(amask[:, P:2 * P], [[-1, P]], 0, 1, ALU.is_ge, -BIG).then_inc(consts, 1)
            pool.wait_ge(at_v, 8 * NKV)
            pool.wait_ge(at_o, 8 * NKV)
            link(nc.gpsimd.memset(smask[0:DSEQ, :, :], 0.0))
            old = smask[0:DSEQ, :, 0:P]
            new = smask[0:DSEQ, :, P:192].rearrange("t b (c u) -> t b c u", u=DSEQ)
            keep_where(old, [[0, NSEQ], [1, P]], -1, -1, ALU.is_ge, -BIG)
            link(keep_where(new, [[0, NSEQ], [0, NSEQ], [-1, DSEQ]], 0, 1, ALU.is_ge, -BIG))
            keep_where(new, [[1, NSEQ], [-1, NSEQ], [0, DSEQ]], 0, 0, ALU.is_equal, -BIG).then_inc(mask_made, 1)

            for t in range(NT, 3 * NT):
                rms(t)


_INS = ["x_prompt", "x_sample", "state_C", "state_n", "state_m", "cache_k", "cache_v", "norm_attn", "w_in", "b_gate",
        "mlstm_norm", "sinks", "w_out", "norm_mlp", "w_up", "w_down", "norm_final"]
_OUTS = [(1, SEQ, D), (NSEQ, DSEQ, D), (1, 1, MH, DK, DV), (1, 1, MH, DK), (1, 1, MH),
         (1, 1, WIN, NKV, HD), (1, 1, WIN, NKV, HD), (1, NSEQ, MH, DK, DV), (1, NSEQ, MH, DK), (1, NSEQ, MH),
         (1, NSEQ, WIN, NKV, HD), (1, NSEQ, WIN, NKV, HD)]


def kernel(**inputs):
    import numpy as _np
    import concourse.bacc as _bacc
    from concourse import mybir as _mybir
    from concourse.bass_utils import run_bass_kernel_spmd as _run

    nc = _bacc.Bacc("TRN2", target_bir_lowering=False, num_devices=1, dynamic_dma_scratch_size=1024)
    arrays, args = {}, []
    for name in _INS:
        a = _np.ascontiguousarray(inputs[name])
        arrays[f"in_{name}"] = a
        args.append(nc.dram_tensor(f"in_{name}", a.shape, _mybir.dt.from_np(a.dtype), kind="ExternalInput").ap())
    for i, shape in enumerate(_OUTS):
        args.append(nc.dram_tensor(f"out_{i}", shape, _mybir.dt.float32, kind="ExternalOutput").ap())
    layer_kernel(nc, *args)
    r = _run(nc, [arrays], core_ids=[0])
    return tuple(r.results[0][f"out_{i}"] for i in range(len(_OUTS)))
```

```python
from contextlib import ExitStack

import concourse.bass as bass
from concourse import mybir

F32 = mybir.dt.float32
F32R = mybir.dt.float32r
ALU = mybir.AluOpType
ACT = mybir.ActivationFunctionType

P = 128
D = 1024
SEQ = 1024
NSEQ = 8
DSEQ = 8
T = SEQ + NSEQ * DSEQ
NT = (T + P - 1) // P
KT = D // P
MH = 4
DK = 128
DV = 256
VA = DV + 1
HD = 64
NKV = 4
GRP = 4
WIN = 128
FF = 4096
EPS = 1e-6
BIG = 1e30
C_MQ, C_MK, C_MV, C_MO = 0, 512, 1024, 2048
C_GATE = 3072
C_AQ = 3080
C_AK = 4104
C_AV = 4360
C_GA = 4616
C_GB = 5640
WCOLS = 256
BLK = KT * (WCOLS + 8)
CHUNKS = [(0, 384), (384, 384), (768, 320)]
QK_SCALE = float(DK) ** -0.5
ATT_SCALE = float(HD) ** -0.5
NG = FF // WCOLS


def rows_of(i):
    return P if i < NT - 1 else T - P * (NT - 1)


def block_list():
    out = [("v", 0), ("v", 1), ("mk", 0), ("mq", 0), ("v", 2), ("v", 3), ("mk", 1), ("mq", 1), ("av",), ("ak",)]
    out += [(kind, 0, 0) for kind in ("mo", "ga")]
    out += [("aq", p, gg) for p in range(2) for gg in range(2)]
    out += [(kind, p, gg) for p, gg in ((0, 1), (1, 0), (1, 1)) for kind in ("mo", "ga")]
    out += [("gb", p, gg) for p in range(2) for gg in range(2)]
    out += [("out", cq) for cq in range(4)]
    return out


BLOCKS = block_list()
NPROJ = len(BLOCKS) - 4
NATURAL = ("v", "av", "out")


def n_units(b):
    return NT if BLOCKS[b][0] in NATURAL else 2 * len(CHUNKS)


FIRST_UNIT = [sum(n_units(x) for x in range(b)) for b in range(NPROJ + 1)]
PROJ_UNITS = FIRST_UNIT[NPROJ]
OUT_UNITS = 4 * NT
B_MLP = len(BLOCKS)
RING = 3
UP_UNITS = 2 * len(CHUNKS)
DN_UNITS = 2 * NT


def units_of(first, last):
    return [(b, u) for b in range(first, last + 1) for u in range(n_units(b))]


def spread(units, slots):
    n, out, at = sum(slots), [], 0
    for k in range(len(slots)):
        upto = -(-len(units) * sum(slots[:k + 1]) // n)
        out.append(units[at:upto])
        at = upto
    return out


FILL_ML = [spread(units_of(4, 7), [2, 1] * NT), spread(units_of(8, 11), [2, 1] * NT)]
FILL_ATT = spread(units_of(16, 21), [3] * 32 + [20] + [3] * 16)
GATES = {}
for _b in range(NPROJ):
    if BLOCKS[_b][0] in ("mo", "ga", "gb"):
        for _u in range(n_units(_b)):
            GATES[_b, _u] = len(GATES)


def layer_kernel(nc, x_prompt, x_sample, state_C, state_n, state_m, cache_k, cache_v, norm_attn, w_in, b_gate,
                 mlstm_norm, sinks, w_out, norm_mlp, w_up, w_down, norm_final,
                 y_prompt, y_sample, p_C, p_n, p_m, p_k, p_v, s_C, s_n, s_m, s_k, s_v):
    xs_flat = x_sample.rearrange("b t d -> (b t) d")
    ys_flat = y_sample.rearrange("b t d -> (b t) d")

    def x_rows(i):
        return x_prompt[0, i * P:(i + 1) * P, :] if i < NT - 1 else xs_flat

    def y_rows(i):
        return y_prompt[0, i * P:(i + 1) * P, :] if i < NT - 1 else ys_flat

    w_in_k = w_in[0].rearrange("(k p) c -> p k c", p=P)
    w_up_k = w_up[0].rearrange("(k p) c -> p k c", p=P)
    w_dn_k = w_down[0].rearrange("(k p) c -> p k c", p=P)
    gate_rows = nc.dram_tensor("gate_rows", (2, MH, T), F32, kind="Internal").ap()
    ends_dram = nc.dram_tensor("ends_dram", (MH, 16), F32, kind="Internal").ap()
    mask_dram = nc.dram_tensor("mask_dram", (DSEQ, NSEQ * 192), F32, kind="Internal").ap()

    ctx = ExitStack()
    with ctx:
        def scope_alloc(stack):
            def alloc(name, shape, dt=F32):
                return stack.enter_context(nc.sbuf_tensor(name, shape, dt))
            return alloc

        sb = scope_alloc(ctx)

        def sem(name):
            return ctx.enter_context(nc.semaphore(name))

        bank = [ctx.enter_context(nc.psum_tensor(f"bank{n}", [P, 512], F32)) for n in range(8)]

        ident = sb("ident", [P, P])
        causal = sb("causal", [P, P])
        causal8 = sb("causal8", [64, 64])
        seq_ind = sb("seq_ind", [64, NSEQ])
        gain_b = sb("gain_b", [P, D])
        with ExitStack() as s:
            raw = scope_alloc(s)("raw", [P, 2, BLK])
        w_lo = sb("w_lo", [P, 2, BLK], F32R)
        w_hi = sb("w_hi", [P, 2, BLK], F32R)
        xT_hi = sb("xT_hi", [P, KT, T], F32R)
        xT_lo = sb("xT_lo", [P, KT, T], F32R)
        stat = sb("stat", [P, 3, NT])
        rstd = sb("rstd", [P, 3, NT])
        neghalf = sb("neghalf", [P, 2])
        mnorm = sb("mnorm", [P, KT])
        sink_b = sb("sink_b", [P, 16])
        sink_s = sb("sink_s", [P, 1])
        sig = sb("sig", [P, 2, 384])

        with ExitStack() as s:
            a = scope_alloc(s)
            xin = a("xin", [P, 3, D])
            xn = a("xn", [P, 2, D])
            junk = a("junk", [P, D])
        s = ExitStack()
        with s:
            a = scope_alloc(s)
            hT = a("hT", [P, KT, T])
            vaug0 = a("vaug0", [P, NT, 2, VA])
            gnat = a("gnat", [P, NT, 8])
            nat = a("nat", [P, NT, 4, MH])
            sm_rows = a("sm_rows", [MH, NSEQ])
            bias_i = a("bias_i", [MH, 1])
            bias_f = a("bias_f", [MH, 1])
            ends = a("ends", [MH, 16])
            m_out = a("m_out", [MH, NSEQ + 1])
            dec = a("dec", [P, MH, 16])
            Cst = a("Cst", [P, 2, VA])
            small = a("small", [P, 2, 8])
            qz = a("qz", [P, 2, 576])
            with ExitStack() as s2:
                a2 = scope_alloc(s2)
                vaug1 = a2("vaug1", [P, NT, 2, VA])
                Cin = a2("Cin", [P, 2, 4, VA])
                bc = a2("bc", [P, 2, 4, P])
                hh_b = a2("hh_b", [P, 2, GRP, 2, HD])
                kwz = a2("kwz", [64, NSEQ, P])
                hjunk = a2("hjunk", [P, DV])
                wgt = a2("wgt", [P, 2, 2, P])
                qs = a2("qs", [P, 2, 2, P])
                kw = a2("kw", [P, 2, 2, P])
            a2 = a
            row_i = a2("row_i", [MH, T])
            row_f = a2("row_f", [MH, T])
            row_t = a2("row_t", [MH, T])
            row_b = a2("row_b", [MH, T])
            row_m = a2("row_m", [MH, T])
            row_x = a2("row_x", [MH, T])
            row_r = a2("row_r", [MH, T])
            q4 = a2("q4", [P, T])
        vaug = (vaug0, vaug1)
        with ExitStack() as s:
            a = scope_alloc(s)
            a("under_hT", [P, KT, T])
            akT = a("akT", [P, 2, T])
            avn = a("avn", [P, NT, NKV * HD])
            aqT = a("aqT", [P, KT, T])
            with ExitStack() as s2:
                a2 = scope_alloc(s2)
                amask = a2("amask", [P, 2 * P])
                prob = a2("prob", [P, 2, GRP, 2 * P])
                pT = a2("pT", [P, 2, GRP * P])
                ast = a2("ast", [P, 2, 6, GRP])
            with ExitStack() as s2:
                a2 = scope_alloc(s2)
                smask = a2("smask", [P, NSEQ, 192])
                kc = a2("kc", [P, 2, NKV * HD])
                vc = a2("vc", [P, 2, NKV * HD])
                kcT = a2("kcT", [P, 2, 2, P])
                sprob = a2("sprob", [P, 2, 192])
                spT = a2("spT", [P, 2, P])
                o2 = a2("o2", [P, P])
                qsmp = a2("qsmp", [P, 2, NSEQ, GRP, DSEQ])
                sst = a2("sst", [P, 2, 6])
                kout = a2("kout", [P, 2, NKV * HD])
        with ExitStack() as s:
            a = scope_alloc(s)
            x2 = a("x2", [P, NT, D])
            hid_hi = a("hid_hi", [P, 2, 2, T], F32R)
            hid_lo = a("hid_lo", [P, 2, 2, T], F32R)
            relu = a("relu", [P, 2, 384])
            sqr = a("sqr", [P, 2, 384])
            ybuf = a("ybuf", [P, 2, D])
            junk2 = a("junk2", [P, D])

        x_in = [sem(f"x_in{n}") for n in range(3)]
        raw_in = [sem(f"raw_in{n}") for n in range(2)]
        w_hi_done = sem("w_hi_done")
        w_lo_done = sem("w_lo_done")
        gain_in = sem("gain_in")
        const_in = sem("const_in")
        consts = sem("consts")
        norm_sq = sem("norm_sq")
        norm_rs = sem("norm_rs")
        norm_xn = sem("norm_xn")
        norm_tp = sem("norm_tp")
        norm_hi = sem("norm_hi")
        norm_lo = sem("norm_lo")
        gemm_a = sem("gemm_a")
        free_a = sem("free_a")
        gemm_v = sem("gemm_v")
        free_v = sem("free_v")
        act_chain = sem("act_chain")
        dve_chain = sem("dve_chain")
        pool_chain = sem("pool_chain")
        gate_tp = sem("gate_tp")
        gate_ev = sem("gate_ev")
        gate_ln = sem("gate_ln")
        gate_arg = sem("gate_arg")
        gate_exp = sem("gate_exp")
        gate_fin = sem("gate_fin")
        gate_q4 = sem("gate_q4")
        gate_nat = sem("gate_nat")
        rows_out = sem("rows_out")
        dec_in = sem("dec_in")
        bc_in = [sem(f"bc_in{n}") for n in range(2)]
        ones = sem("ones")
        ml_kt = sem("ml_kt")
        ml_st = sem("ml_st")
        ml_wa = sem("ml_wa")
        ml_we = sem("ml_we")
        ml_sw = sem("ml_sw")
        ml_qs = sem("ml_qs")
        ml_kw = sem("ml_kw")
        ml_n = sem("ml_n")
        ml_u = sem("ml_u")
        ml_ab = sem("ml_ab")
        ml_rc = sem("ml_rc")
        ml_h0 = sem("ml_h0")
        ml_h1 = sem("ml_h1")
        ml_ss = sem("ml_ss")
        ml_rs = sem("ml_rs")
        ml_hn = sem("ml_hn")
        ml_c = sem("ml_c")
        ml_t = sem("ml_t")
        ml_te = sem("ml_te")
        ml_kz = sem("ml_kz")
        ml_su = sem("ml_su")
        ml_sc = sem("ml_sc")
        ml_cl = sem("ml_cl")
        cin_in = [sem(f"cin_in{n}") for n in range(2)]
        cin_out = sem("cin_out")
        pc_out = sem("pc_out")
        at_s = sem("at_s")
        at_m = sem("at_m")
        at_e = sem("at_e")
        at_p = sem("at_p")
        at_t = sem("at_t")
        at_p0 = sem("at_p0")
        at_p1 = sem("at_p1")
        at_v = sem("at_v")
        at_o = sem("at_o")
        kc_in = [sem(f"kc_in{n}") for n in range(2)]
        mask_made = sem("mask_made")
        mask_io = sem("mask_io")
        sk_t = sem("sk_t")
        sk_e = sem("sk_e")
        ss_q = sem("ss_q")
        ss_s = sem("ss_s")
        ss_m = sem("ss_m")
        ss_e = sem("ss_e")
        ss_p = sem("ss_p")
        ss_t = sem("ss_t")
        ss_te = sem("ss_te")
        ss_v = sem("ss_v")
        ss_o2 = sem("ss_o2")
        ss_ot = sem("ss_ot")
        ss_o = sem("ss_o")
        ko_t = sem("ko_t")
        ko_e = sem("ko_e")
        sg_use = sem("sg_use")
        mg_hi = sem("mg_hi")
        mg_lo = sem("mg_lo")
        x2_in = [sem(f"x2_in{n}") for n in range(NT)]
        re_done = sem("re_done")
        hi_done = sem("hi_done")
        sq_done = sem("sq_done")
        lo_done = sem("lo_done")
        y_out = [sem(f"y_out{n}") for n in range(2)]
        y_rdy = sem("y_rdy")
        out_dma = sem("out_dma")

        def w_view(t, b, k):
            n = WCOLS + 8 if b == 0 else WCOLS
            return t[:, b % 2, k * n:(k + 1) * n]

        def w_stat(t, b, k, tile):
            return w_view(t, b, k)[:, tile * P:(tile + 1) * P]

        def block_cols(b):
            return BLK if b == 0 else KT * WCOLS

        def mq(p, hh, at):
            return hT[:, p * GRP + hh, at]

        def mk(p, hh, at):
            return hT[:, p * GRP + 2 + hh, at]

        def half_view(n, rows):
            return bank[n][:, :].rearrange("p (k t) -> p k t", t=P)[:, :, 0:rows]

        RAW_DMAS = [{"aq": 4, "mo": 4, "ga": 4, "gb": 4, "out": 4}.get(x[0], 1) for x in BLOCKS]
        RAW_DMAS[0] = 2
        RAW_AT = [16 * sum(RAW_DMAS[b % 2:b + 1:2]) for b in range(B_MLP)]
        RAW_ALL = RAW_AT[-2:]

        def by_group(v):
            return v.rearrange("t (g c) -> t g c", g=GRP)

        def cols(i):
            return slice(i * P, i * P + rows_of(i))

        def done_before(b):
            if b < NPROJ:
                return gemm_a, FIRST_UNIT[b + 1]
            return gemm_v, NT * (b - NPROJ + 1)

        S_PER = NT
        ML_BLOCKS = ((4, 7), (8, 11))
        AQ_BLOCKS = (12, 15)
        GB_BLOCKS = (22, 25)

        block = ctx.enter_context(nc.Block())

        @block.sync
        def _(sp):
            def load_block(b):
                kind = BLOCKS[b][0]
                if b >= 2:
                    sp.wait_ge(*done_before(b - 2))
                r = raw[:, b % 2, 0:KT * WCOLS].rearrange("p (k c) -> p k c", k=KT)
                if b == 0:
                    r = raw[:, b % 2, 0:BLK].rearrange("p (k c) -> p k c", k=KT)
                    sp.dma_start(r[:, :, 0:8], w_in_k[:, :, C_GATE:C_GATE + 8],
                                 allow_slow_non_contiguous=True).then_inc(raw_in[b % 2], 16)
                    sp.dma_start(r[:, :, 8:], w_in_k[:, :, C_MV:C_MV + DV]).then_inc(raw_in[b % 2], 16)
                elif kind in ("v", "mk", "mq", "av", "ak"):
                    c0 = {"v": C_MV, "mk": C_MK, "mq": C_MQ, "av": C_AV, "ak": C_AK}[kind]
                    c0 += WCOLS * (BLOCKS[b][1] if len(BLOCKS[b]) > 1 else 0)
                    sp.dma_start(r, w_in_k[:, :, c0:c0 + WCOLS]).then_inc(raw_in[b % 2], 16)
                elif kind == "out":
                    cq = BLOCKS[b][1]
                    src = w_out[0].rearrange("(p h g c) n -> h p c g n", p=2, h=2, g=GRP)
                    for h in range(2):
                        for p in range(2):
                            sp.dma_start(r[64 * h:64 * h + 64, GRP * p:GRP * p + GRP, :],
                                         src[h, p, :, :, cq * WCOLS:(cq + 1) * WCOLS]).then_inc(raw_in[b % 2], 16)
                else:
                    c0 = {"aq": C_AQ, "mo": C_MO, "ga": C_GA, "gb": C_GB}[kind]
                    _, p, gg = BLOCKS[b]
                    for h in range(2):
                        for g in range(2):
                            at = c0 + (2 * p + h) * 256 + (2 * gg + g) * HD
                            sp.dma_start(r[:, :, (2 * g + h) * HD:(2 * g + h + 1) * HD],
                                         w_in_k[:, :, at:at + HD]).then_inc(raw_in[b % 2], 16)

            def small(dst, src):
                sp.dma_start(dst, src, allow_slow_non_contiguous=True).then_inc(const_in, 16)

            def load_x(i):
                if i >= 3:
                    sp.wait_ge(norm_xn, i - 2)
                sp.dma_start(xin[0:rows_of(i), i % 3, :], x_rows(i)).then_inc(x_in[i % 3], 16)

            load_x(0)
            sp.dma_start(gain_b[:, :], norm_attn[0].partition_broadcast(P)).then_inc(gain_in, 16)
            load_x(1)
            load_block(0)
            load_x(2)
            small(bias_i[:, :], b_gate[0, 0:MH].unsqueeze(1))
            small(bias_f[:, :], b_gate[0, MH:2 * MH].unsqueeze(1))
            small(sm_rows[:, :], state_m[0].rearrange("b h -> h b"))
            small(sink_b[:, :], sinks[0].partition_broadcast(P))
            small(sink_s[:, :], sinks[0].unsqueeze(1).broadcast_to([16, DSEQ]).unsqueeze(2))
            mn = mlstm_norm[0].rearrange("(p h g c) -> h p c g", p=2, h=2, g=GRP)
            for h in range(2):
                for p in range(2):
                    small(mnorm[64 * h:64 * h + 64, GRP * p:GRP * p + GRP], mn[h, p])
            load_x(3)
            load_block(1)
            for i in range(4, NT):
                load_x(i)
            for b in range(NSEQ):
                sp.dma_start(s_k[0, b, 0:WIN - DSEQ], cache_k[0, b, DSEQ:WIN]).then_inc(out_dma, 16)
                sp.dma_start(s_v[0, b, 0:WIN - DSEQ], cache_v[0, b, DSEQ:WIN]).then_inc(out_dma, 16)
            sp.wait_ge(norm_xn, NT)
            sp.dma_start(gain_b[:, :], norm_mlp[0].partition_broadcast(P)).then_inc(gain_in, 16)

            def store_gate_rows():
                sp.wait_ge(gate_fin, 1)
                sp.dma_start(gate_rows[0], row_x[:, :]).then_inc(rows_out, 16)
                sp.dma_start(gate_rows[1], row_t[:, :]).then_inc(rows_out, 16)
                sp.dma_start(ends_dram, ends[:, :]).then_inc(rows_out, 16)
                sp.dma_start(p_m[0].rearrange("b h -> h b"), m_out[:, NSEQ:NSEQ + 1],
                             allow_slow_non_contiguous=True).then_inc(out_dma, 16)
                sp.dma_start(s_m[0].rearrange("b h -> h b"), m_out[:, 0:NSEQ],
                             allow_slow_non_contiguous=True).then_inc(out_dma, 16)
                sp.wait_ge(rows_out, 48)
                sp.dma_start(dec[:, :, :].rearrange("p h e -> p (h e)"),
                             ends_dram.rearrange("h e -> (h e)").unsqueeze(0).broadcast_to([P, MH * 16]))\
                    .then_inc(dec_in, 16)

            def load_bc(s):
                p, i = divmod(s, S_PER)
                if s >= 2:
                    sp.wait_ge(ml_wa, s - 1)
                    sp.wait_ge(ml_qs, s - 1)
                for q in range(2):
                    sp.dma_start(bc[:, s % 2, 2 * q:2 * q + 2, 0:rows_of(i)],
                                 gate_rows[q, 2 * p:2 * p + 2, cols(i)].unsqueeze(0)
                                 .broadcast_to([P, 2, rows_of(i)])).then_inc(bc_in[s % 2], 16)

            def load_cin(n):
                p, hh, half = n // 4, n // 2 % 2, n % 2
                h = 2 * p + hh
                if n >= 2:
                    sp.wait_ge(cin_out, 32 * 4 * p if n % 4 < 2 else 32 * (n - 1))
                sp.dma_start(Cin[:, half, :, 0:DV],
                             state_C[0, 4 * half:4 * half + 4, h].rearrange("b k v -> k b v")).then_inc(cin_in[half], 16)
                sp.dma_start(Cin[:, half, :, DV:VA],
                             state_n[0, 4 * half:4 * half + 4, h].rearrange("b k -> k b").unsqueeze(2),
                             allow_slow_non_contiguous=True).then_inc(cin_in[half], 16)

            def store_cin(n):
                p, hh, half = n // 4, n // 2 % 2, n % 2
                h = 2 * p + hh
                sp.wait_ge(ml_sc, 4 * (n + 1))
                sp.dma_start(s_C[0, 4 * half:4 * half + 4, h].rearrange("b k v -> k b v"),
                             Cin[:, half, :, 0:DV]).then_inc(cin_out, 16)
                sp.dma_start(s_n[0, 4 * half:4 * half + 4, h].rearrange("b k -> k b").unsqueeze(2),
                             Cin[:, half, :, DV:VA], allow_slow_non_contiguous=True).then_inc(cin_out, 16)

            def fill(units):
                for b, u in units:
                    if u == 0:
                        load_block(b + 1)

            def mlstm(p):
                s0 = p * S_PER
                if p == 0:
                    sp.wait_ge(gate_nat, 1)
                load_cin(4 * p)
                load_cin(4 * p + 1)
                load_bc(s0)
                load_bc(s0 + 1)
                for i in range(NT - 1):
                    fill(FILL_ML[p][2 * i])
                    fill(FILL_ML[p][2 * i + 1])
                    if i + 2 < NT:
                        load_bc(s0 + i + 2)
                sp.wait_ge(ml_c, (NT - 1) * (p + 1))
                sp.dma_start(p_C[0, 0, 2 * p:2 * p + 2].rearrange("h k v -> k h v"),
                             Cst[:, :, 0:DV]).then_inc(pc_out, 16)
                sp.dma_start(p_n[0, 0, 2 * p:2 * p + 2].rearrange("h k -> k h").unsqueeze(2),
                             Cst[:, :, DV:VA], allow_slow_non_contiguous=True).then_inc(pc_out, 16)
                for n in range(4 * p, 4 * p + 2):
                    store_cin(n)
                    load_cin(n + 2)
                fill(FILL_ML[p][2 * NT - 2])
                for n in range(4 * p + 2, 4 * p + 4):
                    store_cin(n)
                fill(FILL_ML[p][2 * NT - 1])

            def attention():
                for u in range(8 * NKV):
                    fill(FILL_ATT[u])
                sp.wait_ge(at_v, 8 * NKV)
                sp.wait_ge(at_o, 8 * NKV)
                sp.wait_ge(mask_made, 1)
                sp.dma_start(mask_dram, smask[0:DSEQ, :, :].rearrange("t b c -> t (b c)")).then_inc(mask_io, 16)
                sp.wait_ge(mask_io, 16)
                for n in range(16):
                    sp.dma_start(smask[n * DSEQ:(n + 1) * DSEQ, :, :].rearrange("t b c -> t (b c)"),
                                 mask_dram).then_inc(mask_io, 16)
                fill(FILL_ATT[32])
                for s in range(NSEQ):
                    if s >= 2:
                        sp.wait_ge(sk_t, s - 1)
                        sp.wait_ge(ss_v, s - 1)
                    sp.dma_start(kc[:, s % 2, :], cache_k[0, s].rearrange("w h d -> w (h d)")).then_inc(kc_in[s % 2], 16)
                    sp.dma_start(vc[:, s % 2, :], cache_v[0, s].rearrange("w h d -> w (h d)")).then_inc(kc_in[s % 2], 16)
                    if s >= 1:
                        fill(FILL_ATT[33 + 2 * (s - 1)])
                        fill(FILL_ATT[34 + 2 * (s - 1)])
                fill(FILL_ATT[47])
                fill(FILL_ATT[48])
                sp.wait_ge(ko_e, 2)
                sp.dma_start(p_k[0, 0].rearrange("t h d -> t (h d)"), kout[:, 0, :]).then_inc(out_dma, 16)
                sp.dma_start(p_v[0, 0].rearrange("t h d -> t (h d)"), avn[:, NT - 2, :]).then_inc(out_dma, 16)
                for s in range(NSEQ):
                    at = slice(s * DSEQ, (s + 1) * DSEQ)
                    sp.dma_start(s_k[0, s, WIN - DSEQ:].rearrange("t h d -> t (h d)"),
                                 kout[at, 1, :]).then_inc(out_dma, 16)
                    sp.dma_start(s_v[0, s, WIN - DSEQ:].rearrange("t h d -> t (h d)"),
                                 avn[at, NT - 1, :]).then_inc(out_dma, 16)

            fill(units_of(1, 2))
            store_gate_rows()
            fill(units_of(3, 3))
            mlstm(0)
            mlstm(1)
            fill(units_of(*AQ_BLOCKS))
            attention()
            fill(units_of(*GB_BLOCKS))
            load_block(NPROJ + 1)
            sp.wait_ge(mg_lo, NT)
            for i in range(NT):
                sp.dma_start(x2[0:rows_of(i), i, :], x_rows(i)).then_inc(x2_in[i], 16)
            load_block(NPROJ + 2)
            load_block(NPROJ + 3)

            def up_dma(g, slot):
                sp.dma_start(raw[:, slot, 0:KT * WCOLS].rearrange("p (k c) -> p k c", k=KT),
                             w_up_k[:, :, bass.ds(g * WCOLS, WCOLS)]).then_inc(raw_in[slot], 16)

            def dn_dma(g):
                sp.dma_start(raw[:, 0, 0:2 * D].rearrange("p (k c) -> p k c", k=2),
                             w_dn_k[:, bass.ds(2 * g, 2), :]).then_inc(raw_in[0], 16)

            sp.wait_ge(gemm_v, 3 * NT)
            up_dma(0, 0)
            sp.wait_ge(gemm_v, OUT_UNITS)
            up_dma(1, 1)
            sp.wait_ge(gemm_a, PROJ_UNITS + UP_UNITS)
            dn_dma(0)
            with sp.Fori(2, NG) as g:
                sp.wait_ge(gemm_a, g * UP_UNITS + PROJ_UNITS)
                up_dma(g, 1)
                sp.wait_ge(gemm_v, g * DN_UNITS + (OUT_UNITS - DN_UNITS))
                dn_dma(g - 1)
            sp.wait_ge(norm_xn, 2 * NT)
            sp.dma_start(gain_b[:, :], norm_final.partition_broadcast(P)).then_inc(gain_in, 16)
            sp.wait_ge(gemm_a, PROJ_UNITS + UP_UNITS * NG)
            sp.dma_start(raw[:, 1, 0:2 * D].rearrange("p (k c) -> p k c", k=2),
                         w_dn_k[:, 2 * (NG - 1):2 * NG, :]).then_inc(raw_in[1], 16)
            for i in range(NT):
                sp.wait_ge(y_rdy, i + 1)
                sp.dma_start(y_rows(i), ybuf[0:rows_of(i), i % 2, :]).then_inc(y_out[i % 2], 16)
            sp.wait_ge(pc_out, 64)
            sp.wait_ge(cin_out, 32 * 8)
            sp.wait_ge(out_dma, 16 * (2 * NSEQ + 2 + 2 + 2 * NSEQ))
            sp.wait_ge(y_out[0], 16 * ((NT + 1) // 2))
            sp.wait_ge(y_out[1], 16 * (NT // 2))

        @block.tensor
        def _(pe):
            def tr(out, in_, rows):
                return nc.tensor.transpose(out, in_, ident[0:rows, 0:rows])

            def norm_transposes(t, src, hold=None):
                i = t % NT
                rows = rows_of(i)
                pe.wait_ge(norm_xn, t + 1)
                for h in range(2):
                    n = 2 * t + h
                    if n >= 4:
                        pe.wait_ge(norm_lo, n - 3)
                    for k in range(4):
                        last = tr(bank[4 + n % 4][:, k * P:k * P + rows],
                                  src[0:rows, i % 2, (4 * h + k) * P:(4 * h + k + 1) * P], rows)
                    last.then_inc(norm_tp, 1)

            PASSES = ((w_hi, xT_hi), (w_hi, xT_lo), (w_lo, xT_hi))

            def proj_unit(b, u):
                n = FIRST_UNIT[b] + u
                if n >= RING:
                    pe.wait_ge(free_a, n - RING + 1)
                step = 0
                for k in range(KT):
                    for w, x in PASSES:
                        if BLOCKS[b][0] in NATURAL:
                            rhs = w_view(w, b, k)
                            out = bank[n % RING][0:rows_of(u), 0:WCOLS + 8 if b == 0 else WCOLS]
                            lhsT = x[:, k, cols(u)]
                        else:
                            tile, (c0, cn) = u // 3, CHUNKS[u % 3]
                            lhsT = w_stat(w, b, k, tile)
                            rhs = x[:, k, c0:c0 + cn]
                            out = bank[n % RING][:, 0:cn]
                        last = nc.tensor.matmul(out, lhsT, rhs, start=(step == 0), stop=(step == 3 * KT - 1))
                        step += 1
                last.then_inc(gemm_a, 1)

            def gate_transposes():
                pe.wait_ge(free_a, NT)
                def part(b, at, tiles, c):
                    for x, i in enumerate(tiles):
                        last = tr(bank[b][0:MH, at + x * P:at + x * P + rows_of(i)],
                                  gnat[0:rows_of(i), i, c:c + MH], rows_of(i))
                    return last
                pe.wait_ge(norm_lo, 2 * NT)
                part(4, 0, range(0, 4), 0).then_inc(gate_tp, 1)
                part(5, 0, range(4, 8), 0).then_inc(gate_tp, 1)
                part(6, 0, [8], 0)
                part(6, 64, [8], MH).then_inc(gate_tp, 1)
                part(7, 0, range(0, 4), MH).then_inc(gate_tp, 1)
                pe.wait_ge(gate_ev, 1)
                part(4, 0, range(4, 8), MH).then_inc(gate_tp, 1)

            def q4_transposes():
                pe.wait_ge(gate_exp, 3)
                pe.wait_ge(gate_ev, 6)
                for b, tiles in ((4, range(0, 4)), (5, range(4, 8)), (6, [8])):
                    for x, i in enumerate(tiles):
                        last = tr(bank[b][0:rows_of(i), x * P:x * P + P], q4[:, cols(i)], P)
                    last.then_inc(gate_q4, 1)

            def ml_scores(s):
                p, i = divmod(s, S_PER)
                n = rows_of(i)
                if i:
                    pe.wait_ge(ml_c, (NT - 1) * p + i)
                elif p:
                    pe.wait_ge(ml_sc, 2 * NSEQ)
                for hh in range(2):
                    last = tr(bank[4][0:n, hh * P:(hh + 1) * P], mk(p, hh, cols(i)), P)
                last.then_inc(ml_kt, 1)
                for hh in range(2):
                    last = nc.tensor.matmul(bank[5][0:n, hh * P:hh * P + n], mk(p, hh, cols(i)), mq(p, hh, cols(i)),
                                            start=True, stop=True)
                last.then_inc(ml_st, 1)

            def ml_step(s):
                p, i = divmod(s, S_PER)
                n = rows_of(i)
                pe.wait_ge(ml_sw, s + 1)
                pe.wait_ge(ml_qs, s + 1)
                if s >= 1:
                    pe.wait_ge(ml_h0, s)
                    pe.wait_ge(ml_h1, s)
                c = (NT - 1) * p + i
                if c:
                    pe.wait_ge(ml_c, c)
                for hh in range(2):
                    last = nc.tensor.matmul(bank[6 + hh][0:n, 0:VA], wgt[0:n, s % 2, hh, 0:n],
                                            vaug[p][0:n, i, hh, :], start=True, stop=(i == 0))
                    if i > 0:
                        last = nc.tensor.matmul(bank[6 + hh][0:n, 0:VA], qs[:, s % 2, hh, 0:n], Cst[:, hh, :],
                                                start=False, stop=True)
                last.then_inc(ml_n, 1)
                pe.wait_ge(ml_kw, s + 1)
                for hh in range(2):
                    last = nc.tensor.matmul(bank[4 + hh][:, 0:VA], kw[0:n, s % 2, hh, :], vaug[p][0:n, i, hh, :],
                                            start=True, stop=True)
                last.then_inc(ml_u, 1)

            def ml_sampled(p, hh):
                s, i = p * S_PER + NT - 1, NT - 1
                n = rows_of(i)
                if hh == 0:
                    pe.wait_ge(ml_sw, s + 1)
                    pe.wait_ge(ml_qs, s + 1)
                    pe.wait_ge(ml_h0, s)
                    pe.wait_ge(ml_h1, s)
                nc.tensor.matmul(bank[6 + hh][0:n, 0:VA], wgt[0:n, s % 2, hh, 0:n], vaug[p][0:n, i, hh, :],
                                 start=True, stop=False)
                for half in range(2):
                    pe.wait_ge(cin_in[half], 32 * (2 * p + hh + 1))
                    for b in range(4 * half, 4 * half + 4):
                        last = nc.tensor.matmul(bank[6 + hh][0:n, 0:VA], qz[:, hh, 64 * b:64 * b + 64],
                                                Cin[:, half, b % 4, :], start=False, stop=(b == NSEQ - 1))
                if hh == 1:
                    last.then_inc(ml_n, 1)
                pe.wait_ge(ml_kz, 2 * p + hh + 1)
                for b in range(NSEQ):
                    c = (2 * p + hh) * NSEQ + b
                    if b >= 2:
                        pe.wait_ge(ml_sc, c - 1)
                    elif hh:
                        pe.wait_ge(ml_sc, c)
                    elif b == 0:
                        pe.wait_ge(ml_kw, s + 1)
                    nc.tensor.matmul(bank[4 + b % 2][:, 0:VA], kwz[0:n, b, :], vaug[p][0:n, i, hh, :],
                                     start=True, stop=True).then_inc(ml_su, 1)

            def ml_transposes(s):
                i = s % S_PER
                n = rows_of(i)
                pe.wait_ge(ml_hn, s + 1)
                if s >= 1:
                    pe.wait_ge(ml_te, s)
                for g in range(GRP):
                    last = tr(bank[3][:, g * P:g * P + n],
                              hh_b[0:n, s % 2, g, :, :].rearrange("t h c -> t (h c)"), n)
                last.then_inc(ml_t, 1)

            def mlstm(p):
                pe.wait_ge(free_a, FIRST_UNIT[4 * p + 4])
                pe.wait_ge(gate_nat, 1)
                if p:
                    pe.wait_ge(ones, 1)
                s0 = p * S_PER
                ml_scores(s0)
                for i in range(NT):
                    s = s0 + i
                    if i < NT - 1:
                        ml_step(s)
                        fill(FILL_ML[p][2 * i])
                    else:
                        ml_sampled(p, 0)
                        fill(FILL_ML[p][2 * i])
                        ml_sampled(p, 1)
                    if i:
                        ml_transposes(s - 1)
                    if i < NT - 1:
                        ml_scores(s + 1)
                    fill(FILL_ML[p][2 * i + 1])
                ml_transposes(s0 + NT - 1)

            def at_scores(u):
                i, kv = divmod(u, NKV)
                p, half = divmod(kv, 2)
                lo = 0 if i else P
                if u >= 1:
                    pe.wait_ge(at_m, u)
                at = slice(64 * half, 64 * half + 64)
                for g in range(GRP):
                    out = bank[3 + g // 2][:, (g % 2) * 256 + lo:(g % 2) * 256 + 256]
                    last = nc.tensor.matmul(out, aqT[at, p * GRP + g, cols(i)],
                                            akT[at, p, (i - 1) * P + lo:(i + 1) * P], start=True, stop=True)
                last.then_inc(at_s, 1)

            def at_transposes(u):
                i, kv = divmod(u, NKV)
                pe.wait_ge(at_p, u + 1)
                if u > NKV:
                    pe.wait_ge(at_p0, u - NKV)
                if u >= 1:
                    pe.wait_ge(at_p1, u)
                for kb in range(2 if i else 1):
                    kb = kb if i else 1
                    for g in range(GRP):
                        last = tr(bank[5 + kb][:, g * P:(g + 1) * P], prob[:, u % 2, g, kb * P:(kb + 1) * P], P)
                last.then_inc(at_t, 1)

            def at_values(u):
                i, kv = divmod(u, NKV)
                half = kv % 2
                if u >= 1:
                    pe.wait_ge(at_o, u)
                out = bank[7][64 * half:64 * half + 64, :]
                for kb in range(2):
                    if kb:
                        pe.wait_ge(at_p1, u + 1)
                    elif i:
                        pe.wait_ge(at_p0, u + 1 - NKV)
                    if kb or i:
                        last = nc.tensor.matmul(out, avn[:, i - 1 + kb, kv * HD:(kv + 1) * HD], pT[:, kb, :],
                                                start=(kb == 0 or i == 0), stop=(kb == 1))
                last.then_inc(at_v, 1)

            def ss_keys(b):
                pe.wait_ge(kc_in[b % 2], 32 * (b // 2 + 1))
                if b >= 1:
                    pe.wait_ge(sk_e, b)
                for p in range(2):
                    last = tr(bank[3][:, p * P:(p + 1) * P], kc[:, b % 2, p * P:(p + 1) * P], P)
                last.then_inc(sk_t, 1)

            def ss_scores(b):
                pe.wait_ge(sk_e, b + 1)
                pe.wait_ge(ss_q, 1)
                if b >= 1:
                    pe.wait_ge(ss_m, b)
                for kv in range(NKV):
                    p, half = divmod(kv, 2)
                    at = slice(64 * half, 64 * half + 64)
                    q = qsmp[at, p, b, :, :].rearrange("c g t -> c (g t)")
                    out = bank[4][32 * kv:32 * kv + 32, :]
                    nc.tensor.matmul(out[:, 0:P], q, kcT[at, b % 2, p, :], start=True, stop=True)
                    last = nc.tensor.matmul(out[:, P:192], q, akT[at, p, SEQ:T], start=True, stop=True)
                last.then_inc(ss_s, 1)

            def ss_transposes(b):
                pe.wait_ge(ss_p, b + 1)
                if b >= 1:
                    pe.wait_ge(ss_te, b)
                tr(bank[5][:, 0:P], sprob[:, b % 2, 0:P], P)
                tr(bank[5][0:64, P:2 * P], sprob[:, b % 2, P:192], P).then_inc(ss_t, 1)

            def ss_values(b):
                pe.wait_ge(ss_te, b + 1)
                if b >= 1:
                    pe.wait_ge(ss_o2, b)
                nc.tensor.matmul(bank[6][:, 0:256], spT[:, 0, :], vc[:, b % 2, :], start=True, stop=False)
                nc.tensor.matmul(bank[6][:, 0:256], spT[0:64, 1, :], avn[0:64, NT - 1, :], start=False,
                                 stop=True).then_inc(ss_v, 1)

            def ss_outputs(b):
                pe.wait_ge(ss_o2, b + 1)
                if b >= 1:
                    pe.wait_ge(ss_o, b)
                tr(bank[7][:, 0:P], o2[:, :], P).then_inc(ss_ot, 1)

            def attention():
                pe.wait_ge(free_a, FIRST_UNIT[AQ_BLOCKS[1] + 1])
                pe.wait_ge(ml_te, 2 * S_PER)
                pe.wait_ge(ml_sc, 4 * NSEQ)
                n = 8 * NKV
                at_scores(0)
                for u in range(n):
                    if u + 1 < n:
                        at_scores(u + 1)
                    at_transposes(u)
                    fill(FILL_ATT[u])
                    at_values(u)
                for x, i in enumerate((NT - 2, NT - 1)):
                    for p in range(2):
                        last = tr(bank[5 + x][0:rows_of(i), p * P:(p + 1) * P], akT[:, p, cols(i)], P)
                    last.then_inc(ko_t, 1)
                fill(FILL_ATT[n])
                pe.wait_ge(at_o, n)
                pe.wait_ge(ko_e, 2)
                ss_keys(0)
                ss_scores(0)
                for b in range(NSEQ):
                    if b + 1 < NSEQ:
                        ss_keys(b + 1)
                    if b >= 1:
                        ss_outputs(b - 1)
                    ss_transposes(b)
                    fill(FILL_ATT[n + 1 + 2 * b])
                    if b + 1 < NSEQ:
                        ss_scores(b + 1)
                    ss_values(b)
                    fill(FILL_ATT[n + 2 + 2 * b])
                ss_outputs(NSEQ - 1)

            def fill(units):
                for b, u in units:
                    if u == 0:
                        pe.wait_ge(w_lo_done, b + 1)
                    proj_unit(b, u)

            pe.wait_ge(consts, 1)
            norm_transposes(0, xn)
            norm_transposes(1, xn)
            pe.wait_ge(w_lo_done, 1)
            for u in range(NT):
                if u + 2 < NT:
                    norm_transposes(u + 2, xn)
                pe.wait_ge(norm_lo, 2 * (u + 1))
                proj_unit(0, u)
            gate_transposes()
            fill(units_of(1, 2))
            q4_transposes()
            fill(units_of(3, 3))
            mlstm(0)
            mlstm(1)
            fill(units_of(*AQ_BLOCKS))
            attention()
            fill(units_of(*GB_BLOCKS))

            for cq in range(4):
                b = NPROJ + cq
                pe.wait_ge(w_lo_done, b + 1)
                for i in range(NT):
                    m = NT * cq + i
                    if cq == 0:
                        pe.wait_ge(mg_lo, i + 1)
                    if m >= 4:
                        pe.wait_ge(free_v, m - 3)
                    step = 0
                    for k in range(KT):
                        for w, x in PASSES:
                            last = nc.tensor.matmul(bank[m % 4][0:rows_of(i), 0:WCOLS], x[:, k, cols(i)],
                                                    w_view(w, b, k), start=(step == 0), stop=(step == 3 * KT - 1))
                            step += 1
                    last.then_inc(gemm_v, 1)
                    if cq == 3 and i >= 2:
                        norm_transposes(NT + i - 2, ybuf)
            norm_transposes(2 * NT - 2, ybuf)
            norm_transposes(2 * NT - 1, ybuf)

            def up(g, wait_b, slot, hslot):
                pe.wait_ge(w_lo_done, wait_b)
                for u in range(UP_UNITS):
                    tile, (c0, cn) = u // 3, CHUNKS[u % 3]
                    n = hslot * UP_UNITS + u
                    pe.wait_ge(free_a, g * UP_UNITS + (PROJ_UNITS + u - 3))
                    step = 0
                    for k in range(KT):
                        for w, x in PASSES:
                            last = nc.tensor.matmul(
                                bank[n % 4][:, 0:cn], w[:, slot, k * WCOLS + tile * P:k * WCOLS + (tile + 1) * P],
                                x[:, k, c0:c0 + cn], start=(step == 0), stop=(step == 3 * KT - 1))
                            step += 1
                    last.then_inc(gemm_a, 1)

            def down(g, wait_b, slot, hslot):
                pe.wait_ge(w_lo_done, wait_b)
                pe.wait_ge(lo_done, g * UP_UNITS + UP_UNITS)
                for i in range(NT):
                    for half in range(2):
                        d = hslot * DN_UNITS + 2 * i + half
                        pe.wait_ge(free_v, g * DN_UNITS + (OUT_UNITS + 2 * i + half - 3))
                        step = 0
                        for k in range(2):
                            for w, x in ((w_hi, hid_hi), (w_hi, hid_lo), (w_lo, hid_hi)):
                                last = nc.tensor.matmul(
                                    bank[4 + d % 4][0:rows_of(i), :], x[:, hslot, k, cols(i)],
                                    w[:, slot, k * D + half * 512:k * D + half * 512 + 512],
                                    start=(step == 0), stop=(step == 5))
                                step += 1
                        last.then_inc(gemm_v, 1)

            pe.wait_ge(norm_lo, 4 * NT)
            pe.wait_ge(free_v, OUT_UNITS)
            up(0, B_MLP + 1, 0, 0)
            with pe.Fori(0, NG // 2 - 1) as it:
                for x in range(2):
                    up(it * 2 + (1 + x), it * 4 + (B_MLP + 2 + 2 * x), 1, (1 + x) % 2)
                    down(it * 2 + x, it * 4 + (B_MLP + 3 + 2 * x), 0, x)
            up(NG - 1, B_MLP + 2 * NG - 2, 1, 1)
            down(NG - 2, B_MLP + 2 * NG - 1, 0, 0)
            down(NG - 1, B_MLP + 2 * NG, 1, 1)

        @block.scalar
        def _(act):
            chain = [0]

            def link(ins):
                chain[0] += 1
                ins.then_inc(act_chain, 1)
                act.wait_ge(act_chain, chain[0])

            def split(b):
                act.wait_ge(raw_in[b % 2], RAW_AT[b])
                n = block_cols(b)
                nc.scalar.activation(w_hi[:, b % 2, 0:n], raw[:, b % 2, 0:n], ACT.Copy).then_inc(w_hi_done, 1)

            def square(t, src, to):
                rows = rows_of(t % NT)
                if t:
                    act.wait_ge(norm_sq, t)
                ins = nc.scalar.activation(to[0:rows, :], src, ACT.Square,
                                           accum_out=stat[0:rows, t // NT, t % NT:t % NT + 1])
                ins.then_inc(norm_sq, 1)

            def round_x(t):
                i = t % NT
                for h in range(2):
                    n = 2 * t + h
                    act.wait_ge(norm_tp, n + 1)
                    if t >= NT and h == 0:
                        act.wait_ge(gemm_v, 3 * NT + i + 1)
                    nc.scalar.activation(xT_hi[:, 4 * h:4 * h + 4, cols(i)], half_view(4 + n % 4, rows_of(i)),
                                         ACT.Copy).then_inc(norm_hi, 1)

            def read_unit(b, u):
                kind = BLOCKS[b][0]
                n = FIRST_UNIT[b] + u
                src = bank[n % RING]
                act.wait_ge(gemm_a, n + 1)
                if kind == "v":
                    r = rows_of(u)
                    off = 8 if b == 0 else 0
                    if b == 0:
                        nc.scalar.activation(gnat[0:r, u, :], src[0:r, 0:8], ACT.Copy)
                    if b == 4 and u == 0:
                        act.wait_ge(gate_nat, 1)
                        act.wait_ge(rows_out, 48)
                    dst = vaug[BLOCKS[b][1] // 2][0:r, u, BLOCKS[b][1] % 2, 0:DV]
                    nc.scalar.activation(dst, src[0:r, off:off + DV], ACT.Copy).then_inc(free_a, 1)
                elif kind == "av":
                    r = rows_of(u)
                    if u == 0:
                        act.wait_ge(ml_su, 2 * NSEQ)
                    nc.scalar.activation(avn[0:r, u, :], src[0:r, 0:WCOLS], ACT.Copy).then_inc(free_a, 1)
                elif kind in ("mk", "mq", "ak", "aq"):
                    tile, (c0, cn) = u // 3, CHUNKS[u % 3]
                    if kind == "aq":
                        if b == AQ_BLOCKS[0] and u == 0:
                            act.wait_ge(cin_out, 32 * 8)
                            act.wait_ge(pc_out, 64)
                            act.wait_ge(ml_t, 2 * S_PER)
                        j = BLOCKS[b][1] * GRP + 2 * BLOCKS[b][2] + tile
                        dst = aqT[:, j, c0:c0 + cn]
                    else:
                        at = slice(c0, c0 + cn)
                        dst = akT[:, tile, at] if kind == "ak" else (mk if kind == "mk" else mq)(BLOCKS[b][1], tile, at)
                    nc.scalar.activation(dst, src[:, 0:cn], ACT.Copy,
                                         scale=QK_SCALE if kind == "mq" else 1.0).then_inc(free_a, 1)
                else:
                    c0, cn = CHUNKS[u % 3]
                    m = GATES[b, u]
                    if m >= 2:
                        act.wait_ge(sg_use, m - 1)
                    nc.scalar.activation(sig[:, m % 2, 0:cn], src[:, 0:cn], ACT.Sigmoid).then_inc(free_a, 1)

            def gate_rows_act():
                act.wait_ge(const_in, 16 * 9)
                def row(dst, at, n, b, c, bias, wait):
                    act.wait_ge(gate_tp, wait)
                    return nc.scalar.activation(dst[:, at:at + n], bank[b][0:MH, c:c + n], ACT.Identity,
                                                bias=bias[:, :])
                row(row_i, 0, 512, 4, 0, bias_i, 1).then_inc(gate_ev, 1)
                row(row_i, 512, 512, 5, 0, bias_i, 2).then_inc(gate_ev, 1)
                row(row_i, 1024, 64, 6, 0, bias_i, 3).then_inc(gate_ev, 1)
                row(row_f, 1024, 64, 6, 64, bias_f, 3).then_inc(gate_ev, 1)
                row(row_f, 0, 512, 7, 0, bias_f, 4).then_inc(gate_ev, 1)
                row(row_f, 512, 512, 4, 0, bias_f, 5).then_inc(gate_ev, 1)
                act.wait_ge(gate_ev, 6)
                link(nc.scalar.activation(row_t[:, :], row_f[:, :], ACT.Abs))
                link(nc.scalar.activation(row_t[:, :], row_t[:, :], ACT.Exp, scale=-1.0))
                nc.scalar.activation(row_t[:, :], row_t[:, :], ACT.Ln, bias=1.0).then_inc(gate_ln, 1)

            def gate_exps():
                act.wait_ge(gate_arg, 1)
                nc.scalar.activation(row_t[:, :], row_t[:, :], ACT.Exp).then_inc(gate_exp, 1)
                nc.scalar.activation(q4[64:64 + MH, :], row_m[:, :], ACT.Exp, scale=-1.0).then_inc(gate_exp, 1)
                nc.scalar.activation(q4[96:96 + MH, :], row_i[:, :], ACT.Exp).then_inc(gate_exp, 1)

            def ml_first(s):
                p, i = divmod(s, S_PER)
                n = rows_of(i)
                if s == 0:
                    act.wait_ge(gate_nat, 1)
                act.wait_ge(ml_kt, s + 1)
                if s == NT + 1:
                    act.wait_ge(ml_kz, 2)
                elif s >= 2:
                    act.wait_ge(ml_u, s - 1 - s // NT if s != NT else NT - 1)
                for hh in range(2):
                    ins = nc.scalar.activation(kw[0:n, s % 2, hh, :], bank[4][0:n, hh * P:(hh + 1) * P], ACT.Copy,
                                               scale=nat[0:n, i, 3, 2 * p + hh:2 * p + hh + 1])
                ins.then_inc(ml_kw, 1)
                act.wait_ge(ml_wa, s + 1)
                nc.scalar.activation(wgt[0:n, s % 2, :, 0:n], wgt[0:n, s % 2, :, 0:n], ACT.Exp).then_inc(ml_we, 1)

            def ml_second(s):
                p, i = divmod(s, S_PER)
                n = rows_of(i)
                act.wait_ge(ml_n, s + 1)
                for hh in range(2):
                    ins = nc.scalar.activation(small[0:n, s % 2, hh:hh + 1], bank[6 + hh][0:n, DV:VA], ACT.Abs)
                ins.then_inc(ml_ab, 1)
                act.wait_ge(ml_rc, s + 1)
                if s >= 2:
                    act.wait_ge(ml_t, s - 1)
                nc.scalar.activation(hh_b[0:n, s % 2, :, 0, :], by_group(bank[6][0:n, 0:DV]), ACT.Copy,
                                     scale=small[0:n, s % 2, 2:3]).then_inc(ml_h0, 1)
                for hh in range(2):
                    act.wait_ge((ml_h0, ml_h1)[hh], s + 1)
                    if s or hh:
                        act.wait_ge(ml_ss, 2 * s + hh)
                    ins = nc.scalar.activation(by_group(hjunk[0:n, :]), hh_b[0:n, s % 2, :, hh, :], ACT.Square,
                                               accum_out=small[0:n, s % 2, 4 + hh:5 + hh])
                    ins.then_inc(ml_ss, 1)

            def ml_third(s):
                p, i = divmod(s, S_PER)
                n = rows_of(i)
                act.wait_ge(ml_t, s + 1)
                nc.scalar.activation(hT[:, p * GRP:(p + 1) * GRP, cols(i)], half_view(3, n), ACT.Copy)\
                    .then_inc(ml_te, 1)

            def fill(units):
                for b, u in units:
                    read_unit(b, u)
                    if u == 2:
                        split(b + 1)

            def mlstm_act(p):
                s0 = p * S_PER
                ml_first(s0)
                for i in range(NT):
                    s = s0 + i
                    if i < NT - 1:
                        ml_second(s)
                        fill(FILL_ML[p][2 * i])
                    else:
                        fill(FILL_ML[p][2 * i])
                        ml_second(s)
                    if i:
                        ml_third(s - 1)
                    if i < NT - 1:
                        ml_first(s + 1)
                    fill(FILL_ML[p][2 * i + 1])
                ml_third(s0 + NT - 1)

            def at_exps(u):
                i = u // NKV
                lo = 0 if i else P
                act.wait_ge(at_m, u + 1)
                nc.scalar.activation(ast[:, u % 2, 3, :], ast[:, u % 2, 3, :], ACT.Exp)
                for g in range(GRP):
                    v = prob[:, u % 2, g, lo:]
                    ins = nc.scalar.activation(v, v, ACT.Exp, bias=ast[:, u % 2, 2, g:g + 1], scale=ATT_SCALE,
                                               accum_out=ast[:, u % 2, 4, g:g + 1])
                ins.then_inc(at_e, 1)

            def at_prev(u):
                if u < NKV:
                    return
                act.wait_ge(at_t, u + 1)
                act.wait_ge(at_v, u)
                nc.scalar.activation(pT[:, 0, :], bank[5][:, :], ACT.Copy).then_inc(at_p0, 1)

            def at_out(u):
                i, kv = divmod(u, NKV)
                p, half = divmod(kv, 2)
                at = slice(64 * half, 64 * half + 64)
                act.wait_ge(at_v, u + 1)
                nc.scalar.activation(aqT[at, p * GRP:(p + 1) * GRP, cols(i)],
                                     bank[7][at, :].rearrange("c (g t) -> c g t", g=GRP),
                                     ACT.Copy).then_inc(at_o, 1)

            def ss_keys(b):
                act.wait_ge(sk_t, b + 1)
                if b >= 2:
                    act.wait_ge(ss_s, b - 1)
                nc.scalar.activation(kcT[:, b % 2, :, :], bank[3][:, 0:256].rearrange("c (p w) -> c p w", p=2),
                                     ACT.Copy).then_inc(sk_e, 1)

            def ss_exps(b):
                act.wait_ge(ss_m, b + 1)
                nc.scalar.activation(sst[:, b % 2, 3:4], sst[:, b % 2, 3:4], ACT.Exp)
                nc.scalar.activation(sprob[:, b % 2, :], sprob[:, b % 2, :], ACT.Exp, bias=sst[:, b % 2, 2:3],
                                     scale=ATT_SCALE, accum_out=sst[:, b % 2, 4:5]).then_inc(ss_e, 1)

            def ss_pT(b):
                act.wait_ge(ss_t, b + 1)
                if b >= 1:
                    act.wait_ge(ss_v, b)
                nc.scalar.activation(spT[:, 0, :], bank[5][:, 0:P], ACT.Copy)
                nc.scalar.activation(spT[0:64, 1, :], bank[5][0:64, P:2 * P], ACT.Copy).then_inc(ss_te, 1)

            def ss_out(b):
                act.wait_ge(ss_ot, b + 1)
                for half in range(2):
                    at = slice(64 * half, 64 * half + 64)
                    src = bank[7][at, 0:P].rearrange("c (p h r) -> c p h r", p=2, h=2)[:, :, half, :]
                    dst = aqT[at, :, SEQ + b * DSEQ:SEQ + (b + 1) * DSEQ]
                    for p in range(2):
                        ins = nc.scalar.activation(dst[:, p * GRP:(p + 1) * GRP, :],
                                                   src[:, p, :].rearrange("c (g t) -> c g t", g=GRP), ACT.Copy)
                ins.then_inc(ss_o, 1)

            def attention_act():
                n = 8 * NKV
                at_exps(0)
                for u in range(n):
                    at_prev(u)
                    if u + 1 < n:
                        at_exps(u + 1)
                    fill(FILL_ATT[u])
                    at_out(u)
                act.wait_ge(ko_t, 2)
                nc.scalar.activation(kout[:, 0, :], bank[5][:, 0:256], ACT.Copy).then_inc(ko_e, 1)
                nc.scalar.activation(kout[0:64, 1, :], bank[6][0:64, 0:256], ACT.Copy).then_inc(ko_e, 1)
                fill(FILL_ATT[n])
                ss_keys(0)
                ss_exps(0)
                for b in range(NSEQ):
                    if b + 1 < NSEQ:
                        ss_keys(b + 1)
                    if b >= 1:
                        ss_out(b - 1)
                    ss_pT(b)
                    fill(FILL_ATT[n + 1 + 2 * b])
                    if b + 1 < NSEQ:
                        ss_exps(b + 1)
                    fill(FILL_ATT[n + 2 + 2 * b])
                ss_out(NSEQ - 1)

            def square_x(i):
                act.wait_ge(x_in[i % 3], 16 * (i // 3 + 1))
                square(i, xin[0:rows_of(i), i % 3, :], junk)

            square_x(0)
            square_x(1)
            round_x(0)
            split(0)
            square_x(2)
            round_x(1)
            for u in range(NT):
                if u + 3 < NT:
                    square_x(u + 3)
                if u + 2 < NT:
                    round_x(u + 2)
                if u == 4:
                    split(1)
                read_unit(0, u)
            gate_rows_act()
            fill(units_of(1, 1))
            gate_exps()
            fill(units_of(2, 3))
            mlstm_act(0)
            mlstm_act(1)
            fill(units_of(*AQ_BLOCKS))
            attention_act()
            fill(units_of(*GB_BLOCKS))

            act.wait_ge(gemm_a, PROJ_UNITS)
            act.wait_ge(sg_use, 72)
            for i in range(NT):
                nc.scalar.activation(xT_hi[:, :, cols(i)], hT[:, :, cols(i)], ACT.Copy).then_inc(mg_hi, 1)
            split(NPROJ + 1)
            split(NPROJ + 2)
            split(NPROJ + 3)

            def split_mlp(raw_n, slot):
                act.wait_ge(raw_in[slot], raw_n)
                n = KT * WCOLS
                nc.scalar.activation(w_hi[:, slot, 0:n], raw[:, slot, 0:n], ACT.Copy).then_inc(w_hi_done, 1)

            for i in range(NT):
                t = NT + i
                act.wait_ge(free_v, 3 * NT + i + 1)
                square(t, x2[0:rows_of(i), i, :], junk2)
                if i == 2:
                    split_mlp(RAW_ALL[0] + 16, 0)
                if i >= 1:
                    round_x(t - 1)
            round_x(2 * NT - 1)

            def read_up(g, hslot, raw_n, slot):
                for u in range(UP_UNITS):
                    tile, (c0, cn) = u // 3, CHUNKS[u % 3]
                    n = hslot * UP_UNITS + u
                    act.wait_ge(gemm_a, g * UP_UNITS + (PROJ_UNITS + u + 1))
                    if u >= 2:
                        act.wait_ge(lo_done, g * UP_UNITS + (u - 1))
                    elif not isinstance(g, int) or g:
                        act.wait_ge(lo_done, g * UP_UNITS + (u - 1))
                    nc.scalar.activation(relu[:, u % 2, 0:cn], bank[n % 4][:, 0:cn], ACT.Relu).then_inc(free_a, 1)
                    act.wait_ge(free_a, g * UP_UNITS + (PROJ_UNITS + u + 1))
                    nc.scalar.activation(hid_hi[:, hslot, tile, c0:c0 + cn], relu[:, u % 2, 0:cn],
                                         ACT.Square).then_inc(hi_done, 1)
                    if u == 1:
                        split_mlp(raw_n, slot)

            read_up(0, 0, RAW_ALL[1] + 16, 1)
            with act.Fori(0, NG // 2 - 1) as it:
                for x in range(2):
                    g = it * 2 + (1 + x)
                    read_up(g, (1 + x) % 2, it * 32 + (RAW_ALL[0] + 32 + 16 * x), 0)
                    split_mlp(it * 32 + (RAW_ALL[1] + 32 + 16 * x), 1)
            g = NG - 1
            read_up(g, 1, RAW_ALL[0] + 16 * NG, 0)
            split_mlp(RAW_ALL[1] + 16 * NG, 1)
            for i in range(NT):
                act.wait_ge(free_v, OUT_UNITS + DN_UNITS * g + 2 * i + 2)
                square(2 * NT + i, x2[0:rows_of(i), i, :], junk2)

        @block.vector
        def _(dve):
            chain = [0]

            def link(ins):
                chain[0] += 1
                ins.then_inc(dve_chain, 1)
                dve.wait_ge(dve_chain, chain[0])

            def split(b):
                dve.wait_ge(w_hi_done, b + 1)
                n = block_cols(b)
                nc.vector.tensor_tensor(w_lo[:, b % 2, 0:n], raw[:, b % 2, 0:n], w_hi[:, b % 2, 0:n].bitcast(F32),
                                        ALU.subtract).then_inc(w_lo_done, 1)

            def normalise(t, src, dst, wait_slot):
                i = t % NT
                rows = rows_of(i)
                dve.wait_ge(norm_rs, t + 1)
                wait_slot()
                return nc.vector.scalar_tensor_tensor(dst[0:rows, i % 2, :], src, rstd[0:rows, t // NT, i:i + 1],
                                                      gain_b[0:rows, :], ALU.mult, ALU.mult)

            def norm_tile(t, src, dst):
                def slot():
                    if t % NT >= 2:
                        dve.wait_ge(norm_tp, 2 * (t - 1))
                normalise(t, src, dst, slot).then_inc(norm_xn, 1)

            def rest_x(t):
                i = t % NT
                for h in range(2):
                    n = 2 * t + h
                    dve.wait_ge(norm_hi, n + 1)
                    out = xT_lo[:, 4 * h:4 * h + 4, cols(i)]
                    nc.vector.tensor_tensor(out, half_view(4 + n % 4, rows_of(i)),
                                            xT_hi[:, 4 * h:4 * h + 4, cols(i)].bitcast(F32),
                                            ALU.subtract).then_inc(norm_lo, 1)

            def gate_scans():
                dve.wait_ge(gate_ln, 1)
                dve.wait_ge(consts, 3)
                link(nc.vector.scalar_tensor_tensor(row_f[:, :], row_f[:, :], 0.0, row_t[:, :], ALU.min, ALU.subtract))
                nc.vector.tensor_tensor_scan(row_b[:, :], row_r[:, :], row_f[:, :], 0.0, ALU.mult, ALU.add)
                nc.vector.tensor_tensor_scan(row_m[:, 0:SEQ], row_f[:, 0:SEQ], row_i[:, 0:SEQ], 0.0, ALU.add, ALU.max)
                for b in range(NSEQ):
                    at = slice(SEQ + b * DSEQ, SEQ + (b + 1) * DSEQ)
                    ins = nc.vector.tensor_tensor_scan(row_m[:, at], row_f[:, at], row_i[:, at], sm_rows[:, b:b + 1],
                                                       ALU.add, ALU.max)
                link(ins)
                nc.vector.tensor_tensor(q4[0:MH, :], row_i[:, :], row_b[:, :], ALU.subtract)
                link(nc.vector.tensor_tensor(row_x[:, :], row_b[:, :], row_m[:, :], ALU.subtract))

                def runs(t, a, b, n):
                    return t[0:MH, a:b].rearrange("h (c t) -> h c t", t=n)

                def spread(v, c, n):
                    return v.unsqueeze(2).broadcast_to([MH, c, n])

                nc.vector.tensor_copy(row_t[:, 0:P], row_x[:, 0:P])
                nc.vector.tensor_tensor(runs(row_t, P, SEQ, P), runs(row_x, P, SEQ, P),
                                        spread(row_m[:, P - 1:SEQ - P:P], SEQ // P - 1, P), ALU.add)
                nc.vector.tensor_tensor(runs(row_t, SEQ, T, DSEQ), runs(row_x, SEQ, T, DSEQ),
                                        spread(sm_rows[:, :], NSEQ, DSEQ), ALU.add)
                nc.vector.tensor_tensor(runs(row_i, 0, SEQ, P), runs(q4, 0, SEQ, P),
                                        spread(row_x[:, P - 1:SEQ:P], SEQ // P, P), ALU.add)
                nc.vector.tensor_tensor(runs(row_i, SEQ, T, DSEQ), runs(q4, SEQ, T, DSEQ),
                                        spread(row_x[:, SEQ + DSEQ - 1:T:DSEQ], NSEQ, DSEQ), ALU.add)\
                    .then_inc(gate_arg, 1)

            def gate_ends():
                dve.wait_ge(gate_exp, 1)
                nc.vector.tensor_copy(ends[:, 0:8], row_t[:, P - 1:SEQ:P])
                nc.vector.tensor_copy(ends[:, 8:16], row_t[:, SEQ + DSEQ - 1:T:DSEQ])
                nc.vector.tensor_copy(m_out[:, 0:NSEQ], row_m[:, SEQ + DSEQ - 1:T:DSEQ])
                nc.vector.tensor_copy(m_out[:, NSEQ:NSEQ + 1], row_m[:, SEQ - 1:SEQ]).then_inc(gate_fin, 1)

            def gate_columns():
                dve.wait_ge(gate_q4, 3)
                for b, i0, k, r in ((4, 0, 4, P), (5, 4, 4, P), (6, 8, 1, 64)):
                    for q in range(4):
                        if q != 1:
                            src = bank[b][0:r, 0:k * P].rearrange("t (i q h) -> t i q h", q=4, h=32)[:, :, q, 0:MH]
                            ins = nc.vector.tensor_copy(nat[0:r, i0:i0 + k, q, :], src)
                ins.then_inc(gate_nat, 1)

            def ml_first(s):
                p, i = divmod(s, S_PER)
                n = rows_of(i)
                dve.wait_ge(bc_in[s % 2], 32 * (s // 2 + 1))
                if s >= 2:
                    dve.wait_ge(ml_n, s - 1)
                if s == 0:
                    dve.wait_ge(gate_nat, 1)
                    dve.wait_ge(consts, 3)
                mask = causal if n == P else causal8
                for hh in range(2):
                    ins = nc.vector.scalar_tensor_tensor(wgt[0:n, s % 2, hh, 0:n], bc[0:n, s % 2, hh, 0:n],
                                                         nat[0:n, i, 0, 2 * p + hh:2 * p + hh + 1], mask[0:n, 0:n],
                                                         ALU.add, ALU.min)
                ins.then_inc(ml_wa, 1)
                dve.wait_ge(ml_st, s + 1)
                dve.wait_ge(ml_we, s + 1)
                w = wgt[0:n, s % 2, :, 0:n]
                nc.vector.tensor_tensor(w, bank[5][0:n, 0:256].rearrange("s (h t) -> s h t", h=2)[:, :, 0:n], w,
                                        ALU.mult).then_inc(ml_sw, 1)

            def ml_norm(s):
                n = rows_of(s % S_PER)
                dve.wait_ge(ml_rs, s + 1)
                for hh in range(2):
                    v = hh_b[0:n, s % 2, :, hh, :]
                    ins = nc.vector.tensor_scalar(v, v, small[0:n, s % 2, 6 + hh:7 + hh], None, ALU.mult)
                ins.then_inc(ml_hn, 1)

            def sampled_states(p, hh):
                for b in range(NSEQ):
                    dve.wait_ge(ml_su, (2 * p + hh) * NSEQ + b + 1)
                    v = Cin[:, b // 4, b % 4, :]
                    nc.vector.scalar_tensor_tensor(v, v, dec[:, 2 * p + hh, 8 + b:9 + b], bank[4 + b % 2][:, 0:VA],
                                                   ALU.mult, ALU.add).then_inc(ml_sc, 1)

            def ml_second(s):
                p, i = divmod(s, S_PER)
                n = rows_of(i)
                dve.wait_ge(ml_ab, s + 1)
                link(nc.vector.tensor_tensor(small[0:n, s % 2, 2:4], small[0:n, s % 2, 0:2],
                                             nat[0:n, i, 2, 2 * p:2 * p + 2], ALU.max))
                ins = nc.vector.reciprocal(small[0:n, s % 2, 2:4], small[0:n, s % 2, 2:4])
                ins.then_inc(ml_rc, 1)
                dve.wait_ge(ml_rc, s + 1)
                nc.vector.tensor_scalar(hh_b[0:n, s % 2, :, 1, :], by_group(bank[7][0:n, 0:DV]), small[0:n, s % 2, 3:4], None,
                                        ALU.mult).then_inc(ml_h1, 1)
                if i < NT - 1:
                    c = (NT - 1) * p + i
                    dve.wait_ge(ml_u, c + 1)
                    if i == 0:
                        dve.wait_ge(dec_in, 16)
                        dve.wait_ge(ml_cl, p + 1)
                    else:
                        dve.wait_ge(ml_c, c)
                    for hh in range(2):
                        ins = nc.vector.scalar_tensor_tensor(Cst[:, hh, :], Cst[:, hh, :],
                                                             dec[:, 2 * p + hh, i:i + 1], bank[4 + hh][:, 0:VA],
                                                             ALU.mult, ALU.add)
                    ins.then_inc(ml_c, 1)
                    return
                sampled_states(p, 1)

            def fill(units):
                for b, u in units:
                    if (b, u) in GATES:
                        gated(b, u)
                    if u == 2:
                        split(b + 1)

            def mlstm_dve(p):
                s0 = p * S_PER
                ml_first(s0)
                for i in range(NT):
                    s = s0 + i
                    if i == NT - 1:
                        sampled_states(p, 0)
                        fill(FILL_ML[p][2 * i])
                    ml_second(s)
                    ml_norm(s)
                    if i < NT - 1:
                        fill(FILL_ML[p][2 * i])
                        ml_first(s + 1)
                    fill(FILL_ML[p][2 * i + 1])

            def at_mask(u):
                i, kv = divmod(u, NKV)
                lo = 0 if i else P
                dve.wait_ge(at_s, u + 1)
                if u == 0:
                    dve.wait_ge(consts, 6)
                if u >= 2:
                    dve.wait_ge(at_t, u - 1)
                st = ast[:, u % 2]
                for g in range(GRP):
                    src = bank[3 + g // 2][:, (g % 2) * 256 + lo:(g % 2) * 256 + 256]
                    ins = nc.vector.tensor_tensor_reduce(out=prob[:, u % 2, g, lo:], in0=src, in1=amask[:, lo:],
                                                         scale=1.0, scalar=-BIG, op0=ALU.add, op1=ALU.max,
                                                         accum_out=st[:, 0, g:g + 1])
                link(ins)
                sk = sink_b[:, kv * GRP:(kv + 1) * GRP]
                link(nc.vector.scalar_tensor_tensor(st[:, 1, :], st[:, 0, :], ATT_SCALE, sk, ALU.mult, ALU.max))
                nc.vector.tensor_scalar(st[:, 2, :], st[:, 1, :], -1.0, None, ALU.mult)
                nc.vector.tensor_tensor(st[:, 3, :], sk, st[:, 1, :], ALU.subtract).then_inc(at_m, 1)

            def at_divide(u):
                lo = 0 if u >= NKV else P
                dve.wait_ge(at_e, u + 1)
                st = ast[:, u % 2]
                link(nc.vector.tensor_tensor(st[:, 5, :], st[:, 4, :], st[:, 3, :], ALU.add))
                link(nc.vector.reciprocal(st[:, 5, :], st[:, 5, :]))
                for g in range(GRP):
                    v = prob[:, u % 2, g, lo:]
                    ins = nc.vector.tensor_scalar(v, v, st[:, 5, g:g + 1], None, ALU.mult)
                ins.then_inc(at_p, 1)

            def at_own(u):
                dve.wait_ge(at_t, u + 1)
                if u >= 1:
                    dve.wait_ge(at_v, u)
                nc.vector.tensor_copy(pT[:, 1, :], bank[6][:, :]).then_inc(at_p1, 1)

            def ss_mask(b):
                dve.wait_ge(ss_s, b + 1)
                if b == 0:
                    dve.wait_ge(mask_io, 16 * 17)
                if b >= 2:
                    dve.wait_ge(ss_t, b - 1)
                st = sst[:, b % 2]
                link(nc.vector.tensor_tensor_reduce(out=sprob[:, b % 2, :], in0=bank[4][:, 0:192], in1=smask[:, b, :],
                                                    scale=1.0, scalar=-BIG, op0=ALU.add, op1=ALU.max,
                                                    accum_out=st[:, 0:1]))
                link(nc.vector.scalar_tensor_tensor(st[:, 1:2], st[:, 0:1], ATT_SCALE, sink_s[:, :], ALU.mult, ALU.max))
                nc.vector.tensor_scalar(st[:, 2:3], st[:, 1:2], -1.0, None, ALU.mult)
                nc.vector.tensor_tensor(st[:, 3:4], sink_s[:, :], st[:, 1:2], ALU.subtract).then_inc(ss_m, 1)

            def ss_divide(b):
                dve.wait_ge(ss_e, b + 1)
                st = sst[:, b % 2]
                link(nc.vector.tensor_tensor(st[:, 5:6], st[:, 4:5], st[:, 3:4], ALU.add))
                link(nc.vector.reciprocal(st[:, 5:6], st[:, 5:6]))
                v = sprob[:, b % 2, :]
                nc.vector.tensor_scalar(v, v, st[:, 5:6], None, ALU.mult).then_inc(ss_p, 1)

            def ss_gather(b):
                dve.wait_ge(ss_v, b + 1)
                if b >= 1:
                    dve.wait_ge(ss_ot, b)
                if b == 0:
                    link(nc.vector.memset(o2[:, :], 0.0))
                for kv in range(NKV):
                    at = slice(32 * kv, 32 * kv + 32)
                    half = kv % 2
                    ins = nc.vector.tensor_copy(o2[at, 64 * half:64 * half + 64], bank[6][at, kv * HD:(kv + 1) * HD])
                ins.then_inc(ss_o2, 1)

            def attention_dve():
                n = 8 * NKV
                at_mask(0)
                for u in range(n):
                    at_divide(u)
                    if u + 1 < n:
                        at_mask(u + 1)
                    at_own(u)
                    fill(FILL_ATT[u])
                dve.wait_ge(at_v, n)
                for p in range(2):
                    ins = nc.vector.tensor_copy(qsmp[:, p, :, :, :].rearrange("c b g t -> c g b t"),
                                                aqT[:, p * GRP:(p + 1) * GRP, SEQ:T]
                                                .rearrange("c g (b t) -> c g b t", t=DSEQ))
                ins.then_inc(ss_q, 1)
                fill(FILL_ATT[n])
                ss_mask(0)
                ss_divide(0)
                for b in range(NSEQ):
                    fill(FILL_ATT[n + 1 + 2 * b])
                    if b + 1 < NSEQ:
                        ss_mask(b + 1)
                        ss_divide(b + 1)
                    ss_gather(b)
                    fill(FILL_ATT[n + 2 + 2 * b])

            def gated(b, u):
                kind, p, gg = BLOCKS[b]
                m = GATES[b, u]
                tile, (c0, cn) = u // 3, CHUNKS[u % 3]
                j = p * GRP + 2 * gg + tile
                dve.wait_ge(free_a, FIRST_UNIT[b] + u + 1)
                h = hT[:, j, c0:c0 + cn]
                g = sig[:, m % 2, 0:cn]
                if kind == "mo":
                    nc.vector.scalar_tensor_tensor(h, h, mnorm[:, j:j + 1], g, ALU.mult, ALU.mult).then_inc(sg_use, 1)
                elif kind == "ga":
                    dve.wait_ge(sg_use, m - 5)
                    nc.vector.tensor_tensor(h, h, g, ALU.mult).then_inc(sg_use, 1)
                else:
                    a = aqT[:, j, c0:c0 + cn]
                    dve.wait_ge(sg_use, 48)
                    link(nc.vector.tensor_tensor(a, a, g, ALU.mult))
                    nc.vector.tensor_tensor(h, h, a, ALU.add).then_inc(sg_use, 1)

            dve.wait_ge(gain_in, 16)
            norm_tile(0, xin[:, 0, :], xn)
            norm_tile(1, xin[:, 1, :], xn)
            rest_x(0)
            split(0)
            norm_tile(2, xin[:, 2, :], xn)
            rest_x(1)
            for i in range(3, NT + 1):
                if i < NT:
                    norm_tile(i, xin[0:rows_of(i), i % 3, :], xn)
                rest_x(i - 1)
                if i == 6:
                    split(1)
            fill(units_of(1, 1))
            gate_scans()
            gate_ends()
            fill(units_of(2, 3))
            gate_columns()
            mlstm_dve(0)
            mlstm_dve(1)
            fill(units_of(*AQ_BLOCKS))
            attention_dve()
            fill(units_of(*GB_BLOCKS))

            for i in range(NT):
                dve.wait_ge(mg_hi, i + 1)
                nc.vector.tensor_tensor(xT_lo[:, :, cols(i)], hT[:, :, cols(i)], xT_hi[:, :, cols(i)].bitcast(F32),
                                        ALU.subtract).then_inc(mg_lo, 1)
            def split_mlp(count, slot):
                dve.wait_ge(w_hi_done, count)
                n = KT * WCOLS
                nc.vector.tensor_tensor(w_lo[:, slot, 0:n], raw[:, slot, 0:n], w_hi[:, slot, 0:n].bitcast(F32),
                                        ALU.subtract).then_inc(w_lo_done, 1)

            for cq in range(4):
                for i in range(NT):
                    if i == 3 and cq < 3:
                        split(NPROJ + 1 + cq)
                    m = NT * cq + i
                    r = rows_of(i)
                    if cq == 0:
                        dve.wait_ge(x2_in[i], 16)
                    dve.wait_ge(gemm_v, m + 1)
                    v = x2[0:r, i, cq * WCOLS:(cq + 1) * WCOLS]
                    nc.vector.tensor_tensor(v, bank[m % 4][0:r, 0:WCOLS], v, ALU.add).then_inc(free_v, 1)
                    if cq < 3:
                        continue
                    if i == 1:
                        dve.wait_ge(gain_in, 32)
                    if i >= 1:
                        norm_tile(NT + i - 1, x2[:, i - 1, :], ybuf)
                    if i == 4:
                        split_mlp(B_MLP + 1, 0)
                    if i >= 2:
                        rest_x(NT + i - 2)
            norm_tile(2 * NT - 1, x2[0:rows_of(NT - 1), NT - 1, :], ybuf)
            rest_x(2 * NT - 2)
            rest_x(2 * NT - 1)

            def hidden(g, hslot, count, slot):
                for u in range(UP_UNITS):
                    tile, (c0, cn) = u // 3, CHUNKS[u % 3]
                    dve.wait_ge(free_a, g * UP_UNITS + (PROJ_UNITS + u + 1))
                    nc.vector.tensor_tensor(sqr[:, u % 2, 0:cn], relu[:, u % 2, 0:cn], relu[:, u % 2, 0:cn],
                                            ALU.mult).then_inc(sq_done, 1)
                    dve.wait_ge(sq_done, g * UP_UNITS + (u + 1))
                    dve.wait_ge(hi_done, g * UP_UNITS + (u + 1))
                    nc.vector.tensor_tensor(hid_lo[:, hslot, tile, c0:c0 + cn], sqr[:, u % 2, 0:cn],
                                            hid_hi[:, hslot, tile, c0:c0 + cn].bitcast(F32),
                                            ALU.subtract).then_inc(lo_done, 1)
                    if u == 1:
                        split_mlp(count, slot)

            def accumulate(g, hslot, i):
                for half in range(2):
                    r = rows_of(i)
                    d = hslot * DN_UNITS + 2 * i + half
                    dve.wait_ge(gemm_v, g * DN_UNITS + (OUT_UNITS + 2 * i + half + 1))
                    v = x2[0:r, i, half * 512:half * 512 + 512]
                    nc.vector.tensor_tensor(v, bank[4 + d % 4][0:r, :], v, ALU.add).then_inc(free_v, 1)

            hidden(0, 0, B_MLP + 2, 1)
            with dve.Fori(0, NG // 2 - 1) as it:
                for x in range(2):
                    hidden(it * 2 + (1 + x), (1 + x) % 2, it * 4 + (B_MLP + 3 + 2 * x), 0)
                    for i in range(NT):
                        accumulate(it * 2 + x, x, i)
                        if i == 4:
                            split_mlp(it * 4 + (B_MLP + 4 + 2 * x), 1)
            hidden(NG - 1, 1, B_MLP + 2 * NG - 1, 0)
            for i in range(NT):
                accumulate(NG - 2, 0, i)
                if i == 4:
                    split_mlp(B_MLP + 2 * NG, 1)
            dve.wait_ge(gain_in, 48)

            def final(i):
                def slot():
                    if i >= 2:
                        dve.wait_ge(y_out[i % 2], 16 * (i // 2))
                normalise(2 * NT + i, x2[0:rows_of(i), i, :], ybuf, slot).then_inc(y_rdy, 1)

            for i in range(NT):
                accumulate(NG - 1, 1, i)
                if i >= 1:
                    final(i - 1)
            final(NT - 1)

        @block.gpsimd
        def _(pool):
            chain = [0]

            def link(ins):
                chain[0] += 1
                ins.then_inc(pool_chain, 1)
                pool.wait_ge(pool_chain, chain[0])

            def keep_where(t, pattern, base, ch, op, fill):
                return nc.gpsimd.affine_select(out=t, in_=t, compare_op=op, fill=fill, base=base, pattern=pattern,
                                               channel_multiplier=ch)

            nc.gpsimd.memset(neghalf[:, :], -0.5)
            link(nc.gpsimd.memset(ident[:, :], 0.0))
            keep_where(ident[:, :], [[-1, P]], 0, 1, ALU.not_equal, 1.0).then_inc(consts, 1)

            def rms(t):
                rows = rows_of(t % NT)
                pool.wait_ge(norm_sq, t + 1)
                v = rstd[0:rows, t // NT, t % NT:t % NT + 1]
                link(nc.gpsimd.tensor_scalar(v, stat[0:rows, t // NT, t % NT:t % NT + 1], 1.0 / D, EPS,
                                             ALU.mult, ALU.add))
                nc.gpsimd.tensor_tensor(v, v, neghalf[0:rows, 0:1], ALU.pow).then_inc(norm_rs, 1)

            for t in range(NT):
                rms(t)
            nc.gpsimd.memset(causal8[:, :], BIG)
            nc.gpsimd.memset(seq_ind[:, :], 1.0)
            nc.gpsimd.memset(vaug0[:, :, :, DV:VA], 1.0)
            link(nc.gpsimd.memset(causal[:, :], BIG))
            keep_where(causal[:, :], [[1, P]], 0, -1, ALU.is_ge, -BIG)
            link(keep_where(causal8[:, :], [[1, 64]], 0, -1, ALU.is_ge, -BIG))
            c8 = causal8[:, :].rearrange("s (b t) -> s b t", t=DSEQ)
            keep_where(c8, [[-DSEQ, NSEQ], [0, DSEQ]], 0, 1, ALU.is_ge, -BIG)
            link(keep_where(seq_ind[:, :], [[-DSEQ, NSEQ]], 0, 1, ALU.is_ge, 0.0))
            keep_where(seq_ind[:, :], [[DSEQ, NSEQ]], DSEQ - 1, -1, ALU.is_ge, 0.0)
            nc.gpsimd.memset(qz[:, :, :], 0.0)
            nc.gpsimd.memset(Cst[:, :, :], 0.0).then_inc(ml_cl, 1)
            nc.gpsimd.memset(q4[:, :], 0.0).then_inc(consts, 1)
            link(nc.gpsimd.memset(row_r[:, :], 1.0))
            nc.gpsimd.memset(row_r[:, 0:SEQ:P], 0.0)
            nc.gpsimd.memset(row_r[:, SEQ:T:DSEQ], 0.0).then_inc(consts, 1)

            def ml_query(s):
                p, i = divmod(s, S_PER)
                n = rows_of(i)
                pool.wait_ge(bc_in[s % 2], 32 * (s // 2 + 1))
                if i == 0:
                    pool.wait_ge(free_a, FIRST_UNIT[4 * p + 4])
                if i < NT - 1:
                    if s >= 2:
                        pool.wait_ge(ml_n, s - 1)
                    nc.gpsimd.tensor_tensor(qs[:, s % 2, :, 0:n], hT[:, p * GRP:p * GRP + 2, cols(i)], bc[:, s % 2, 2:4, 0:n],
                                            ALU.mult).then_inc(ml_qs, 1)
                    return
                for hh in range(2):
                    dst = qz[:, hh, :].rearrange("c (b x) -> c b x", x=72)[:, :, 0:DSEQ]
                    ins = nc.gpsimd.tensor_tensor(dst, mq(p, hh, cols(i)).rearrange("c (b t) -> c b t", t=DSEQ),
                                                  bc[:, s % 2, 2 + hh, 0:n].rearrange("c (b t) -> c b t", t=DSEQ),
                                                  ALU.mult)
                ins.then_inc(ml_qs, 1)

            def ml_keys(s, hh):
                p = s // S_PER
                n = rows_of(NT - 1)
                pool.wait_ge(ml_kw, s + 1)
                if hh or p:
                    pool.wait_ge(ml_su, (2 * p + hh) * NSEQ)
                nc.gpsimd.tensor_tensor(kwz[:, :, :],
                                        kw[0:n, s % 2, hh, :].unsqueeze(1).broadcast_to([n, NSEQ, DK]),
                                        seq_ind[:, :].unsqueeze(2).broadcast_to([n, NSEQ, DK]),
                                        ALU.mult).then_inc(ml_kz, 1)

            def ml_rms(s):
                n = rows_of(s % S_PER)
                pool.wait_ge(ml_ss, 2 * s + 2)
                v = small[0:n, s % 2, 6:8]
                link(nc.gpsimd.tensor_scalar(v, small[0:n, s % 2, 4:6], 1.0 / DV, EPS, ALU.mult, ALU.add))
                nc.gpsimd.tensor_tensor(v, v, neghalf[0:n, :], ALU.pow).then_inc(ml_rs, 1)

            pool.wait_ge(gate_nat, 1)
            pool.wait_ge(rows_out, 48)
            nc.gpsimd.memset(vaug1[:, :, :, DV:VA], 1.0).then_inc(ones, 1)
            for p in range(2):
                if p:
                    pool.wait_ge(pc_out, 32)
                    nc.gpsimd.memset(Cst[:, :, :], 0.0).then_inc(ml_cl, 1)
                s0 = p * S_PER
                ml_query(s0)
                for s in range(s0, s0 + S_PER):
                    if s + 1 < s0 + S_PER:
                        ml_query(s + 1)
                    if s == s0 + NT - 2:
                        ml_keys(s + 1, 0)
                    if s == s0 + NT - 1:
                        ml_keys(s, 1)
                    ml_rms(s)

            pool.wait_ge(cin_out, 32 * 8)
            pool.wait_ge(pc_out, 64)
            pool.wait_ge(ml_hn, 2 * S_PER)
            pool.wait_ge(ml_t, 2 * S_PER)
            link(nc.gpsimd.memset(amask[:, :], 0.0))
            keep_where(amask[:, 0:P], [[1, P]], -1, -1, ALU.is_ge, -BIG).then_inc(consts, 2)
            keep_where(amask[:, P:2 * P], [[-1, P]], 0, 1, ALU.is_ge, -BIG).then_inc(consts, 1)
            pool.wait_ge(at_v, 8 * NKV)
            pool.wait_ge(at_o, 8 * NKV)
            link(nc.gpsimd.memset(smask[0:DSEQ, :, :], 0.0))
            old = smask[0:DSEQ, :, 0:P]
            new = smask[0:DSEQ, :, P:192].rearrange("t b (c u) -> t b c u", u=DSEQ)
            keep_where(old, [[0, NSEQ], [1, P]], -1, -1, ALU.is_ge, -BIG)
            link(keep_where(new, [[0, NSEQ], [0, NSEQ], [-1, DSEQ]], 0, 1, ALU.is_ge, -BIG))
            keep_where(new, [[1, NSEQ], [-1, NSEQ], [0, DSEQ]], 0, 0, ALU.is_equal, -BIG).then_inc(mask_made, 1)

            for t in range(NT, 3 * NT):
                rms(t)


_INS = ["x_prompt", "x_sample", "state_C", "state_n", "state_m", "cache_k", "cache_v", "norm_attn", "w_in", "b_gate",
        "mlstm_norm", "sinks", "w_out", "norm_mlp", "w_up", "w_down", "norm_final"]
_OUTS = [(1, SEQ, D), (NSEQ, DSEQ, D), (1, 1, MH, DK, DV), (1, 1, MH, DK), (1, 1, MH),
         (1, 1, WIN, NKV, HD), (1, 1, WIN, NKV, HD), (1, NSEQ, MH, DK, DV), (1, NSEQ, MH, DK), (1, NSEQ, MH),
         (1, NSEQ, WIN, NKV, HD), (1, NSEQ, WIN, NKV, HD)]


def kernel(**inputs):
    import numpy as _np
    import concourse.bacc as _bacc
    from concourse import mybir as _mybir
    from concourse.bass_utils import run_bass_kernel_spmd as _run

    nc = _bacc.Bacc("TRN2", target_bir_lowering=False, num_devices=1, dynamic_dma_scratch_size=1024)
    arrays, args = {}, []
    for name in _INS:
        a = _np.ascontiguousarray(inputs[name])
        arrays[f"in_{name}"] = a
        args.append(nc.dram_tensor(f"in_{name}", a.shape, _mybir.dt.from_np(a.dtype), kind="ExternalInput").ap())
    for i, shape in enumerate(_OUTS):
        args.append(nc.dram_tensor(f"out_{i}", shape, _mybir.dt.float32, kind="ExternalOutput").ap())
    layer_kernel(nc, *args)
    r = _run(nc, [arrays], core_ids=[0])
    return tuple(r.results[0][f"out_{i}"] for i in range(len(_OUTS)))
```

```python
from contextlib import ExitStack

import concourse.bass as bass
from concourse import mybir

F32 = mybir.dt.float32
F32R = mybir.dt.float32r
ALU = mybir.AluOpType
ACT = mybir.ActivationFunctionType

P = 128
D = 1024
SEQ = 1024
NSEQ = 8
DSEQ = 8
T = SEQ + NSEQ * DSEQ
NT = (T + P - 1) // P
KT = D // P
MH = 4
DK = 128
DV = 256
VA = DV + 1
HD = 64
NKV = 4
GRP = 4
WIN = 128
FF = 4096
EPS = 1e-6
BIG = 1e30
C_MQ = 0
C_MK = C_MQ + MH * DK
C_MV = C_MK + MH * DK
C_MO = C_MV + MH * DV
C_GATE = C_MO + MH * DV
C_AQ = C_GATE + 2 * MH
C_AK = C_AQ + D
C_AV = C_AK + NKV * HD
C_GA = C_AV + NKV * HD
C_GB = C_GA + D
WCOLS = 256
BLK = KT * (WCOLS + 8)
CHUNKS = [(0, 384), (384, 384), (768, 320)]
QK_SCALE = float(DK) ** -0.5
ATT_SCALE = float(HD) ** -0.5
NG = FF // WCOLS


def rows_of(i):
    return P if i < NT - 1 else T - P * (NT - 1)


def block_list():
    out = [("v", 0), ("v", 1), ("mk", 0), ("mq", 0), ("v", 2), ("v", 3), ("mk", 1), ("mq", 1)]
    out += [("av",), ("mo", 0, 0), ("ga", 0, 0), ("mo", 0, 1)]
    out += [("ak",)] + [("aq", p, gg) for p in range(2) for gg in range(2)]
    out += [("ga", 0, 1)] + [(kind, 1, gg) for gg in range(2) for kind in ("mo", "ga")]
    out += [("gb", p, gg) for p in range(2) for gg in range(2)]
    out += [("out", cq) for cq in range(4)]
    return out


BLOCKS = block_list()
NPROJ = len(BLOCKS) - 4
NATURAL = ("v", "av", "out")


def n_units(b):
    return NT if BLOCKS[b][0] in NATURAL else 2 * len(CHUNKS)


FIRST_UNIT = [sum(n_units(x) for x in range(b)) for b in range(NPROJ + 1)]
PROJ_UNITS = FIRST_UNIT[NPROJ]
OUT_UNITS = 4 * NT
B_MLP = len(BLOCKS)
RING = 3
SPLIT_AT = 3
NB = SEQ // P
MASKW = WIN + (2 * NSEQ - 1) * DSEQ
UP_UNITS = 2 * len(CHUNKS)
DN_UNITS = 2 * NT
DN_ORDER = [NT - 1] + list(range(NT - 1))
NS = NSEQ * DSEQ


def tile_of(t):
    return t % NT if t < 2 * NT else DN_ORDER[t % NT]


def units_of(first, last):
    return [(b, u) for b in range(first, last + 1) for u in range(n_units(b))]


def spread(units, slots):
    n, out, at = sum(slots), [], 0
    for k in range(len(slots)):
        upto = -(-len(units) * sum(slots[:k + 1]) // n)
        out.append(units[at:upto])
        at = upto
    return out


W_P0, W_SS, W_P1 = [3] + [3] * 16, [8] + [4, 2] * NSEQ, [3] + [3] * 16
FILL_ML = [spread(units_of(4, 7), [2] + [2, 1] * NT),
           spread(units_of(8, 11), [3] + [2, 1] * (NT - 1) + [4, 2])]
HALF = 2 * NB
FILL_ATT = spread(units_of(15, 23), W_P0 + W_SS + W_P1)
FILL_P0, FILL_SS, FILL_P1 = FILL_ATT[:HALF + 1], FILL_ATT[HALF + 1:-HALF - 1], FILL_ATT[-HALF - 1:]
GATES = {}
for _b in range(NPROJ):
    if BLOCKS[_b][0] in ("mo", "ga", "gb"):
        for _u in range(n_units(_b)):
            GATES[_b, _u] = len(GATES)


def layer_kernel(nc, x_prompt, x_sample, state_C, state_n, state_m, cache_k, cache_v, norm_attn, w_in, b_gate,
                 mlstm_norm, sinks, w_out, norm_mlp, w_up, w_down, norm_final,
                 y_prompt, y_sample, p_C, p_n, p_m, p_k, p_v, s_C, s_n, s_m, s_k, s_v):
    xs_flat = x_sample.rearrange("b t d -> (b t) d")
    ys_flat = y_sample.rearrange("b t d -> (b t) d")

    def x_rows(i):
        return x_prompt[0, i * P:(i + 1) * P, :] if i < NT - 1 else xs_flat

    def y_rows(i):
        return y_prompt[0, i * P:(i + 1) * P, :] if i < NT - 1 else ys_flat

    w_in_k = w_in[0].rearrange("(k p) c -> p k c", p=P)
    w_up_k = w_up[0].rearrange("(k p) c -> p k c", p=P)
    w_dn_k = w_down[0].rearrange("(k p) c -> p k c", p=P)
    gate_rows = nc.dram_tensor("gate_rows", (2, MH, T), F32, kind="Internal").ap()
    ends_dram = nc.dram_tensor("ends_dram", (MH, 16), F32, kind="Internal").ap()
    mask_dram = nc.dram_tensor("mask_dram", (DSEQ, MASKW), F32, kind="Internal").ap()

    ctx = ExitStack()
    with ctx:
        def scope_alloc(stack):
            def alloc(name, shape, dt=F32):
                return stack.enter_context(nc.sbuf_tensor(name, shape, dt))
            return alloc

        sb = scope_alloc(ctx)

        def sem(name):
            return ctx.enter_context(nc.semaphore(name))

        bank = [ctx.enter_context(nc.psum_tensor(f"bank{n}", [P, 512], F32)) for n in range(8)]

        ident = sb("ident", [P, P])
        with ExitStack() as s:
            kout = scope_alloc(s)("kout", [P, 2, NKV * HD])
        gain_b = sb("gain_b", [P, D])
        with ExitStack() as s:
            raw = scope_alloc(s)("raw", [P, 2, BLK])
        w_lo = sb("w_lo", [P, 2, BLK], F32R)
        w_hi = sb("w_hi", [P, 2, BLK], F32R)
        xT_hi = sb("xT_hi", [P, KT, T], F32R)
        xT_lo = sb("xT_lo", [P, KT, T], F32R)
        stat = sb("stat", [P, 3, NT])
        rstd = sb("rstd", [P, 3, NT])
        neghalf = sb("neghalf", [P, 2])
        mnorm = sb("mnorm", [P, KT])
        sink_b = sb("sink_b", [P, 16])
        sink_s = sb("sink_s", [P, 1])
        sig = sb("sig", [P, 2, 384])

        with ExitStack() as s:
            a = scope_alloc(s)
            xin = a("xin", [P, 3, D])
            xn = a("xn", [P, 2, D])
            junk = a("junk", [P, D])
        s = ExitStack()
        with s:
            a = scope_alloc(s)
            hT = a("hT", [P, KT, T])
            vaug0 = a("vaug0", [P, NT, 2, VA])
            gnat = a("gnat", [P, NT, 8])
            nat = a("nat", [P, NT, 4, MH])
            sm_rows = a("sm_rows", [MH, NSEQ])
            bias_i = a("bias_i", [MH, 1])
            bias_f = a("bias_f", [MH, 1])
            ends = a("ends", [MH, 16])
            m_out = a("m_out", [MH, NSEQ + 1])
            dec = a("dec", [P, MH, 16])
            Cst = a("Cst", [P, 2, VA])
            small = a("small", [P, 2, 8])
            qz = a("qz", [P, 2, 576])
            causal = a("causal", [P, P])
            causal8 = a("causal8", [64, 64])
            seq_ind = a("seq_ind", [64, NSEQ])
            with ExitStack() as s2:
                a2 = scope_alloc(s2)
                vaug1 = a2("vaug1", [P, NT, 2, VA])
                Cin = a2("Cin", [P, 2, 4, VA])
                bc = a2("bc", [P, 2, 4, P])
                hh_b = a2("hh_b", [P, 2, GRP, 2, HD])
                kwz = a2("kwz", [64, NSEQ, P])
                hjunk = a2("hjunk", [P, DV])
                wgt = a2("wgt", [P, 2, 2, P])
                qs = a2("qs", [P, 2, 2, P])
                kw = a2("kw", [P, 2, 2, P])
            row_i = a("row_i", [MH, T])
            row_f = a("row_f", [MH, T])
            row_t = a("row_t", [MH, T])
            row_b = a("row_b", [MH, T])
            row_m = a("row_m", [MH, T])
            row_x = a("row_x", [MH, T])
            row_r = a("row_r", [MH, T])
            q4 = a("q4", [P, T])
        vaug = (vaug0, vaug1)
        with ExitStack() as s:
            a = scope_alloc(s)
            a("under_hT", [P, KT, T])
            avn = a("avn", [P, NT, NKV * HD])
            akz = a("akz", [P, NKV, T])
            aqT = a("aqT", [P, KT, T])
            amask = a("amask", [P, 2 * P])
            smask = a("smask", [P, MASKW])
            with ExitStack() as s2:
                a2 = scope_alloc(s2)
                prob = a2("prob", [P, 2, GRP, 2 * P])
                pT = a2("pT", [P, 2, 2, GRP * P])
                ast = a2("ast", [P, 2, 6, GRP])
            with ExitStack() as s2:
                a2 = scope_alloc(s2)
                kc = a2("kc", [P, 2, NKV * HD])
                vc = a2("vc", [P, 2, NKV * HD])
                kcT = a2("kcT", [P, 2, 2, P])
                sprob = a2("sprob", [P, 2, 192])
                spT = a2("spT", [P, 2, P])
                o2 = a2("o2", [P, P])
                qsmp = a2("qsmp", [P, 2, NSEQ, GRP, DSEQ])
                sst = a2("sst", [P, 2, 6])
        with ExitStack() as s:
            a = scope_alloc(s)
            x2 = a("x2", [P, NT, D])
            hid_hi = a("hid_hi", [P, 2, 2, T + NS], F32R)
            hid_lo = a("hid_lo", [P, 2, 2, T], F32R)
            relu = a("relu", [P, 2, 384])
            sqr = a("sqr", [P, 2, 384])
            ybuf = a("ybuf", [P, 2, D])
            junk2 = a("junk2", [P, D])

        x_in = [sem(f"x_in{n}") for n in range(3)]
        raw_in = [sem(f"raw_in{n}") for n in range(2)]
        w_hi_done = sem("w_hi_done")
        w_hi_half = sem("w_hi_half")
        w_lo_done = sem("w_lo_done")
        gain_in = sem("gain_in")
        const_in = sem("const_in")
        consts = sem("consts")
        norm_sq = sem("norm_sq")
        norm_rs = sem("norm_rs")
        norm_xn = sem("norm_xn")
        norm_tp = sem("norm_tp")
        norm_hi = sem("norm_hi")
        norm_lo = sem("norm_lo")
        gemm_a = sem("gemm_a")
        free_a = sem("free_a")
        gemm_v = sem("gemm_v")
        free_v = sem("free_v")
        act_chain = sem("act_chain")
        dve_chain = sem("dve_chain")
        pool_chain = sem("pool_chain")
        gate_tp = sem("gate_tp")
        gate_ev = sem("gate_ev")
        gate_ln = sem("gate_ln")
        gate_arg = sem("gate_arg")
        gate_exp = sem("gate_exp")
        gate_fin = sem("gate_fin")
        gate_q4 = sem("gate_q4")
        gate_nat = sem("gate_nat")
        rows_out = sem("rows_out")
        dec_in = sem("dec_in")
        bc_in = [sem(f"bc_in{n}") for n in range(2)]
        ones = sem("ones")
        ml_kt = sem("ml_kt")
        ml_st = sem("ml_st")
        ml_wa = sem("ml_wa")
        ml_we = sem("ml_we")
        ml_sw = sem("ml_sw")
        ml_qs = sem("ml_qs")
        ml_kw = sem("ml_kw")
        ml_n = sem("ml_n")
        ml_u = sem("ml_u")
        ml_ab = sem("ml_ab")
        ml_rc = sem("ml_rc")
        ml_h0 = sem("ml_h0")
        ml_h1 = sem("ml_h1")
        ml_ss = sem("ml_ss")
        ml_rs = sem("ml_rs")
        ml_hn = sem("ml_hn")
        ml_c = sem("ml_c")
        ml_t = sem("ml_t")
        ml_te = sem("ml_te")
        ml_kz = sem("ml_kz")
        ml_su = sem("ml_su")
        ml_sc = sem("ml_sc")
        ml_cl = sem("ml_cl")
        cin_in = [sem(f"cin_in{n}") for n in range(2)]
        cin_out = sem("cin_out")
        pc_out = sem("pc_out")
        at_s = sem("at_s")
        at_m = sem("at_m")
        at_e = sem("at_e")
        at_p = sem("at_p")
        at_t = sem("at_t")
        at_p0 = sem("at_p0")
        at_p1 = sem("at_p1")
        at_v = sem("at_v")
        at_o = sem("at_o")
        kc_in = [sem(f"kc_in{n}") for n in range(2)]
        vc_in = [sem(f"vc_in{n}") for n in range(2)]
        mask_made = sem("mask_made")
        mask_io = sem("mask_io")
        sk_t = sem("sk_t")
        sk_e = sem("sk_e")
        ss_q = sem("ss_q")
        ss_s = sem("ss_s")
        ss_m = sem("ss_m")
        ss_e = sem("ss_e")
        ss_p = sem("ss_p")
        ss_t = sem("ss_t")
        ss_te = sem("ss_te")
        ss_v = sem("ss_v")
        ss_o2 = sem("ss_o2")
        ss_ot = sem("ss_ot")
        ss_o = sem("ss_o")
        ko_t = sem("ko_t")
        ko_e = sem("ko_e")
        sg_use = sem("sg_use")
        mg_hi = sem("mg_hi")
        mg_lo = sem("mg_lo")
        x2_in = [sem(f"x2_in{n}") for n in range(NT)]
        re_done = sem("re_done")
        hi_done = sem("hi_done")
        sq_done = sem("sq_done")
        lo_done = sem("lo_done")
        y_out = [sem(f"y_out{n}") for n in range(2)]
        folded = sem("folded")
        folded_in = sem("folded_in")
        y_rdy = sem("y_rdy")
        out_dma = sem("out_dma")

        def w_view(t, b, k):
            n = WCOLS + 8 if b == 0 else WCOLS
            return t[:, b % 2, k * n:(k + 1) * n]

        def w_stat(t, b, k, tile):
            return w_view(t, b, k)[:, tile * P:(tile + 1) * P]

        def part_cols(b, half):
            n = BLK if b == 0 else KT * WCOLS
            return slice(0, n) if half is None else slice(half * (n // 2), (half + 1) * (n // 2))

        def mq(p, hh, at):
            return hT[:, p * GRP + hh, at]

        def mk(p, hh, at):
            return hT[:, p * GRP + 2 + hh, at]

        def half_view(n, rows):
            return bank[n][:, :].rearrange("p (k t) -> p k t", t=P)[:, :, 0:rows]

        RAW_DMAS = [{"aq": 4, "mo": 4, "ga": 4, "gb": 4, "out": 4}.get(x[0], 1) for x in BLOCKS]
        RAW_DMAS[0] = 2
        RAW_AT = [16 * sum(RAW_DMAS[b % 2:b + 1:2]) for b in range(B_MLP)]
        RAW_ALL = RAW_AT[-2:]

        def by_group(v):
            return v.rearrange("t (g c) -> t g c", g=GRP)

        def cols(i):
            return slice(i * P, i * P + rows_of(i))

        def done_before(b):
            if b < NPROJ:
                return gemm_a, FIRST_UNIT[b + 1]
            return gemm_v, NT * (b - NPROJ + 1)

        S_PER = NT
        AQ_BLOCKS = (12, 14)
        GB_BLOCKS = (24, 25)

        def out_ring(m):
            return 8 if m < 3 * NT else 4

        def at_unit(u):
            return u % (2 * NB) // 2, u // (2 * NB), u % 2

        def prev_count(u):
            return u + 1 - 2 * (at_unit(u)[1] + 1)

        block = ctx.enter_context(nc.Block())

        @block.sync
        def _(sp):
            def load_block(b):
                kind = BLOCKS[b][0]
                if b >= 2:
                    sp.wait_ge(*done_before(b - 2))
                r = raw[:, b % 2, 0:KT * WCOLS].rearrange("p (k c) -> p k c", k=KT)
                if b == 0:
                    r = raw[:, b % 2, 0:BLK].rearrange("p (k c) -> p k c", k=KT)
                    sp.dma_start(r[:, :, 0:8], w_in_k[:, :, C_GATE:C_GATE + 8],
                                 allow_slow_non_contiguous=True).then_inc(raw_in[b % 2], 16)
                    sp.dma_start(r[:, :, 8:], w_in_k[:, :, C_MV:C_MV + DV]).then_inc(raw_in[b % 2], 16)
                elif kind in ("v", "mk", "mq", "av", "ak"):
                    c0 = {"v": C_MV, "mk": C_MK, "mq": C_MQ, "av": C_AV, "ak": C_AK}[kind]
                    c0 += WCOLS * (BLOCKS[b][1] if len(BLOCKS[b]) > 1 else 0)
                    sp.dma_start(r, w_in_k[:, :, c0:c0 + WCOLS]).then_inc(raw_in[b % 2], 16)
                elif kind == "out":
                    cq = BLOCKS[b][1]
                    src = w_out[0].rearrange("(p h g c) n -> h p c g n", p=2, h=2, g=GRP)
                    for h in range(2):
                        for p in range(2):
                            sp.dma_start(r[64 * h:64 * h + 64, GRP * p:GRP * p + GRP, :],
                                         src[h, p, :, :, cq * WCOLS:(cq + 1) * WCOLS]).then_inc(raw_in[b % 2], 16)
                else:
                    c0 = {"aq": C_AQ, "mo": C_MO, "ga": C_GA, "gb": C_GB}[kind]
                    _, p, gg = BLOCKS[b]
                    for h in range(2):
                        for g in range(2):
                            at = c0 + (2 * p + h) * 256 + (2 * gg + g) * HD
                            sp.dma_start(r[:, :, (2 * g + h) * HD:(2 * g + h + 1) * HD],
                                         w_in_k[:, :, at:at + HD]).then_inc(raw_in[b % 2], 16)
            def small(dst, src):
                sp.dma_start(dst, src, allow_slow_non_contiguous=True).then_inc(const_in, 16)

            def load_x(i):
                if i >= 3:
                    sp.wait_ge(norm_xn, i - 2)
                sp.dma_start(xin[0:rows_of(i), i % 3, :], x_rows(i)).then_inc(x_in[i % 3], 16)

            load_x(0)
            sp.dma_start(gain_b[:, :], norm_attn[0].partition_broadcast(P)).then_inc(gain_in, 16)
            load_x(1)
            load_block(0)
            load_x(2)
            small(bias_i[:, :], b_gate[0, 0:MH].unsqueeze(1))
            small(bias_f[:, :], b_gate[0, MH:2 * MH].unsqueeze(1))
            small(sm_rows[:, :], state_m[0].rearrange("b h -> h b"))
            small(sink_b[:, :], sinks[0].partition_broadcast(P))
            small(sink_s[:, :], sinks[0].unsqueeze(1).broadcast_to([16, DSEQ]).unsqueeze(2))
            mn = mlstm_norm[0].rearrange("(p h g c) -> h p c g", p=2, h=2, g=GRP)
            for h in range(2):
                for p in range(2):
                    small(mnorm[64 * h:64 * h + 64, GRP * p:GRP * p + GRP], mn[h, p])
            load_x(3)
            load_block(1)
            for i in range(4, NT):
                load_x(i)
            for b in range(NSEQ):
                sp.dma_start(s_k[0, b, 0:WIN - DSEQ], cache_k[0, b, DSEQ:WIN]).then_inc(out_dma, 16)
                sp.dma_start(s_v[0, b, 0:WIN - DSEQ], cache_v[0, b, DSEQ:WIN]).then_inc(out_dma, 16)

            def store_gate_rows():
                sp.wait_ge(gate_fin, 1)
                sp.dma_start(gate_rows[0], row_x[:, :]).then_inc(rows_out, 16)
                sp.dma_start(gate_rows[1], row_t[:, :]).then_inc(rows_out, 16)
                sp.dma_start(ends_dram, ends[:, :]).then_inc(rows_out, 16)
                sp.dma_start(p_m[0].rearrange("b h -> h b"), m_out[:, NSEQ:NSEQ + 1],
                             allow_slow_non_contiguous=True).then_inc(out_dma, 16)
                sp.dma_start(s_m[0].rearrange("b h -> h b"), m_out[:, 0:NSEQ],
                             allow_slow_non_contiguous=True).then_inc(out_dma, 16)
                sp.wait_ge(rows_out, 48)
                sp.dma_start(dec[:, :, :].rearrange("p h e -> p (h e)"),
                             ends_dram.rearrange("h e -> (h e)").unsqueeze(0).broadcast_to([P, MH * 16]))\
                    .then_inc(dec_in, 16)

            def load_bc(s):
                p, i = divmod(s, S_PER)
                if s >= 2:
                    sp.wait_ge(ml_wa, s - 1)
                    sp.wait_ge(ml_qs, s - 1)
                for q in range(2):
                    sp.dma_start(bc[:, s % 2, 2 * q:2 * q + 2, 0:rows_of(i)],
                                 gate_rows[q, 2 * p:2 * p + 2, cols(i)].unsqueeze(0)
                                 .broadcast_to([P, 2, rows_of(i)])).then_inc(bc_in[s % 2], 16)

            def load_cin(n):
                p, hh, half = n // 4, n // 2 % 2, n % 2
                h = 2 * p + hh
                if n >= 2:
                    sp.wait_ge(cin_out, 32 * 4 * p if n % 4 < 2 else 32 * (n - 1))
                sp.dma_start(Cin[:, half, :, 0:DV],
                             state_C[0, 4 * half:4 * half + 4, h].rearrange("b k v -> k b v")).then_inc(cin_in[half], 16)
                sp.dma_start(Cin[:, half, :, DV:VA],
                             state_n[0, 4 * half:4 * half + 4, h].rearrange("b k -> k b").unsqueeze(2),
                             allow_slow_non_contiguous=True).then_inc(cin_in[half], 16)

            def store_cin(n):
                p, hh, half = n // 4, n // 2 % 2, n % 2
                h = 2 * p + hh
                sp.wait_ge(ml_sc, 4 * (n + 1))
                sp.dma_start(s_C[0, 4 * half:4 * half + 4, h].rearrange("b k v -> k b v"),
                             Cin[:, half, :, 0:DV]).then_inc(cin_out, 16)
                sp.dma_start(s_n[0, 4 * half:4 * half + 4, h].rearrange("b k -> k b").unsqueeze(2),
                             Cin[:, half, :, DV:VA], allow_slow_non_contiguous=True).then_inc(cin_out, 16)

            def mlstm(p):
                s0 = p * S_PER
                if p == 0:
                    sp.wait_ge(gate_nat, 1)
                load_cin(4 * p)
                load_cin(4 * p + 1)
                load_bc(s0)
                load_bc(s0 + 1)
                fill(FILL_ML[p][0])
                for i in range(2, NT):
                    fill(FILL_ML[p][2 * i - 3])
                    fill(FILL_ML[p][2 * i - 2])
                    load_bc(s0 + i)
                for x in range(2 * NT - 3, 2 * NT - 1):
                    fill(FILL_ML[p][x])
                sp.wait_ge(ml_c, (NT - 1) * (p + 1))
                sp.dma_start(p_C[0, 0, 2 * p:2 * p + 2].rearrange("h k v -> k h v"),
                             Cst[:, :, 0:DV]).then_inc(pc_out, 16)
                sp.dma_start(p_n[0, 0, 2 * p:2 * p + 2].rearrange("h k -> k h").unsqueeze(2),
                             Cst[:, :, DV:VA], allow_slow_non_contiguous=True).then_inc(pc_out, 16)
                fill(FILL_ML[p][2 * NT - 1])
                for n in range(4 * p, 4 * p + 2):
                    store_cin(n)
                    load_cin(n + 2)
                fill(FILL_ML[p][2 * NT])
                for n in range(4 * p + 2, 4 * p + 4):
                    store_cin(n)

            def fill(units):
                for b, u in units:
                    if u == 0:
                        load_block(b + 1)

            def prompt(fills):
                for units in fills:
                    fill(units)

            def store_mask():
                sp.wait_ge(mask_made, 1)
                sp.dma_start(mask_dram, smask[0:DSEQ, :]).then_inc(mask_io, 16)
                sp.wait_ge(mask_io, 16)
                for n in range(16):
                    sp.dma_start(smask[n * DSEQ:(n + 1) * DSEQ, :], mask_dram).then_inc(mask_io, 16)

            def sampled(fills):
                def load_keys(s):
                    if s >= 2:
                        sp.wait_ge(sk_t, s - 1)
                    sp.dma_start(kc[:, s % 2, :], cache_k[0, s].rearrange("w h d -> w (h d)")).then_inc(kc_in[s % 2], 16)

                def load_values(s):
                    if s >= 2:
                        sp.wait_ge(ss_v, s - 1)
                    sp.dma_start(vc[:, s % 2, :], cache_v[0, s].rearrange("w h d -> w (h d)")).then_inc(vc_in[s % 2], 16)

                sp.wait_ge(at_v, NB)
                sp.wait_ge(at_p1, HALF)
                load_keys(0)
                load_keys(1)
                load_values(0)
                fill(fills[0])
                for s in range(1, NSEQ):
                    fill(fills[2 * s - 1])
                    if s + 1 < NSEQ:
                        load_keys(s + 1)
                    fill(fills[2 * s])
                    load_values(s)
                fill(fills[2 * NSEQ - 1])
                fill(fills[2 * NSEQ])
                sp.wait_ge(ko_e, 2)
                sp.dma_start(p_k[0, 0].rearrange("t h d -> t (h d)"), kout[:, 0, :]).then_inc(out_dma, 16)
                sp.dma_start(p_v[0, 0].rearrange("t h d -> t (h d)"), avn[:, NT - 2, :]).then_inc(out_dma, 16)
                for s in range(NSEQ):
                    at = slice(s * DSEQ, (s + 1) * DSEQ)
                    sp.dma_start(s_k[0, s, WIN - DSEQ:].rearrange("t h d -> t (h d)"),
                                 kout[at, 1, :]).then_inc(out_dma, 16)
                    sp.dma_start(s_v[0, s, WIN - DSEQ:].rearrange("t h d -> t (h d)"),
                                 avn[at, NT - 1, :]).then_inc(out_dma, 16)

            fill(units_of(1, 2))
            store_gate_rows()
            fill(units_of(3, 3))
            mlstm(0)
            mlstm(1)
            store_mask()
            fill(units_of(*AQ_BLOCKS))
            prompt(FILL_P0)
            sampled(FILL_SS)
            prompt(FILL_P1)
            fill(units_of(*GB_BLOCKS))
            sp.wait_ge(out_dma, 16 * (2 * NSEQ + 2 + 2 + 2 * NSEQ))
            sp.dma_start(gain_b[:, :], norm_mlp[0].partition_broadcast(P)).then_inc(gain_in, 16)
            load_block(NPROJ + 1)
            sp.wait_ge(mg_lo, NT)
            for i in range(NT):
                sp.dma_start(x2[0:rows_of(i), i, :], x_rows(i)).then_inc(x2_in[i], 16)
            load_block(NPROJ + 2)
            load_block(NPROJ + 3)

            def up_dma(g, slot):
                sp.dma_start(raw[:, slot, 0:KT * WCOLS].rearrange("p (k c) -> p k c", k=KT),
                             w_up_k[:, :, bass.ds(g * WCOLS, WCOLS)]).then_inc(raw_in[slot], 16)

            def dn_dma(g):
                sp.dma_start(raw[:, 0, 0:2 * D].rearrange("p (k c) -> p k c", k=2),
                             w_dn_k[:, bass.ds(2 * g, 2), :]).then_inc(raw_in[0], 16)

            sp.wait_ge(gemm_v, 3 * NT)
            up_dma(0, 0)
            sp.wait_ge(gemm_v, OUT_UNITS)
            up_dma(1, 1)
            sp.wait_ge(gemm_a, PROJ_UNITS + UP_UNITS)
            dn_dma(0)
            with sp.Fori(2, NG) as g:
                sp.wait_ge(gemm_a, g * UP_UNITS + PROJ_UNITS)
                up_dma(g, 1)
                sp.wait_ge(gemm_v, g * DN_UNITS + (OUT_UNITS - DN_UNITS))
                dn_dma(g - 1)
            sp.wait_ge(norm_xn, 2 * NT)
            sp.dma_start(gain_b[:, :], norm_final.partition_broadcast(P)).then_inc(gain_in, 16)
            sp.wait_ge(gemm_a, PROJ_UNITS + UP_UNITS * NG)
            sp.dma_start(raw[:, 1, 0:2 * D].rearrange("p (k c) -> p k c", k=2),
                         w_dn_k[:, 2 * (NG - 1):2 * NG, :]).then_inc(raw_in[1], 16)
            for n, i in enumerate(DN_ORDER):
                sp.wait_ge(y_rdy, n + 1)
                sp.dma_start(y_rows(i), ybuf[0:rows_of(i), n % 2, :]).then_inc(y_out[n % 2], 16)
            sp.wait_ge(pc_out, 64)
            sp.wait_ge(cin_out, 32 * 8)
            sp.wait_ge(out_dma, 16 * (2 * NSEQ + 2 + 2 + 2 * NSEQ))
            sp.wait_ge(y_out[0], 16 * ((NT + 1) // 2))
            sp.wait_ge(y_out[1], 16 * (NT // 2))

        @block.tensor
        def _(pe):
            def tr(out, in_, rows):
                return nc.tensor.transpose(out, in_, ident[0:rows, 0:rows])

            def norm_transposes(t, src):
                i = t % NT
                rows = rows_of(i)
                pe.wait_ge(norm_xn, t + 1)
                for h in range(2):
                    n = 2 * t + h
                    if n >= 4:
                        pe.wait_ge(norm_lo, n - 3)
                    for k in range(4):
                        last = tr(bank[4 + n % 4][:, k * P:k * P + rows],
                                  src[0:rows, i % 2, (4 * h + k) * P:(4 * h + k + 1) * P], rows)
                    last.then_inc(norm_tp, 1)

            PASSES = ((w_hi, xT_hi), (w_hi, xT_lo), (w_lo, xT_hi))

            def proj_unit(b, u):
                n = FIRST_UNIT[b] + u
                if n >= RING:
                    pe.wait_ge(free_a, n - RING + 1)
                if u == 0:
                    pe.wait_ge(w_hi_done, b + 1)
                for step in range(3 * KT):
                    (w, x), k = PASSES[step // KT], step % KT
                    if u == 0 and step == 2 * KT:
                        pe.wait_ge(w_lo_done, b + 1)
                    if BLOCKS[b][0] in NATURAL:
                        rhs = w_view(w, b, k)
                        out = bank[n % RING][0:rows_of(u), 0:WCOLS + 8 if b == 0 else WCOLS]
                        lhsT = x[:, k, cols(u)]
                    else:
                        tile, (c0, cn) = u // 3, CHUNKS[u % 3]
                        lhsT = w_stat(w, b, k, tile)
                        rhs = x[:, k, c0:c0 + cn]
                        out = bank[n % RING][:, 0:cn]
                    last = nc.tensor.matmul(out, lhsT, rhs, start=(step == 0), stop=(step == 3 * KT - 1))
                last.then_inc(gemm_a, 1)

            def gate_transposes():
                pe.wait_ge(free_a, NT)
                def part(b, at, tiles, c):
                    for x, i in enumerate(tiles):
                        last = tr(bank[b][0:MH, at + x * P:at + x * P + rows_of(i)],
                                  gnat[0:rows_of(i), i, c:c + MH], rows_of(i))
                    return last
                pe.wait_ge(norm_lo, 2 * NT)
                part(4, 0, range(0, 4), 0).then_inc(gate_tp, 1)
                part(5, 0, range(4, 8), 0).then_inc(gate_tp, 1)
                part(6, 0, [8], 0)
                part(6, 64, [8], MH).then_inc(gate_tp, 1)
                part(7, 0, range(0, 4), MH).then_inc(gate_tp, 1)
                pe.wait_ge(gate_ev, 1)
                part(4, 0, range(4, 8), MH).then_inc(gate_tp, 1)

            def q4_transposes():
                pe.wait_ge(gate_exp, 3)
                pe.wait_ge(gate_ev, 6)
                for b, tiles in ((4, range(0, 4)), (5, range(4, 8)), (6, [8])):
                    for x, i in enumerate(tiles):
                        last = tr(bank[b][0:rows_of(i), x * P:x * P + P], q4[:, cols(i)], P)
                    last.then_inc(gate_q4, 1)

            def ml_scores(s):
                p, i = divmod(s, S_PER)
                n = rows_of(i)
                if i:
                    pe.wait_ge(ml_c, (NT - 1) * p + i)
                elif p:
                    pe.wait_ge(ml_sc, 2 * NSEQ)
                for hh in range(2):
                    last = tr(bank[4][0:n, hh * P:(hh + 1) * P], mk(p, hh, cols(i)), P)
                last.then_inc(ml_kt, 1)
                for hh in range(2):
                    last = nc.tensor.matmul(bank[5][0:n, hh * P:hh * P + n], mk(p, hh, cols(i)), mq(p, hh, cols(i)),
                                            start=True, stop=True)
                last.then_inc(ml_st, 1)

            def ml_step(s):
                p, i = divmod(s, S_PER)
                n = rows_of(i)
                pe.wait_ge(ml_sw, s + 1)
                pe.wait_ge(ml_qs, s + 1)
                if s >= 1:
                    pe.wait_ge(ml_h0, s)
                    pe.wait_ge(ml_h1, s)
                c = (NT - 1) * p + i
                if c:
                    pe.wait_ge(ml_c, c)
                for hh in range(2):
                    last = nc.tensor.matmul(bank[6 + hh][0:n, 0:VA], wgt[0:n, s % 2, hh, 0:n],
                                            vaug[p][0:n, i, hh, :], start=True, stop=(i == 0))
                    if i > 0:
                        last = nc.tensor.matmul(bank[6 + hh][0:n, 0:VA], qs[:, s % 2, hh, 0:n], Cst[:, hh, :],
                                                start=False, stop=True)
                last.then_inc(ml_n, 1)
                pe.wait_ge(ml_kw, s + 1)
                for hh in range(2):
                    last = nc.tensor.matmul(bank[4 + hh][:, 0:VA], kw[0:n, s % 2, hh, :], vaug[p][0:n, i, hh, :],
                                            start=True, stop=True)
                last.then_inc(ml_u, 1)

            def ml_sampled(p, hh):
                s, i = p * S_PER + NT - 1, NT - 1
                n = rows_of(i)
                if hh == 0:
                    pe.wait_ge(ml_sw, s + 1)
                    pe.wait_ge(ml_qs, s + 1)
                    pe.wait_ge(ml_h0, s)
                    pe.wait_ge(ml_h1, s)
                nc.tensor.matmul(bank[6 + hh][0:n, 0:VA], wgt[0:n, s % 2, hh, 0:n], vaug[p][0:n, i, hh, :],
                                 start=True, stop=False)
                for half in range(2):
                    pe.wait_ge(cin_in[half], 32 * (2 * p + hh + 1))
                    for b in range(4 * half, 4 * half + 4):
                        last = nc.tensor.matmul(bank[6 + hh][0:n, 0:VA], qz[:, hh, 64 * b:64 * b + 64],
                                                Cin[:, half, b % 4, :], start=False, stop=(b == NSEQ - 1))
                if hh == 1:
                    last.then_inc(ml_n, 1)
                pe.wait_ge(ml_kz, 2 * p + hh + 1)
                for b in range(NSEQ):
                    c = (2 * p + hh) * NSEQ + b
                    if b >= 2 or hh:
                        pe.wait_ge(ml_sc, c - 1)
                    elif b == 0:
                        pe.wait_ge(ml_kw, s + 1)
                    nc.tensor.matmul(bank[4 + b % 2][:, 0:VA], kwz[0:n, b, :], vaug[p][0:n, i, hh, :],
                                     start=True, stop=True).then_inc(ml_su, 1)

            def ml_transposes(s):
                i = s % S_PER
                n = rows_of(i)
                pe.wait_ge(ml_hn, s + 1)
                if s >= 1:
                    pe.wait_ge(ml_te, s)
                for g in range(GRP):
                    last = tr(bank[3][:, g * P:g * P + n],
                              hh_b[0:n, s % 2, g, :, :].rearrange("t h c -> t (h c)"), n)
                last.then_inc(ml_t, 1)

            def mlstm(p):
                pe.wait_ge(free_a, FIRST_UNIT[4 * p + 4])
                pe.wait_ge(gate_nat, 1)
                if p:
                    pe.wait_ge(ones, 1)
                s0 = p * S_PER
                ml_scores(s0)
                fill(FILL_ML[p][0])
                for i in range(NT):
                    s = s0 + i
                    if i < NT - 1:
                        ml_step(s)
                        fill(FILL_ML[p][2 * i + 1])
                    else:
                        ml_sampled(p, 0)
                        fill(FILL_ML[p][2 * i + 1])
                        ml_sampled(p, 1)
                    if i:
                        ml_transposes(s - 1)
                    if i < NT - 1:
                        ml_scores(s + 1)
                    fill(FILL_ML[p][2 * i + 2])
                ml_transposes(s0 + NT - 1)

            def at_scores(u):
                i, p, half = at_unit(u)
                kv = 2 * p + half
                lo = 0 if i else P
                if u >= 1:
                    pe.wait_ge(at_m, u)
                for g in range(GRP):
                    out = bank[3 + g // 2][:, (g % 2) * 256 + lo:(g % 2) * 256 + 256]
                    last = nc.tensor.matmul(out, aqT[:, p * GRP + g, cols(i)],
                                            akz[:, kv, (i - 1) * P + lo:(i + 1) * P], start=True, stop=True)
                last.then_inc(at_s, 1)

            def at_transposes(u):
                i, p, half = at_unit(u)
                pe.wait_ge(at_p, u + 1)
                if i and prev_count(u) > 1:
                    pe.wait_ge(at_p0, prev_count(u) - 1)
                if u >= 1:
                    pe.wait_ge(at_p1, u)
                for kb in range(2 if i else 1):
                    kb = kb if i else 1
                    for g in range(GRP):
                        last = tr(bank[5 + kb][:, g * P:(g + 1) * P], prob[:, u % 2, g, kb * P:(kb + 1) * P], P)
                last.then_inc(at_t, 1)

            def at_values(pair):
                i, p, _ = at_unit(2 * pair)
                if pair == NB:
                    pe.wait_ge(ss_o, NSEQ)
                elif pair:
                    pe.wait_ge(at_o, pair)
                for half in range(2):
                    u, kv = 2 * pair + half, 2 * p + half
                    for kb in range(2):
                        if kb:
                            pe.wait_ge(at_p1, u + 1)
                        elif i:
                            pe.wait_ge(at_p0, prev_count(u))
                        if kb or i:
                            last = nc.tensor.matmul(bank[7][64 * half:64 * half + 64, :],
                                                    avn[:, i - 1 + kb, kv * HD:(kv + 1) * HD], pT[:, half, kb, :],
                                                    start=(kb == 0 or i == 0), stop=(kb == 1))
                last.then_inc(at_v, 1)

            def ss_keys(b):
                pe.wait_ge(kc_in[b % 2], 16 * (b // 2 + 1))
                if b >= 1:
                    pe.wait_ge(sk_e, b)
                for p in range(2):
                    last = tr(bank[3][:, p * P:(p + 1) * P], kc[:, b % 2, p * P:(p + 1) * P], P)
                last.then_inc(sk_t, 1)

            def ss_scores(b):
                pe.wait_ge(sk_e, b + 1)
                pe.wait_ge(ss_q, 1)
                if b >= 1:
                    pe.wait_ge(ss_m, b)
                for kv in range(NKV):
                    p, half = divmod(kv, 2)
                    at = slice(64 * half, 64 * half + 64)
                    q = qsmp[at, p, b, :, :].rearrange("c g t -> c (g t)")
                    out = bank[4][32 * kv:32 * kv + 32, :]
                    nc.tensor.matmul(out[:, 0:P], q, kcT[at, b % 2, p, :], start=True, stop=True)
                    last = nc.tensor.matmul(out[:, P:192], q, akz[at, kv, SEQ:T], start=True, stop=True)
                last.then_inc(ss_s, 1)

            def ss_transposes(b):
                pe.wait_ge(ss_p, b + 1)
                if b >= 1:
                    pe.wait_ge(ss_te, b)
                tr(bank[5][:, 0:P], sprob[:, b % 2, 0:P], P)
                tr(bank[5][0:64, P:2 * P], sprob[:, b % 2, P:192], P).then_inc(ss_t, 1)

            def ss_values(b):
                pe.wait_ge(ss_te, b + 1)
                pe.wait_ge(vc_in[b % 2], 16 * (b // 2 + 1))
                if b >= 1:
                    pe.wait_ge(ss_o2, b)
                nc.tensor.matmul(bank[6][:, 0:256], spT[:, 0, :], vc[:, b % 2, :], start=True, stop=False)
                nc.tensor.matmul(bank[6][:, 0:256], spT[0:64, 1, :], avn[0:64, NT - 1, :], start=False,
                                 stop=True).then_inc(ss_v, 1)

            def ss_outputs(b):
                pe.wait_ge(ss_o2, b + 1)
                if b >= 1:
                    pe.wait_ge(ss_o, b)
                tr(bank[7][:, 0:P], o2[:, :], P).then_inc(ss_ot, 1)

            def prompt(p, fills):
                pe.wait_ge(free_a, FIRST_UNIT[15 + 2 * p])
                if p:
                    pe.wait_ge(ss_te, NSEQ)
                u0 = p * HALF
                at_scores(u0)
                fill(fills[0])
                for n in range(HALF):
                    u = u0 + n
                    if n + 1 < HALF:
                        at_scores(u + 1)
                        at_transposes(u)
                        fill(fills[n + 1])
                    else:
                        fill(fills[n + 1])
                        at_transposes(u)
                    if n % 2:
                        at_values(u // 2)

            def sampled(fills):
                for x, i in enumerate((NT - 2, NT - 1)):
                    for kv in range(NKV):
                        p, half = divmod(kv, 2)
                        last = nc.tensor.matmul(bank[5 + x][0:rows_of(i), p * P:(p + 1) * P], akz[:, kv, cols(i)],
                                                ident[:, :], start=(half == 0), stop=(half == 1))
                    last.then_inc(ko_t, 1)
                fill(fills[0])
                pe.wait_ge(free_a, FIRST_UNIT[17])
                pe.wait_ge(at_o, NB)
                ss_keys(0)
                ss_scores(0)
                pe.wait_ge(ko_e, 2)
                for b in range(NSEQ):
                    if b + 1 < NSEQ:
                        ss_keys(b + 1)
                    fill(fills[2 * b + 1])
                    if b >= 1:
                        ss_outputs(b - 1)
                    ss_transposes(b)
                    if b + 1 < NSEQ:
                        ss_scores(b + 1)
                    fill(fills[2 * b + 2])
                    ss_values(b)
                ss_outputs(NSEQ - 1)

            def attention():
                pe.wait_ge(ml_te, 2 * S_PER)
                pe.wait_ge(ml_sc, 4 * NSEQ)
                pe.wait_ge(consts, 4)
                prompt(0, FILL_P0)
                sampled(FILL_SS)
                prompt(1, FILL_P1)

            def fill(units):
                for b, u in units:
                    proj_unit(b, u)

            pe.wait_ge(consts, 1)
            norm_transposes(0, xn)
            norm_transposes(1, xn)
            for u in range(NT):
                pe.wait_ge(norm_lo, 2 * (u + 1))
                proj_unit(0, u)
                if u + 2 < NT:
                    norm_transposes(u + 2, xn)
            gate_transposes()
            fill(units_of(1, 2))
            q4_transposes()
            fill(units_of(3, 3))
            mlstm(0)
            mlstm(1)
            fill(units_of(*AQ_BLOCKS))
            attention()
            fill(units_of(*GB_BLOCKS))

            for cq in range(4):
                b = NPROJ + cq
                pe.wait_ge(w_lo_done, b + 1)
                for i in range(NT):
                    m = NT * cq + i
                    if cq == 0:
                        pe.wait_ge(mg_lo, i + 1)
                    if m >= out_ring(m):
                        pe.wait_ge(free_v, m - out_ring(m) + 1)
                    step = 0
                    for k in range(KT):
                        for w, x in PASSES:
                            last = nc.tensor.matmul(bank[m % out_ring(m)][0:rows_of(i), 0:WCOLS], x[:, k, cols(i)],
                                                    w_view(w, b, k), start=(step == 0), stop=(step == 3 * KT - 1))
                            step += 1
                    last.then_inc(gemm_v, 1)
                    if cq == 3 and i >= 2:
                        norm_transposes(NT + i - 2, ybuf)
            def up_unit(g, u, slot, hslot):
                tile, (c0, cn) = u // 3, CHUNKS[u % 3]
                n = hslot * UP_UNITS + u
                pe.wait_ge(free_a, g * UP_UNITS + (PROJ_UNITS + u - 3))
                step = 0
                for k in range(KT):
                    for w, x in PASSES:
                        last = nc.tensor.matmul(
                            bank[n % 4][:, 0:cn], w[:, slot, k * WCOLS + tile * P:k * WCOLS + (tile + 1) * P],
                            x[:, k, c0:c0 + cn], start=(step == 0), stop=(step == 3 * KT - 1))
                        step += 1
                last.then_inc(gemm_a, 1)

            def up(g, wait_b, slot, hslot):
                pe.wait_ge(w_lo_done, wait_b)
                for u in range(UP_UNITS):
                    up_unit(g, u, slot, hslot)

            def down(g, wait_b, slot, hslot):
                pe.wait_ge(w_lo_done, wait_b)
                pe.wait_ge(lo_done, g * UP_UNITS + UP_UNITS)
                for n, i in enumerate(DN_ORDER):
                    if i == NT - 1:
                        passes, at = ((w_hi, hid_hi), (w_lo, hid_hi)), slice(SEQ, SEQ + P)
                    else:
                        passes, at = ((w_hi, hid_hi), (w_hi, hid_lo), (w_lo, hid_hi)), cols(i)
                    for half in range(2):
                        d = hslot * DN_UNITS + 2 * n + half
                        pe.wait_ge(free_v, g * DN_UNITS + (OUT_UNITS + 2 * n + half - 3))
                        step = 0
                        for k in range(2):
                            for w, x in passes:
                                last = nc.tensor.matmul(
                                    bank[4 + d % 4][:, :], x[:, hslot, k, at],
                                    w[:, slot, k * D + half * 512:k * D + half * 512 + 512],
                                    start=(step == 0), stop=(step == 2 * len(passes) - 1))
                                step += 1
                        last.then_inc(gemm_v, 1)
                    if n == 1 and isinstance(g, int) and g == NG - 1:
                        pe.wait_ge(free_v, g * DN_UNITS + OUT_UNITS + 2)
                        for half in range(2):
                            nc.tensor.matmul(bank[half][0:NS, :], ident[:, NS:P],
                                             x2[:, NT - 1, half * 512:half * 512 + 512],
                                             start=True, stop=True).then_inc(folded, 1)

            pe.wait_ge(w_lo_done, B_MLP + 1)
            pe.wait_ge(norm_lo, 2 * (NT + 3))
            up_unit(0, 0, 0, 0)
            norm_transposes(2 * NT - 2, ybuf)
            pe.wait_ge(norm_lo, 2 * (NT + 6))
            up_unit(0, 1, 0, 0)
            norm_transposes(2 * NT - 1, ybuf)
            pe.wait_ge(norm_lo, 4 * NT)
            for u in range(2, UP_UNITS):
                up_unit(0, u, 0, 0)
            with pe.Fori(0, NG // 2 - 1) as it:
                for x in range(2):
                    up(it * 2 + (1 + x), it * 4 + (B_MLP + 2 + 2 * x), 1, (1 + x) % 2)
                    down(it * 2 + x, it * 4 + (B_MLP + 3 + 2 * x), 0, x)
            up(NG - 1, B_MLP + 2 * NG - 2, 1, 1)
            down(NG - 2, B_MLP + 2 * NG - 1, 0, 0)
            down(NG - 1, B_MLP + 2 * NG, 1, 1)

        @block.scalar
        def _(act):
            chain = [0]

            def link(ins):
                chain[0] += 1
                ins.then_inc(act_chain, 1)
                act.wait_ge(act_chain, chain[0])

            def split(b, half=None):
                act.wait_ge(raw_in[b % 2], RAW_AT[b])
                at = part_cols(b, half)
                nc.scalar.activation(w_hi[:, b % 2, at], raw[:, b % 2, at], ACT.Copy)\
                    .then_inc(w_hi_half if half == 0 else w_hi_done, 1)

            def square(t, src, to):
                rows = rows_of(tile_of(t))
                if t:
                    act.wait_ge(norm_sq, t)
                ins = nc.scalar.activation(to[0:rows, :], src, ACT.Square,
                                           accum_out=stat[0:rows, t // NT, t % NT:t % NT + 1])
                ins.then_inc(norm_sq, 1)

            def round_x(t):
                i = t % NT
                for h in range(2):
                    n = 2 * t + h
                    act.wait_ge(norm_tp, n + 1)
                    if t >= NT and h == 0:
                        act.wait_ge(gemm_v, 3 * NT + i + 1)
                    nc.scalar.activation(xT_hi[:, 4 * h:4 * h + 4, cols(i)], half_view(4 + n % 4, rows_of(i)),
                                         ACT.Copy).then_inc(norm_hi, 1)

            def read_unit(b, u):
                kind = BLOCKS[b][0]
                n = FIRST_UNIT[b] + u
                src = bank[n % RING]
                act.wait_ge(gemm_a, n + 1)
                if kind == "v":
                    r = rows_of(u)
                    off = 8 if b == 0 else 0
                    if b == 0:
                        nc.scalar.activation(gnat[0:r, u, :], src[0:r, 0:8], ACT.Copy)
                    if b == 4 and u == 0:
                        act.wait_ge(gate_nat, 1)
                        act.wait_ge(rows_out, 48)
                    dst = vaug[BLOCKS[b][1] // 2][0:r, u, BLOCKS[b][1] % 2, 0:DV]
                    nc.scalar.activation(dst, src[0:r, off:off + DV], ACT.Copy).then_inc(free_a, 1)
                elif kind == "av":
                    r = rows_of(u)
                    if u == 0:
                        act.wait_ge(ml_su, 2 * NSEQ)
                    nc.scalar.activation(avn[0:r, u, :], src[0:r, 0:WCOLS], ACT.Copy).then_inc(free_a, 1)
                elif kind == "ak":
                    tile, (c0, cn) = u // 3, CHUNKS[u % 3]
                    if u == 0:
                        act.wait_ge(cin_out, 32 * 8)
                        act.wait_ge(pc_out, 64)
                        act.wait_ge(ml_t, 2 * S_PER)
                    for half in range(2):
                        at = slice(64 * half, 64 * half + 64)
                        ins = nc.scalar.activation(akz[at, 2 * tile + half, c0:c0 + cn], src[at, 0:cn], ACT.Copy)
                    ins.then_inc(free_a, 1)
                elif kind in ("mk", "mq", "aq"):
                    tile, (c0, cn) = u // 3, CHUNKS[u % 3]
                    if kind == "aq":
                        j = BLOCKS[b][1] * GRP + 2 * BLOCKS[b][2] + tile
                        dst = aqT[:, j, c0:c0 + cn]
                    else:
                        dst = (mk if kind == "mk" else mq)(BLOCKS[b][1], tile, slice(c0, c0 + cn))
                    nc.scalar.activation(dst, src[:, 0:cn], ACT.Copy,
                                         scale=QK_SCALE if kind == "mq" else 1.0).then_inc(free_a, 1)
                else:
                    c0, cn = CHUNKS[u % 3]
                    m = GATES[b, u]
                    if m >= 2:
                        act.wait_ge(sg_use, m - 1)
                    nc.scalar.activation(sig[:, m % 2, 0:cn], src[:, 0:cn], ACT.Tanh, scale=0.5).then_inc(free_a, 1)

            def gate_rows_act():
                act.wait_ge(const_in, 16 * 9)
                def row(dst, at, n, b, c, bias, wait):
                    act.wait_ge(gate_tp, wait)
                    return nc.scalar.activation(dst[:, at:at + n], bank[b][0:MH, c:c + n], ACT.Identity,
                                                bias=bias[:, :])
                row(row_i, 0, 512, 4, 0, bias_i, 1).then_inc(gate_ev, 1)
                row(row_i, 512, 512, 5, 0, bias_i, 2).then_inc(gate_ev, 1)
                row(row_i, 1024, 64, 6, 0, bias_i, 3).then_inc(gate_ev, 1)
                row(row_f, 1024, 64, 6, 64, bias_f, 3).then_inc(gate_ev, 1)
                row(row_f, 0, 512, 7, 0, bias_f, 4).then_inc(gate_ev, 1)
                row(row_f, 512, 512, 4, 0, bias_f, 5).then_inc(gate_ev, 1)
                act.wait_ge(gate_ev, 6)
                link(nc.scalar.activation(row_t[:, :], row_f[:, :], ACT.Abs))
                link(nc.scalar.activation(row_t[:, :], row_t[:, :], ACT.Exp, scale=-1.0))
                nc.scalar.activation(row_t[:, :], row_t[:, :], ACT.Ln, bias=1.0).then_inc(gate_ln, 1)

            def gate_exps():
                act.wait_ge(gate_arg, 1)
                nc.scalar.activation(row_t[:, :], row_t[:, :], ACT.Exp).then_inc(gate_exp, 1)
                nc.scalar.activation(q4[64:64 + MH, :], row_m[:, :], ACT.Exp, scale=-1.0).then_inc(gate_exp, 1)
                nc.scalar.activation(q4[96:96 + MH, :], row_i[:, :], ACT.Exp).then_inc(gate_exp, 1)

            def ml_weights(s):
                n = rows_of(s % S_PER)
                act.wait_ge(ml_wa, s + 1)
                nc.scalar.activation(wgt[0:n, s % 2, :, 0:n], wgt[0:n, s % 2, :, 0:n], ACT.Exp).then_inc(ml_we, 1)

            def ml_keys(s):
                p, i = divmod(s, S_PER)
                n = rows_of(i)
                if s == 0:
                    act.wait_ge(gate_nat, 1)
                act.wait_ge(ml_kt, s + 1)
                if s == NT + 1:
                    act.wait_ge(ml_kz, 2)
                elif s >= 2:
                    act.wait_ge(ml_u, s - 1 - s // NT if s != NT else NT - 1)
                for hh in range(2):
                    ins = nc.scalar.activation(kw[0:n, s % 2, hh, :], bank[4][0:n, hh * P:(hh + 1) * P], ACT.Copy,
                                               scale=nat[0:n, i, 3, 2 * p + hh:2 * p + hh + 1])
                ins.then_inc(ml_kw, 1)

            def ml_second(s):
                p, i = divmod(s, S_PER)
                n = rows_of(i)
                act.wait_ge(ml_n, s + 1)
                for hh in range(2):
                    ins = nc.scalar.activation(small[0:n, s % 2, hh:hh + 1], bank[6 + hh][0:n, DV:VA], ACT.Abs)
                ins.then_inc(ml_ab, 1)
                act.wait_ge(ml_rc, s + 1)
                if s >= 2:
                    act.wait_ge(ml_t, s - 1)
                nc.scalar.activation(hh_b[0:n, s % 2, :, 0, :], by_group(bank[6][0:n, 0:DV]), ACT.Copy,
                                     scale=small[0:n, s % 2, 2:3]).then_inc(ml_h0, 1)
                for hh in range(2):
                    act.wait_ge((ml_h0, ml_h1)[hh], s + 1)
                    if s or hh:
                        act.wait_ge(ml_ss, 2 * s + hh)
                    ins = nc.scalar.activation(by_group(hjunk[0:n, :]), hh_b[0:n, s % 2, :, hh, :], ACT.Square,
                                               accum_out=small[0:n, s % 2, 4 + hh:5 + hh])
                    ins.then_inc(ml_ss, 1)

            def ml_third(s):
                p, i = divmod(s, S_PER)
                n = rows_of(i)
                act.wait_ge(ml_t, s + 1)
                nc.scalar.activation(hT[:, p * GRP:(p + 1) * GRP, cols(i)], half_view(3, n), ACT.Copy)\
                    .then_inc(ml_te, 1)

            def fill(units):
                for b, u in units:
                    read_unit(b, u)
                    if u in (SPLIT_AT, SPLIT_AT + 1):
                        split(b + 1, u - SPLIT_AT)

            def mlstm_act(p):
                s0 = p * S_PER
                ml_weights(s0)
                ml_keys(s0)
                fill(FILL_ML[p][0])
                for i in range(NT):
                    s = s0 + i
                    if i < NT - 1:
                        ml_weights(s + 1)
                        ml_second(s)
                        fill(FILL_ML[p][2 * i + 1])
                    else:
                        fill(FILL_ML[p][2 * i + 1])
                        ml_second(s)
                    if i:
                        ml_third(s - 1)
                    if i < NT - 1:
                        ml_keys(s + 1)
                    fill(FILL_ML[p][2 * i + 2])
                ml_third(s0 + NT - 1)

            def at_exps(u):
                i = at_unit(u)[0]
                lo = 0 if i else P
                act.wait_ge(at_m, u + 1)
                nc.scalar.activation(ast[:, u % 2, 3, :], ast[:, u % 2, 3, :], ACT.Exp)
                for g in range(GRP):
                    v = prob[:, u % 2, g, lo:]
                    ins = nc.scalar.activation(v, v, ACT.Exp, bias=ast[:, u % 2, 2, g:g + 1], scale=ATT_SCALE,
                                               accum_out=ast[:, u % 2, 4, g:g + 1])
                ins.then_inc(at_e, 1)

            def at_prev(u):
                if at_unit(u)[0] == 0:
                    return
                act.wait_ge(at_t, u + 1)
                act.wait_ge(at_v, u // 2)
                nc.scalar.activation(pT[:, u % 2, 0, :], bank[5][:, :], ACT.Copy).then_inc(at_p0, 1)

            def at_out(pair):
                i, p, _ = at_unit(2 * pair)
                act.wait_ge(at_v, pair + 1)
                nc.scalar.activation(aqT[:, p * GRP:(p + 1) * GRP, cols(i)], half_view(7, P), ACT.Copy).then_inc(at_o, 1)

            def ss_keys(b):
                act.wait_ge(sk_t, b + 1)
                if b >= 2:
                    act.wait_ge(ss_s, b - 1)
                nc.scalar.activation(kcT[:, b % 2, :, :], bank[3][:, 0:256].rearrange("c (p w) -> c p w", p=2),
                                     ACT.Copy).then_inc(sk_e, 1)

            def ss_exps(b):
                act.wait_ge(ss_m, b + 1)
                nc.scalar.activation(sst[:, b % 2, 3:4], sst[:, b % 2, 3:4], ACT.Exp)
                nc.scalar.activation(sprob[:, b % 2, :], sprob[:, b % 2, :], ACT.Exp, bias=sst[:, b % 2, 2:3],
                                     scale=ATT_SCALE, accum_out=sst[:, b % 2, 4:5]).then_inc(ss_e, 1)

            def ss_pT(b):
                act.wait_ge(ss_t, b + 1)
                if b >= 1:
                    act.wait_ge(ss_v, b)
                nc.scalar.activation(spT[:, 0, :], bank[5][:, 0:P], ACT.Copy)
                nc.scalar.activation(spT[0:64, 1, :], bank[5][0:64, P:2 * P], ACT.Copy).then_inc(ss_te, 1)

            def ss_out(b):
                act.wait_ge(ss_ot, b + 1)
                for half in range(2):
                    at = slice(64 * half, 64 * half + 64)
                    src = bank[7][at, 0:P].rearrange("c (p h r) -> c p h r", p=2, h=2)[:, :, half, :]
                    dst = aqT[at, :, SEQ + b * DSEQ:SEQ + (b + 1) * DSEQ]
                    for p in range(2):
                        ins = nc.scalar.activation(dst[:, p * GRP:(p + 1) * GRP, :],
                                                   src[:, p, :].rearrange("c (g t) -> c g t", g=GRP), ACT.Copy)
                ins.then_inc(ss_o, 1)

            def prompt_act(p, fills):
                u0 = p * HALF
                at_exps(u0)
                fill(fills[0])
                for n in range(HALF):
                    u = u0 + n
                    if n + 1 < HALF:
                        at_prev(u)
                        at_exps(u + 1)
                        fill(fills[n + 1])
                    else:
                        fill(fills[n + 1])
                        at_prev(u)
                    if n % 2:
                        at_out(u // 2)

            def sampled_act(fills):
                act.wait_ge(ko_t, 2)
                nc.scalar.activation(kout[:, 0, :], bank[5][:, 0:256], ACT.Copy).then_inc(ko_e, 1)
                nc.scalar.activation(kout[0:64, 1, :], bank[6][0:64, 0:256], ACT.Copy).then_inc(ko_e, 1)
                fill(fills[0])
                ss_keys(0)
                ss_exps(0)
                for b in range(NSEQ):
                    if b + 1 < NSEQ:
                        ss_keys(b + 1)
                    fill(fills[2 * b + 1])
                    if b >= 1:
                        ss_out(b - 1)
                    ss_pT(b)
                    if b + 1 < NSEQ:
                        ss_exps(b + 1)
                    fill(fills[2 * b + 2])
                ss_out(NSEQ - 1)

            def square_x(i):
                act.wait_ge(x_in[i % 3], 16 * (i // 3 + 1))
                square(i, xin[0:rows_of(i), i % 3, :], junk)

            square_x(0)
            square_x(1)
            round_x(0)
            split(0)
            square_x(2)
            round_x(1)
            for u in range(NT):
                if u + 3 < NT:
                    square_x(u + 3)
                if u + 2 < NT:
                    round_x(u + 2)
                if u == 7:
                    split(1)
                read_unit(0, u)
            gate_rows_act()
            fill(units_of(1, 1))
            gate_exps()
            fill(units_of(2, 3))
            mlstm_act(0)
            mlstm_act(1)
            fill(units_of(*AQ_BLOCKS))
            prompt_act(0, FILL_P0)
            sampled_act(FILL_SS)
            prompt_act(1, FILL_P1)
            *before, last = units_of(*GB_BLOCKS)
            fill(before)

            act.wait_ge(gemm_a, PROJ_UNITS)
            for i in range(NT):
                if i == 1:
                    fill([last])
                if i % 3 == 0:
                    act.wait_ge(sg_use, len(GATES) - 2 + i // 3)
                nc.scalar.activation(xT_hi[:, :, cols(i)], hT[:, :, cols(i)], ACT.Copy).then_inc(mg_hi, 1)
            split(NPROJ + 1)
            split(NPROJ + 2)
            split(NPROJ + 3)

            def split_mlp(raw_n, slot):
                act.wait_ge(raw_in[slot], raw_n)
                n = KT * WCOLS
                nc.scalar.activation(w_hi[:, slot, 0:n], raw[:, slot, 0:n], ACT.Copy).then_inc(w_hi_done, 1)

            for i in range(NT):
                t = NT + i
                act.wait_ge(free_v, 3 * NT + i + 1)
                square(t, x2[0:rows_of(i), i, :], junk2)
                if i == 2:
                    split_mlp(RAW_ALL[0] + 16, 0)
                if i >= 1:
                    round_x(t - 1)
            round_x(2 * NT - 1)

            def read_up(g, hslot, raw_n, slot):
                for u in range(UP_UNITS):
                    tile, (c0, cn) = u // 3, CHUNKS[u % 3]
                    n = hslot * UP_UNITS + u
                    act.wait_ge(gemm_a, g * UP_UNITS + (PROJ_UNITS + u + 1))
                    if u >= 2:
                        act.wait_ge(lo_done, g * UP_UNITS + (u - 1))
                    elif not isinstance(g, int) or g:
                        act.wait_ge(lo_done, g * UP_UNITS + (u - 1))
                    nc.scalar.activation(relu[:, u % 2, 0:cn], bank[n % 4][:, 0:cn], ACT.Relu).then_inc(free_a, 1)
                    act.wait_ge(free_a, g * UP_UNITS + (PROJ_UNITS + u + 1))
                    nc.scalar.activation(hid_hi[:, hslot, tile, c0:c0 + cn], relu[:, u % 2, 0:cn],
                                         ACT.Square).then_inc(hi_done, 1)
                    if u == 1:
                        split_mlp(raw_n, slot)

            read_up(0, 0, RAW_ALL[1] + 16, 1)
            with act.Fori(0, NG // 2 - 1) as it:
                for x in range(2):
                    g = it * 2 + (1 + x)
                    read_up(g, (1 + x) % 2, it * 32 + (RAW_ALL[0] + 32 + 16 * x), 0)
                    split_mlp(it * 32 + (RAW_ALL[1] + 32 + 16 * x), 1)
            g = NG - 1
            read_up(g, 1, RAW_ALL[0] + 16 * NG, 0)
            split_mlp(RAW_ALL[1] + 16 * NG, 1)
            for n, i in enumerate(DN_ORDER):
                if i == NT - 1:
                    act.wait_ge(folded_in, 2)
                else:
                    act.wait_ge(free_v, OUT_UNITS + DN_UNITS * g + 2 * n + 2)
                square(2 * NT + n, x2[0:rows_of(i), i, :], junk2)

        @block.vector
        def _(dve):
            chain = [0]

            def link(ins):
                chain[0] += 1
                ins.then_inc(dve_chain, 1)
                dve.wait_ge(dve_chain, chain[0])

            def split(b, half=None):
                if half == 0:
                    dve.wait_ge(w_hi_half, b - 1)
                else:
                    dve.wait_ge(w_hi_done, b + 1)
                at = part_cols(b, half)
                ins = nc.vector.tensor_tensor(w_lo[:, b % 2, at], raw[:, b % 2, at], w_hi[:, b % 2, at].bitcast(F32),
                                              ALU.subtract)
                if half != 0:
                    ins.then_inc(w_lo_done, 1)

            def normalise(t, src, dst, wait_slot):
                i = t % NT
                rows = rows_of(tile_of(t))
                dve.wait_ge(norm_rs, t + 1)
                wait_slot()
                return nc.vector.scalar_tensor_tensor(dst[0:rows, i % 2, :], src, rstd[0:rows, t // NT, i:i + 1],
                                                      gain_b[0:rows, :], ALU.mult, ALU.mult)

            def norm_tile(t, src, dst):
                def slot():
                    if t % NT >= 2:
                        dve.wait_ge(norm_tp, 2 * (t - 1))
                normalise(t, src, dst, slot).then_inc(norm_xn, 1)

            def rest_x(t):
                i = t % NT
                for h in range(2):
                    n = 2 * t + h
                    dve.wait_ge(norm_hi, n + 1)
                    out = xT_lo[:, 4 * h:4 * h + 4, cols(i)]
                    nc.vector.tensor_tensor(out, half_view(4 + n % 4, rows_of(i)),
                                            xT_hi[:, 4 * h:4 * h + 4, cols(i)].bitcast(F32),
                                            ALU.subtract).then_inc(norm_lo, 1)

            def gate_scans():
                dve.wait_ge(gate_ln, 1)
                dve.wait_ge(consts, 3)
                link(nc.vector.scalar_tensor_tensor(row_f[:, :], row_f[:, :], 0.0, row_t[:, :], ALU.min, ALU.subtract))
                nc.vector.tensor_tensor_scan(row_b[:, :], row_r[:, :], row_f[:, :], 0.0, ALU.mult, ALU.add)
                nc.vector.tensor_tensor_scan(row_m[:, 0:SEQ], row_f[:, 0:SEQ], row_i[:, 0:SEQ], 0.0, ALU.add, ALU.max)
                for b in range(NSEQ):
                    at = slice(SEQ + b * DSEQ, SEQ + (b + 1) * DSEQ)
                    ins = nc.vector.tensor_tensor_scan(row_m[:, at], row_f[:, at], row_i[:, at], sm_rows[:, b:b + 1],
                                                       ALU.add, ALU.max)
                link(ins)
                nc.vector.tensor_tensor(q4[0:MH, :], row_i[:, :], row_b[:, :], ALU.subtract)
                link(nc.vector.tensor_tensor(row_x[:, :], row_b[:, :], row_m[:, :], ALU.subtract))

                def runs(t, a, b, n):
                    return t[0:MH, a:b].rearrange("h (c t) -> h c t", t=n)

                def spread(v, c, n):
                    return v.unsqueeze(2).broadcast_to([MH, c, n])

                nc.vector.tensor_copy(row_t[:, 0:P], row_x[:, 0:P])
                nc.vector.tensor_tensor(runs(row_t, P, SEQ, P), runs(row_x, P, SEQ, P),
                                        spread(row_m[:, P - 1:SEQ - P:P], SEQ // P - 1, P), ALU.add)
                nc.vector.tensor_tensor(runs(row_t, SEQ, T, DSEQ), runs(row_x, SEQ, T, DSEQ),
                                        spread(sm_rows[:, :], NSEQ, DSEQ), ALU.add)
                nc.vector.tensor_tensor(runs(row_i, 0, SEQ, P), runs(q4, 0, SEQ, P),
                                        spread(row_x[:, P - 1:SEQ:P], SEQ // P, P), ALU.add)
                nc.vector.tensor_tensor(runs(row_i, SEQ, T, DSEQ), runs(q4, SEQ, T, DSEQ),
                                        spread(row_x[:, SEQ + DSEQ - 1:T:DSEQ], NSEQ, DSEQ), ALU.add)\
                    .then_inc(gate_arg, 1)

            def gate_ends():
                dve.wait_ge(gate_exp, 1)
                nc.vector.tensor_copy(ends[:, 0:8], row_t[:, P - 1:SEQ:P])
                nc.vector.tensor_copy(ends[:, 8:16], row_t[:, SEQ + DSEQ - 1:T:DSEQ])
                nc.vector.tensor_copy(m_out[:, 0:NSEQ], row_m[:, SEQ + DSEQ - 1:T:DSEQ])
                nc.vector.tensor_copy(m_out[:, NSEQ:NSEQ + 1], row_m[:, SEQ - 1:SEQ]).then_inc(gate_fin, 1)

            def gate_columns():
                dve.wait_ge(gate_q4, 3)
                for b, i0, k, r in ((4, 0, 4, P), (5, 4, 4, P), (6, 8, 1, 64)):
                    for q in range(4):
                        if q != 1:
                            src = bank[b][0:r, 0:k * P].rearrange("t (i q h) -> t i q h", q=4, h=32)[:, :, q, 0:MH]
                            ins = nc.vector.tensor_copy(nat[0:r, i0:i0 + k, q, :], src)
                ins.then_inc(gate_nat, 1)

            def ml_exponents(s):
                p, i = divmod(s, S_PER)
                n = rows_of(i)
                dve.wait_ge(bc_in[s % 2], 32 * (s // 2 + 1))
                if s >= 2:
                    dve.wait_ge(ml_n, s - 1)
                if s == 0:
                    dve.wait_ge(gate_nat, 1)
                    dve.wait_ge(consts, 3)
                mask = causal if n == P else causal8
                for hh in range(2):
                    ins = nc.vector.scalar_tensor_tensor(wgt[0:n, s % 2, hh, 0:n], bc[0:n, s % 2, hh, 0:n],
                                                         nat[0:n, i, 0, 2 * p + hh:2 * p + hh + 1], mask[0:n, 0:n],
                                                         ALU.add, ALU.min)
                ins.then_inc(ml_wa, 1)

            def ml_weigh(s):
                n = rows_of(s % S_PER)
                dve.wait_ge(ml_st, s + 1)
                dve.wait_ge(ml_we, s + 1)
                w = wgt[0:n, s % 2, :, 0:n]
                nc.vector.tensor_tensor(w, bank[5][0:n, 0:256].rearrange("s (h t) -> s h t", h=2)[:, :, 0:n], w,
                                        ALU.mult).then_inc(ml_sw, 1)

            def ml_norm(s):
                n = rows_of(s % S_PER)
                dve.wait_ge(ml_rs, s + 1)
                for hh in range(2):
                    v = hh_b[0:n, s % 2, :, hh, :]
                    ins = nc.vector.tensor_scalar(v, v, small[0:n, s % 2, 6 + hh:7 + hh], None, ALU.mult)
                ins.then_inc(ml_hn, 1)

            def sampled_states(p, hh):
                for b in range(NSEQ):
                    dve.wait_ge(ml_su, (2 * p + hh) * NSEQ + b + 1)
                    v = Cin[:, b // 4, b % 4, :]
                    nc.vector.scalar_tensor_tensor(v, v, dec[:, 2 * p + hh, 8 + b:9 + b], bank[4 + b % 2][:, 0:VA],
                                                   ALU.mult, ALU.add).then_inc(ml_sc, 1)

            def ml_second(s):
                p, i = divmod(s, S_PER)
                n = rows_of(i)
                dve.wait_ge(ml_ab, s + 1)
                link(nc.vector.tensor_tensor(small[0:n, s % 2, 2:4], small[0:n, s % 2, 0:2],
                                             nat[0:n, i, 2, 2 * p:2 * p + 2], ALU.max))
                ins = nc.vector.reciprocal(small[0:n, s % 2, 2:4], small[0:n, s % 2, 2:4])
                ins.then_inc(ml_rc, 1)
                dve.wait_ge(ml_rc, s + 1)
                nc.vector.tensor_scalar(hh_b[0:n, s % 2, :, 1, :], by_group(bank[7][0:n, 0:DV]), small[0:n, s % 2, 3:4], None,
                                        ALU.mult).then_inc(ml_h1, 1)
                if i < NT - 1:
                    c = (NT - 1) * p + i
                    dve.wait_ge(ml_u, c + 1)
                    if i == 0:
                        dve.wait_ge(dec_in, 16)
                        dve.wait_ge(ml_cl, p + 1)
                    else:
                        dve.wait_ge(ml_c, c)
                    for hh in range(2):
                        ins = nc.vector.scalar_tensor_tensor(Cst[:, hh, :], Cst[:, hh, :],
                                                             dec[:, 2 * p + hh, i:i + 1], bank[4 + hh][:, 0:VA],
                                                             ALU.mult, ALU.add)
                    ins.then_inc(ml_c, 1)
                    return
                sampled_states(p, 1)

            def fill(units):
                for b, u in units:
                    if (b, u) in GATES:
                        gated(b, u)
                    if u in (SPLIT_AT, SPLIT_AT + 1):
                        split(b + 1, u - SPLIT_AT)

            def mlstm_dve(p):
                s0 = p * S_PER
                ml_exponents(s0)
                ml_weigh(s0)
                fill(FILL_ML[p][0])
                for i in range(NT):
                    s = s0 + i
                    if i < NT - 1:
                        ml_exponents(s + 1)
                    else:
                        sampled_states(p, 0)
                        fill(FILL_ML[p][2 * i + 1])
                    ml_second(s)
                    ml_norm(s)
                    if i < NT - 1:
                        fill(FILL_ML[p][2 * i + 1])
                        ml_weigh(s + 1)
                    fill(FILL_ML[p][2 * i + 2])

            def at_mask(u):
                i, p, half = at_unit(u)
                kv = 2 * p + half
                lo = 0 if i else P
                dve.wait_ge(at_s, u + 1)
                if u == 0:
                    dve.wait_ge(consts, 5)
                if u == HALF:
                    dve.wait_ge(ss_v, NSEQ)
                    dve.wait_ge(ss_ot, NSEQ)
                if u >= 2:
                    dve.wait_ge(at_t, u - 1)
                st = ast[:, u % 2]
                for g in range(GRP):
                    src = bank[3 + g // 2][:, (g % 2) * 256 + lo:(g % 2) * 256 + 256]
                    ins = nc.vector.tensor_tensor_reduce(out=prob[:, u % 2, g, lo:], in0=src, in1=amask[:, lo:],
                                                         scale=1.0, scalar=-BIG, op0=ALU.add, op1=ALU.max,
                                                         accum_out=st[:, 0, g:g + 1])
                link(ins)
                sk = sink_b[:, kv * GRP:(kv + 1) * GRP]
                link(nc.vector.scalar_tensor_tensor(st[:, 1, :], st[:, 0, :], ATT_SCALE, sk, ALU.mult, ALU.max))
                nc.vector.tensor_scalar(st[:, 2, :], st[:, 1, :], -1.0, None, ALU.mult)
                nc.vector.tensor_tensor(st[:, 3, :], sk, st[:, 1, :], ALU.subtract).then_inc(at_m, 1)

            def at_divide(u):
                lo = 0 if at_unit(u)[0] else P
                dve.wait_ge(at_e, u + 1)
                st = ast[:, u % 2]
                link(nc.vector.tensor_tensor(st[:, 5, :], st[:, 4, :], st[:, 3, :], ALU.add))
                link(nc.vector.reciprocal(st[:, 5, :], st[:, 5, :]))
                for g in range(GRP):
                    v = prob[:, u % 2, g, lo:]
                    ins = nc.vector.tensor_scalar(v, v, st[:, 5, g:g + 1], None, ALU.mult)
                ins.then_inc(at_p, 1)

            def at_own(u):
                dve.wait_ge(at_t, u + 1)
                if u >= 2:
                    dve.wait_ge(at_v, u // 2)
                nc.vector.tensor_copy(pT[:, u % 2, 1, :], bank[6][:, :]).then_inc(at_p1, 1)

            def ss_mask(b):
                dve.wait_ge(ss_s, b + 1)
                if b == 0:
                    dve.wait_ge(mask_io, 16 * 17)
                if b >= 2:
                    dve.wait_ge(ss_t, b - 1)
                st = sst[:, b % 2]
                own = WIN + DSEQ * (NSEQ - 1 - b)
                for x, lo, hi, m in ((0, 0, WIN, 0), (5, WIN, WIN + 64, own)):
                    ins = nc.vector.tensor_tensor_reduce(out=sprob[:, b % 2, lo:hi], in0=bank[4][:, lo:hi],
                                                         in1=smask[:, m:m + hi - lo], scale=1.0, scalar=-BIG,
                                                         op0=ALU.add, op1=ALU.max, accum_out=st[:, x:x + 1])
                link(ins)
                link(nc.vector.tensor_tensor(st[:, 0:1], st[:, 0:1], st[:, 5:6], ALU.max))
                link(nc.vector.scalar_tensor_tensor(st[:, 1:2], st[:, 0:1], ATT_SCALE, sink_s[:, :], ALU.mult, ALU.max))
                nc.vector.tensor_scalar(st[:, 2:3], st[:, 1:2], -1.0, None, ALU.mult)
                nc.vector.tensor_tensor(st[:, 3:4], sink_s[:, :], st[:, 1:2], ALU.subtract).then_inc(ss_m, 1)

            def ss_divide(b):
                dve.wait_ge(ss_e, b + 1)
                st = sst[:, b % 2]
                link(nc.vector.tensor_tensor(st[:, 5:6], st[:, 4:5], st[:, 3:4], ALU.add))
                link(nc.vector.reciprocal(st[:, 5:6], st[:, 5:6]))
                v = sprob[:, b % 2, :]
                nc.vector.tensor_scalar(v, v, st[:, 5:6], None, ALU.mult).then_inc(ss_p, 1)

            def ss_gather(b):
                dve.wait_ge(ss_v, b + 1)
                if b >= 1:
                    dve.wait_ge(ss_ot, b)
                if b == 0:
                    link(nc.vector.memset(o2[:, :], 0.0))
                for kv in range(NKV):
                    at = slice(32 * kv, 32 * kv + 32)
                    half = kv % 2
                    ins = nc.vector.tensor_copy(o2[at, 64 * half:64 * half + 64], bank[6][at, kv * HD:(kv + 1) * HD])
                ins.then_inc(ss_o2, 1)

            def prompt_dve(p, fills):
                u0 = p * HALF
                at_mask(u0)
                at_divide(u0)
                fill(fills[0])
                for n in range(HALF):
                    u = u0 + n
                    if n + 1 < HALF:
                        at_mask(u + 1)
                        at_own(u)
                        at_divide(u + 1)
                        fill(fills[n + 1])
                    else:
                        fill(fills[n + 1])
                        at_own(u)

            def sampled_dve(fills):
                fill(fills[0])
                dve.wait_ge(free_a, FIRST_UNIT[17])
                dve.wait_ge(at_v, NB)
                for p in range(2):
                    ins = nc.vector.tensor_copy(qsmp[:, p, :, :, :].rearrange("c b g t -> c g b t"),
                                                aqT[:, p * GRP:(p + 1) * GRP, SEQ:T]
                                                .rearrange("c g (b t) -> c g b t", t=DSEQ))
                ins.then_inc(ss_q, 1)
                ss_mask(0)
                ss_divide(0)
                for b in range(NSEQ):
                    fill(fills[2 * b + 1])
                    if b + 1 < NSEQ:
                        ss_mask(b + 1)
                        ss_divide(b + 1)
                    fill(fills[2 * b + 2])
                    ss_gather(b)

            def gated(b, u):
                kind, p, gg = BLOCKS[b]
                m = GATES[b, u]
                tile, (c0, cn) = u // 3, CHUNKS[u % 3]
                j = p * GRP + 2 * gg + tile
                dve.wait_ge(free_a, FIRST_UNIT[b] + u + 1)
                h = hT[:, j, c0:c0 + cn]
                g = sig[:, m % 2, 0:cn]
                if kind == "mo":
                    link(nc.vector.tensor_scalar(g, g, 1.0, mnorm[:, j:j + 1], ALU.add, ALU.mult))
                    nc.vector.tensor_tensor(h, h, g, ALU.mult).then_inc(sg_use, 1)
                elif kind == "ga":
                    dve.wait_ge(sg_use, m - 5)
                    nc.vector.scalar_tensor_tensor(h, g, 1.0, h, ALU.add, ALU.mult).then_inc(sg_use, 1)
                else:
                    a = aqT[:, j, c0:c0 + cn]
                    dve.wait_ge(sg_use, 48)
                    dve.wait_ge(at_o, NB * (p + 1))
                    dve.wait_ge(ss_o, NSEQ)
                    link(nc.vector.scalar_tensor_tensor(a, g, 1.0, a, ALU.add, ALU.mult))
                    nc.vector.scalar_tensor_tensor(h, a, 0.5, h, ALU.mult, ALU.add).then_inc(sg_use, 1)

            dve.wait_ge(gain_in, 16)
            norm_tile(0, xin[:, 0, :], xn)
            norm_tile(1, xin[:, 1, :], xn)
            rest_x(0)
            split(0)
            norm_tile(2, xin[:, 2, :], xn)
            rest_x(1)
            for i in range(3, NT + 1):
                if i < NT:
                    norm_tile(i, xin[0:rows_of(i), i % 3, :], xn)
                rest_x(i - 1)
            split(1)
            dve.wait_ge(const_in, 16 * 9)
            link(nc.vector.tensor_scalar(mnorm[:, :], mnorm[:, :], 0.25, None, ALU.mult))
            fill(units_of(1, 1))
            gate_scans()
            gate_ends()
            fill(units_of(2, 3))
            gate_columns()
            mlstm_dve(0)
            mlstm_dve(1)
            fill(units_of(*AQ_BLOCKS))
            prompt_dve(0, FILL_P0)
            sampled_dve(FILL_SS)
            prompt_dve(1, FILL_P1)
            *before, last = units_of(*GB_BLOCKS)
            fill(before)

            for i in range(NT):
                if i == 1:
                    fill([last])
                dve.wait_ge(mg_hi, i + 1)
                nc.vector.tensor_tensor(xT_lo[:, :, cols(i)], hT[:, :, cols(i)], xT_hi[:, :, cols(i)].bitcast(F32),
                                        ALU.subtract).then_inc(mg_lo, 1)
            def split_mlp(count, slot):
                dve.wait_ge(w_hi_done, count)
                n = KT * WCOLS
                nc.vector.tensor_tensor(w_lo[:, slot, 0:n], raw[:, slot, 0:n], w_hi[:, slot, 0:n].bitcast(F32),
                                        ALU.subtract).then_inc(w_lo_done, 1)

            for cq in range(4):
                for i in range(NT):
                    if i == 3 and cq < 3:
                        split(NPROJ + 1 + cq)
                    m = NT * cq + i
                    r = rows_of(i)
                    if cq == 0:
                        dve.wait_ge(x2_in[i], 16)
                    if m == 0:
                        nc.vector.memset(x2[NS:P, NT - 1, :], 0.0)
                    dve.wait_ge(gemm_v, m + 1)
                    v = x2[0:r, i, cq * WCOLS:(cq + 1) * WCOLS]
                    nc.vector.tensor_tensor(v, bank[m % out_ring(m)][0:r, 0:WCOLS], v, ALU.add).then_inc(free_v, 1)
                    if cq < 3:
                        continue
                    if i == 1:
                        dve.wait_ge(gain_in, 32)
                    if i >= 1:
                        norm_tile(NT + i - 1, x2[:, i - 1, :], ybuf)
                    if i == 4:
                        split_mlp(B_MLP + 1, 0)
                    if i >= 2:
                        rest_x(NT + i - 2)
            norm_tile(2 * NT - 1, x2[0:rows_of(NT - 1), NT - 1, :], ybuf)
            rest_x(2 * NT - 2)
            rest_x(2 * NT - 1)

            def hidden(g, hslot, count, slot):
                for u in range(UP_UNITS):
                    tile, (c0, cn) = u // 3, CHUNKS[u % 3]
                    dve.wait_ge(free_a, g * UP_UNITS + (PROJ_UNITS + u + 1))
                    nc.vector.tensor_tensor(sqr[:, u % 2, 0:cn], relu[:, u % 2, 0:cn], relu[:, u % 2, 0:cn],
                                            ALU.mult).then_inc(sq_done, 1)
                    dve.wait_ge(sq_done, g * UP_UNITS + (u + 1))
                    dve.wait_ge(hi_done, g * UP_UNITS + (u + 1))
                    n = min(cn, SEQ - c0)
                    ins = nc.vector.tensor_tensor(hid_lo[:, hslot, tile, c0:c0 + n], sqr[:, u % 2, 0:n],
                                                  hid_hi[:, hslot, tile, c0:c0 + n].bitcast(F32), ALU.subtract)
                    if n < cn:
                        ins = nc.vector.tensor_tensor(hid_hi[:, hslot, tile, T:T + NS], sqr[:, u % 2, n:cn],
                                                      hid_hi[:, hslot, tile, SEQ:T].bitcast(F32), ALU.subtract)
                    ins.then_inc(lo_done, 1)
                    if u == 1:
                        split_mlp(count, slot)

            def accumulate(g, hslot, n):
                i = DN_ORDER[n]
                for half in range(2):
                    d = hslot * DN_UNITS + 2 * n + half
                    dve.wait_ge(gemm_v, g * DN_UNITS + (OUT_UNITS + 2 * n + half + 1))
                    v = x2[:, i, half * 512:half * 512 + 512]
                    nc.vector.tensor_tensor(v, bank[4 + d % 4][:, :], v, ALU.add).then_inc(free_v, 1)

            def fold():
                for half in range(2):
                    dve.wait_ge(folded, half + 1)
                    v = x2[0:NS, NT - 1, half * 512:half * 512 + 512]
                    nc.vector.tensor_tensor(v, bank[half][0:NS, :], v, ALU.add).then_inc(folded_in, 1)

            hidden(0, 0, B_MLP + 2, 1)
            with dve.Fori(0, NG // 2 - 1) as it:
                for x in range(2):
                    hidden(it * 2 + (1 + x), (1 + x) % 2, it * 4 + (B_MLP + 3 + 2 * x), 0)
                    for i in range(NT):
                        accumulate(it * 2 + x, x, i)
                        if i == 4:
                            split_mlp(it * 4 + (B_MLP + 4 + 2 * x), 1)
            hidden(NG - 1, 1, B_MLP + 2 * NG - 1, 0)
            for i in range(NT):
                accumulate(NG - 2, 0, i)
                if i == 4:
                    split_mlp(B_MLP + 2 * NG, 1)
            dve.wait_ge(gain_in, 48)

            def final(n):
                i = DN_ORDER[n]

                def slot():
                    if n >= 2:
                        dve.wait_ge(y_out[n % 2], 16 * (n // 2))
                normalise(2 * NT + n, x2[0:rows_of(i), i, :], ybuf, slot).then_inc(y_rdy, 1)

            accumulate(NG - 1, 1, 0)
            accumulate(NG - 1, 1, 1)
            fold()
            for n in range(2, NT):
                accumulate(NG - 1, 1, n)
                if n <= 3:
                    final(n - 2)
                if n >= 3:
                    final(n - 1)
            final(NT - 1)

        @block.gpsimd
        def _(pool):
            chain = [0]

            def link(ins):
                chain[0] += 1
                ins.then_inc(pool_chain, 1)
                pool.wait_ge(pool_chain, chain[0])

            def keep_where(t, pattern, base, ch, op, fill):
                return nc.gpsimd.affine_select(out=t, in_=t, compare_op=op, fill=fill, base=base, pattern=pattern,
                                               channel_multiplier=ch)

            nc.gpsimd.memset(neghalf[:, :], -0.5)
            link(nc.gpsimd.memset(ident[:, :], 0.0))
            keep_where(ident[:, :], [[-1, P]], 0, 1, ALU.not_equal, 1.0).then_inc(consts, 1)

            def rms(t):
                rows = rows_of(tile_of(t))
                pool.wait_ge(norm_sq, t + 1)
                v = rstd[0:rows, t // NT, t % NT:t % NT + 1]
                link(nc.gpsimd.tensor_scalar(v, stat[0:rows, t // NT, t % NT:t % NT + 1], 1.0 / D, EPS,
                                             ALU.mult, ALU.add))
                nc.gpsimd.tensor_tensor(v, v, neghalf[0:rows, 0:1], ALU.pow).then_inc(norm_rs, 1)

            for t in range(NT):
                rms(t)
            nc.gpsimd.memset(causal8[:, :], BIG)
            nc.gpsimd.memset(seq_ind[:, :], 1.0)
            nc.gpsimd.memset(vaug0[:, :, :, DV:VA], 1.0)
            link(nc.gpsimd.memset(causal[:, :], BIG))
            keep_where(causal[:, :], [[1, P]], 0, -1, ALU.is_ge, -BIG)
            link(keep_where(causal8[:, :], [[1, 64]], 0, -1, ALU.is_ge, -BIG))
            c8 = causal8[:, :].rearrange("s (b t) -> s b t", t=DSEQ)
            keep_where(c8, [[-DSEQ, NSEQ], [0, DSEQ]], 0, 1, ALU.is_ge, -BIG)
            link(keep_where(seq_ind[:, :], [[-DSEQ, NSEQ]], 0, 1, ALU.is_ge, 0.0))
            keep_where(seq_ind[:, :], [[DSEQ, NSEQ]], DSEQ - 1, -1, ALU.is_ge, 0.0)
            nc.gpsimd.memset(qz[:, :, :], 0.0)
            nc.gpsimd.memset(Cst[:, :, :], 0.0).then_inc(ml_cl, 1)
            nc.gpsimd.memset(q4[:, :], 0.0).then_inc(consts, 1)
            link(nc.gpsimd.memset(row_r[:, :], 1.0))
            nc.gpsimd.memset(row_r[:, 0:SEQ:P], 0.0)
            nc.gpsimd.memset(row_r[:, SEQ:T:DSEQ], 0.0).then_inc(consts, 1)

            def ml_query(s):
                p, i = divmod(s, S_PER)
                n = rows_of(i)
                pool.wait_ge(bc_in[s % 2], 32 * (s // 2 + 1))
                if i == 0:
                    pool.wait_ge(free_a, FIRST_UNIT[4 * p + 4])
                if i < NT - 1:
                    if s >= 2:
                        pool.wait_ge(ml_n, s - 1)
                    nc.gpsimd.tensor_tensor(qs[:, s % 2, :, 0:n], hT[:, p * GRP:p * GRP + 2, cols(i)], bc[:, s % 2, 2:4, 0:n],
                                            ALU.mult).then_inc(ml_qs, 1)
                    return
                for hh in range(2):
                    dst = qz[:, hh, :].rearrange("c (b x) -> c b x", x=72)[:, :, 0:DSEQ]
                    ins = nc.gpsimd.tensor_tensor(dst, mq(p, hh, cols(i)).rearrange("c (b t) -> c b t", t=DSEQ),
                                                  bc[:, s % 2, 2 + hh, 0:n].rearrange("c (b t) -> c b t", t=DSEQ),
                                                  ALU.mult)
                ins.then_inc(ml_qs, 1)

            def ml_keys(s, hh):
                p = s // S_PER
                n = rows_of(NT - 1)
                pool.wait_ge(ml_kw, s + 1)
                if hh or p:
                    pool.wait_ge(ml_su, (2 * p + hh) * NSEQ)
                nc.gpsimd.tensor_tensor(kwz[:, :, :],
                                        kw[0:n, s % 2, hh, :].unsqueeze(1).broadcast_to([n, NSEQ, DK]),
                                        seq_ind[:, :].unsqueeze(2).broadcast_to([n, NSEQ, DK]),
                                        ALU.mult).then_inc(ml_kz, 1)

            def ml_rms(s):
                n = rows_of(s % S_PER)
                pool.wait_ge(ml_ss, 2 * s + 2)
                v = small[0:n, s % 2, 6:8]
                link(nc.gpsimd.tensor_scalar(v, small[0:n, s % 2, 4:6], 1.0 / DV, EPS, ALU.mult, ALU.add))
                nc.gpsimd.tensor_tensor(v, v, neghalf[0:n, :], ALU.pow).then_inc(ml_rs, 1)

            pool.wait_ge(gate_nat, 1)
            pool.wait_ge(rows_out, 48)
            nc.gpsimd.memset(vaug1[:, :, :, DV:VA], 1.0).then_inc(ones, 1)
            for p in range(2):
                if p:
                    pool.wait_ge(pc_out, 32)
                    nc.gpsimd.memset(Cst[:, :, :], 0.0).then_inc(ml_cl, 1)
                s0 = p * S_PER
                ml_query(s0)
                for s in range(s0, s0 + S_PER):
                    if s + 1 < s0 + S_PER:
                        ml_query(s + 1)
                    if s == s0 + NT - 1:
                        ml_keys(s, 1)
                    ml_rms(s)
                    if s == s0 + NT - 2:
                        ml_keys(s + 1, 0)

            pool.wait_ge(cin_out, 32 * 8)
            pool.wait_ge(pc_out, 64)
            pool.wait_ge(ml_hn, 2 * S_PER)
            pool.wait_ge(ml_t, 2 * S_PER)
            link(nc.gpsimd.memset(smask[0:DSEQ, :], 0.0))
            keep_where(smask[0:DSEQ, 0:WIN], [[1, WIN]], -1, -1, ALU.is_ge, -BIG)
            new = smask[0:DSEQ, WIN:MASKW]
            own = DSEQ * (NSEQ - 1)
            link(keep_where(new, [[-1, MASKW - WIN]], own, 1, ALU.is_ge, -BIG))
            keep_where(new, [[1, MASKW - WIN]], -own, 0, ALU.is_ge, -BIG).then_inc(mask_made, 1)
            for kv in range(NKV):
                link(nc.gpsimd.memset(akz[64 * (1 - kv % 2):64 * (1 - kv % 2) + 64, kv, :], 0.0))
            link(nc.gpsimd.memset(amask[:, :], 0.0))
            keep_where(amask[:, 0:P], [[1, P]], -1, -1, ALU.is_ge, -BIG).then_inc(consts, 1)
            keep_where(amask[:, P:2 * P], [[-1, P]], 0, 1, ALU.is_ge, -BIG).then_inc(consts, 1)
            for t in range(NT, 3 * NT):
                rms(t)


_INS = ["x_prompt", "x_sample", "state_C", "state_n", "state_m", "cache_k", "cache_v", "norm_attn", "w_in", "b_gate",
        "mlstm_norm", "sinks", "w_out", "norm_mlp", "w_up", "w_down", "norm_final"]
_OUTS = [(1, SEQ, D), (NSEQ, DSEQ, D), (1, 1, MH, DK, DV), (1, 1, MH, DK), (1, 1, MH),
         (1, 1, WIN, NKV, HD), (1, 1, WIN, NKV, HD), (1, NSEQ, MH, DK, DV), (1, NSEQ, MH, DK), (1, NSEQ, MH),
         (1, NSEQ, WIN, NKV, HD), (1, NSEQ, WIN, NKV, HD)]


def kernel(**inputs):
    import numpy as _np
    import concourse.bacc as _bacc
    from concourse import mybir as _mybir
    from concourse.bass_utils import run_bass_kernel_spmd as _run

    nc = _bacc.Bacc("TRN2", target_bir_lowering=False, num_devices=1, dynamic_dma_scratch_size=1024)
    arrays, args = {}, []
    for name in _INS:
        a = _np.ascontiguousarray(inputs[name])
        arrays[f"in_{name}"] = a
        args.append(nc.dram_tensor(f"in_{name}", a.shape, _mybir.dt.from_np(a.dtype), kind="ExternalInput").ap())
    for i, shape in enumerate(_OUTS):
        args.append(nc.dram_tensor(f"out_{i}", shape, _mybir.dt.float32, kind="ExternalOutput").ap())
    layer_kernel(nc, *args)
    r = _run(nc, [arrays], core_ids=[0])
    return tuple(r.results[0][f"out_{i}"] for i in range(len(_OUTS)))
```
